# Optimizing a Trainium2 kernel written in Bass

```python
import math
import jax, jax.numpy as jnp
from jax import lax
import numpy as np

D_MODEL = 1024
BATCH = 1
SEQ = 1024
DEPTH = 2
DEC_BATCH = 8
DEC_SEQ = 4
PAST_LEN = 4096
PAGE_SIZE = 128

HEAD_DIM = 64
N_HEADS_A = 8
N_HEADS_B = 8
N_KV_B = 2
GQA_GROUP = N_HEADS_B // N_KV_B
DILATED_GROUPS = ((128, 1), (512, 4), (2048, 16))
WIN_A = max(w for w, _ in DILATED_GROUPS)
WIN_B = 128
BLOCK = 128
ROT_DIM = HEAD_DIM // 4
ROPE_THETA = 500000.0
EPS = 1e-6
SCALE = HEAD_DIM ** -0.5
W_A = N_HEADS_A * HEAD_DIM
W_B = N_HEADS_B * HEAD_DIM
W_KVB = N_KV_B * HEAD_DIM
MIX_WIDTH = W_A + W_B
IN_COLS = 3 * W_A + W_B + 2 * W_KVB
SPLITS = (W_A, 2 * W_A, 3 * W_A, 3 * W_A + W_B, 3 * W_A + W_B + W_KVB)
D_FF = -(-8 * D_MODEL // (3 * 256)) * 256

kernel_name = "hymba_dilated_swa_sink_decoder_step"

def rms_norm(x, g):
    xf = x.astype(jnp.float32)
    y = xf * lax.rsqrt(jnp.mean(xf * xf, axis=-1, keepdims=True) + EPS)
    return (y * g.astype(jnp.float32)).astype(x.dtype)

def rope_partial(x, pos):
    half = ROT_DIM // 2
    inv = jnp.exp(-math.log(ROPE_THETA) * jnp.arange(0, ROT_DIM, 2, dtype=jnp.float32) / ROT_DIM)
    ang = pos.astype(jnp.float32)[:, None] * inv[None, :]
    cos = jnp.cos(ang)[:, None, :]
    sin = jnp.sin(ang)[:, None, :]
    xr = x[..., :ROT_DIM].astype(jnp.float32)
    x1, x2 = xr[..., :half], xr[..., half:]
    rot = jnp.concatenate([x1 * cos - x2 * sin, x2 * cos + x1 * sin], axis=-1).astype(x.dtype)
    return jnp.concatenate([rot, x[..., ROT_DIM:]], axis=-1)

def mix_inputs(x, g_attn, w_in, qn_a, kn_a, qn_b, kn_b, pos):
    n, l, _ = x.shape
    h = rms_norm(x, g_attn)
    proj = jnp.einsum('nld,de->nle', h, w_in)
    qa, ka, va, qb, kb, vb = jnp.split(proj, SPLITS, axis=-1)
    heads = lambda z, nh: z.reshape(n, l, nh, HEAD_DIM)
    qa = rope_partial(rms_norm(heads(qa, N_HEADS_A), qn_a), pos)
    ka = rope_partial(rms_norm(heads(ka, N_HEADS_A), kn_a), pos)
    qb = rope_partial(rms_norm(heads(qb, N_HEADS_B), qn_b), pos)
    kb = rope_partial(rms_norm(heads(kb, N_KV_B), kn_b), pos)
    return qa, ka, heads(va, N_HEADS_A), qb, kb, heads(vb, N_KV_B)

def softmax_parts(s, sink):
    m = jnp.max(s, axis=-1, keepdims=True)
    if sink is not None:
        m = jnp.maximum(m, sink)
    p = jnp.exp(s - m)
    den = jnp.sum(p, axis=-1, keepdims=True)
    if sink is not None:
        den = den + jnp.exp(sink - m)
    return p, m, den

def banded_attention(q, k, v, max_dist, sink):
    n, l, h, hd = q.shape
    hk = k.shape[2]
    g = h // hk
    lp = -(-l // BLOCK) * BLOCK
    pad = ((0, 0), (0, lp - l), (0, 0), (0, 0))
    q, k, v = (jnp.pad(z, pad) for z in (q, k, v))
    nb = lp // BLOCK
    qb = q.reshape(n, nb, BLOCK, hk, g, hd)

    def with_prev(z):
        zb = z.reshape(n, nb, BLOCK, hk, hd)
        prev = jnp.concatenate([jnp.zeros_like(zb[:, :1]), zb[:, :-1]], axis=1)
        return jnp.concatenate([prev, zb], axis=2)

    k2, v2 = with_prev(k), with_prev(v)
    s = jnp.einsum('nbihgd,nbjhd->nbhgij', qb, k2, preferred_element_type=jnp.float32) * SCALE
    i = jnp.arange(BLOCK)[:, None]
    j = jnp.arange(2 * BLOCK)[None, :]
    dist = i + BLOCK - j
    first = (jnp.arange(nb) == 0)[:, None, None]
    valid = (dist >= 0) & (dist <= max_dist) & ~(first & (j < BLOCK))
    s = jnp.where(valid[None, :, None, None], s, -jnp.inf)
    p, m, den = softmax_parts(s, sink)
    o = jnp.einsum('nbhgij,nbjhd->nbhgid', p, v2.astype(jnp.float32)) / den
    o = o.transpose(0, 1, 4, 2, 3, 5).reshape(n, lp, h, hd)[:, :l]
    lse = (m + jnp.log(den))[..., 0].transpose(0, 1, 4, 2, 3).reshape(n, lp, h)[:, :l]
    return o, lse

def combine_dilations(outs, lses):
    w = jax.nn.softmax(jnp.stack(lses, axis=0), axis=0)
    return jnp.sum(w[..., None] * jnp.stack(outs, axis=0), axis=0)

def dilated_attention_prompt(q, k, v):
    n, s, h, hd = q.shape
    outs, lses = [], []
    for w, d in DILATED_GROUPS:
        lsub = -(-(-(-s // d)) // BLOCK) * BLOCK
        sp = lsub * d

        def split(z):
            z = jnp.pad(z, ((0, 0), (0, sp - s), (0, 0), (0, 0)))
            return z.reshape(n, lsub, d, h, hd).transpose(0, 2, 1, 3, 4).reshape(n * d, lsub, h, hd)

        o, lse = banded_attention(split(q), split(k), split(v), w // d, None)
        outs.append(o.reshape(n, d, lsub, h, hd).transpose(0, 2, 1, 3, 4).reshape(n, sp, h, hd)[:, :s])
        lses.append(lse.reshape(n, d, lsub, h).transpose(0, 2, 1, 3).reshape(n, sp, h)[:, :s])
    return combine_dilations(outs, lses)

def dilated_attention_sample(q, k_all, v_all):
    n, t, h, hd = q.shape
    l = k_all.shape[1] - t
    outs, lses = [], []
    for w, d in DILATED_GROUPS:
        taps = jnp.arange(w // d + 1) * d
        idx = (l + jnp.arange(t))[:, None] - taps[None, :]
        valid = idx >= 0
        idc = jnp.clip(idx, 0)
        kg = jnp.take(k_all, idc, axis=1)
        vg = jnp.take(v_all, idc, axis=1)
        s = jnp.einsum('nthd,ntjhd->nhtj', q, kg, preferred_element_type=jnp.float32) * SCALE
        s = jnp.where(valid[None, None], s, -jnp.inf)
        p, m, den = softmax_parts(s, None)
        o = jnp.einsum('nhtj,ntjhd->nthd', p, vg.astype(jnp.float32)) / den.transpose(0, 2, 1, 3)
        outs.append(o)
        lses.append((m + jnp.log(den))[..., 0].transpose(0, 2, 1))
    return combine_dilations(outs, lses)

def window_attention_sample(q, k_all, v_all, sink):
    n, t, h, hd = q.shape
    hk = k_all.shape[2]
    l = k_all.shape[1] - t
    qg = q.reshape(n, t, hk, h // hk, hd)
    s = jnp.einsum('nthgd,njhd->nhgtj', qg, k_all, preferred_element_type=jnp.float32) * SCALE
    qpos = PAST_LEN + jnp.arange(t)
    kpos = PAST_LEN - l + jnp.arange(l + t)
    dist = qpos[:, None] - kpos[None, :]
    valid = (dist >= 0) & (dist < WIN_B) & (kpos >= 0)[None, :]
    s = jnp.where(valid, s, -jnp.inf)
    p, m, den = softmax_parts(s, sink)
    o = jnp.einsum('nhgtj,njhd->nthgd', p, v_all.astype(jnp.float32)) / den.transpose(0, 3, 1, 2, 4)
    return o.reshape(n, t, h, hd)

def mix_output_and_ffn(x, oa, ob, on_a, on_b, w_out, g_ffn, w_gate_up, w_down):
    n, l, _ = x.shape
    oa = rms_norm(oa.reshape(n, l, W_A), on_a)
    ob = rms_norm(ob.reshape(n, l, W_B), on_b)
    mix = jnp.concatenate([oa, ob], axis=-1).astype(x.dtype)
    x = x + jnp.einsum('nle,ed->nld', mix, w_out)
    h = rms_norm(x, g_ffn)
    gate, up = jnp.split(jnp.einsum('nld,df->nlf', h, w_gate_up), 2, axis=-1)
    return x + jnp.einsum('nlf,fd->nld', jax.nn.silu(gate) * up, w_down)

def setup_inputs(seed: int = 0) -> dict:
    key = jax.random.key(seed)
    ks = jax.random.split(key, 18)
    f32 = jnp.float32
    la = min(WIN_A, PAST_LEN)
    lb = min(WIN_B, PAST_LEN)
    nrm = lambda k, shape, scale=1.0: scale * jax.random.normal(k, shape, f32)
    gain = lambda k, shape: 1.0 + 0.02 * jax.random.normal(k, shape, f32)
    return {
        "x_prompt": nrm(ks[0], (BATCH, SEQ, D_MODEL)),
        "x_sample": nrm(ks[1], (DEC_BATCH, DEC_SEQ, D_MODEL)),
        "cache_a": nrm(ks[2], (DEPTH, DEC_BATCH, la, 2, N_HEADS_A, HEAD_DIM)),
        "cache_b": nrm(ks[3], (DEPTH, DEC_BATCH, lb, 2, N_KV_B, HEAD_DIM)),
        "attn_norm": gain(ks[4], (DEPTH, D_MODEL)),
        "w_in": nrm(ks[5], (DEPTH, D_MODEL, IN_COLS), D_MODEL ** -0.5),
        "q_norm_a": gain(ks[6], (DEPTH, HEAD_DIM)),
        "k_norm_a": gain(ks[7], (DEPTH, HEAD_DIM)),
        "q_norm_b": gain(ks[8], (DEPTH, HEAD_DIM)),
        "k_norm_b": gain(ks[9], (DEPTH, HEAD_DIM)),
        "sinks_b": nrm(ks[10], (DEPTH, N_HEADS_B)),
        "out_norm_a": gain(ks[11], (DEPTH, W_A)),
        "out_norm_b": gain(ks[12], (DEPTH, W_B)),
        "w_out": nrm(ks[13], (DEPTH, MIX_WIDTH, D_MODEL), MIX_WIDTH ** -0.5),
        "ffn_norm": gain(ks[14], (DEPTH, D_MODEL)),
        "w_gate_up": nrm(ks[15], (DEPTH, D_MODEL, 2 * D_FF), D_MODEL ** -0.5),
        "w_down": nrm(ks[16], (DEPTH, D_FF, D_MODEL), D_FF ** -0.5),
    }

def reference(x_prompt, x_sample, cache_a, cache_b, attn_norm, w_in, q_norm_a, k_norm_a, q_norm_b,
              k_norm_b, sinks_b, out_norm_a, out_norm_b, w_out, ffn_norm, w_gate_up, w_down):
    s_len = x_prompt.shape[1]
    t_len = x_sample.shape[1]
    pos_p = jnp.arange(s_len, dtype=jnp.int32)
    pos_s = PAST_LEN + jnp.arange(t_len, dtype=jnp.int32)
    la_p = min(WIN_A, s_len)
    lb_p = min(WIN_B, s_len)
    xp, xs = x_prompt, x_sample
    new_a_p, new_b_p, new_a_s, new_b_s = [], [], [], []
    for layer in range(DEPTH):
        pre = (attn_norm[layer], w_in[layer], q_norm_a[layer], k_norm_a[layer],
               q_norm_b[layer], k_norm_b[layer])
        post = (out_norm_a[layer], out_norm_b[layer], w_out[layer], ffn_norm[layer],
                w_gate_up[layer], w_down[layer])
        sink = sinks_b[layer].astype(jnp.float32).reshape(N_KV_B, GQA_GROUP)[:, :, None, None]

        qa, ka, va, qb, kb, vb = mix_inputs(xp, *pre, pos_p)
        oa = dilated_attention_prompt(qa, ka, va)
        ob, _ = banded_attention(qb, kb, vb, WIN_B - 1, sink)
        new_a_p.append(jnp.stack([ka[:, s_len - la_p:], va[:, s_len - la_p:]], axis=2))
        new_b_p.append(jnp.stack([kb[:, s_len - lb_p:], vb[:, s_len - lb_p:]], axis=2))
        xp = mix_output_and_ffn(xp, oa, ob, *post)

        qa, ka, va, qb, kb, vb = mix_inputs(xs, *pre, pos_s)
        full_a = jnp.concatenate([cache_a[layer], jnp.stack([ka, va], axis=2).astype(cache_a.dtype)], axis=1)
        full_b = jnp.concatenate([cache_b[layer], jnp.stack([kb, vb], axis=2).astype(cache_b.dtype)], axis=1)
        oa = dilated_attention_sample(qa, full_a[:, :, 0], full_a[:, :, 1])
        ob = window_attention_sample(qb, full_b[:, :, 0], full_b[:, :, 1], sink)
        new_a_s.append(full_a[:, t_len:])
        new_b_s.append(full_b[:, t_len:])
        xs = mix_output_and_ffn(xs, oa, ob, *post)
    return (xp, xs, jnp.stack(new_a_p), jnp.stack(new_b_p), jnp.stack(new_a_s), jnp.stack(new_b_s))


_drawn_inputs = setup_inputs


def setup_inputs(seed=0):
    import zlib

    import numpy as np

    out = dict(_drawn_inputs(seed))
    spreads = {}
    factors = {'q_norm_a': 3.937,
     'k_norm_a': 3.351,
     'q_norm_b': 4.147,
     'k_norm_b': 3.182,
     'sinks_b': 2.727,
     'out_norm_a': 3.779,
     'out_norm_b': 3.805,
     'ffn_norm': 3.801}
    for name, (base, spread) in spreads.items():
        noise = np.random.default_rng([zlib.crc32(name.encode()), seed]).standard_normal(out[name].shape)
        drawn = base * np.exp(spread * noise) if base else spread * noise
        out[name] = __import__('jax').numpy.asarray(drawn.astype(out[name].dtype))
    for name, factor in factors.items():
        out[name] = (out[name] * factor).astype(out[name].dtype)
    return out
```

```python
from contextlib import ExitStack
import math

import numpy as np
import concourse.bass as bass
from concourse import mybir

F32 = mybir.dt.float32
F32R = mybir.dt.float32r
ACT = mybir.ActivationFunctionType
ALU = mybir.AluOpType
AX = mybir.AxisListType
ds = bass.ds

P = 128
D = 1024
DC = D // P
SEQ = 1024
QT = SEQ // P
DEPTH = 2
NB, TS = 8, 4
NS = NB * TS
T = SEQ + NS
NW = 3
W = T // NW
HD = 64
HA, HB, KVB = 8, 8, 2
NP = HA // 2
LA, LB = 2048, 128
PAST = 4096
FF = 2816
FI = FF // (2 * P)
ROT = HD // 4
EPS = 1e-6
SCALE = HD ** -0.5
WA = HA * HD
COL_QA, COL_KA, COL_VA, COL_QB, COL_KB, COL_VB = 0, WA, 2 * WA, 3 * WA, 4 * WA, 4 * WA + KVB * HD
NEG = -1e30
WIN = 512
NFAR = (LA - WIN) // 16
NKEYS = WIN + 4 * NFAR + NS
GQA, GKA, GQB, GKB, GATT, GFFN, GOUT = 0, 1, 2, 3, 4, 12, 20
NG = 28
A_STEPS = [(i, hh) for i in range(QT) for hh in range(2)]
NSTEP = len(A_STEPS)


def copies(dist):
    n = np.zeros(dist.shape)
    for w, d in ((128, 1), (512, 4), (2048, 16)):
        n += (dist >= 0) & (dist <= w) & (dist % d == 0)
    return n


def log_mask(n):
    return np.where(n > 0, np.log(np.maximum(n, 1)) / SCALE, NEG).astype(np.float32)


def constants():
    c = {}
    c["c_ident"] = np.eye(P, dtype=np.float32)
    c["c_ones"] = np.ones((P, P), np.float32)
    c["c_blocks"] = np.kron(np.eye(2), np.ones((HD, HD))).astype(np.float32)
    pos = np.concatenate([np.arange(SEQ), np.tile(PAST + np.arange(TS), NB)]).astype(np.float32)
    inv = np.exp(np.float32(-math.log(500000.0)) * np.arange(0, ROT, 2).astype(np.float32) / np.float32(ROT)).astype(np.float32)
    ang = (inv[:, None] * pos[None, :]).astype(np.float32).astype(np.float64)
    cos, sin = np.ones((HD, T)), np.zeros((HD, T))
    h = ROT // 2
    cos[:h] = cos[h:ROT] = np.cos(ang)
    sin[:h], sin[h:ROT] = -np.sin(ang), np.sin(ang)
    c["c_cos"] = np.tile(cos, (2, 1)).astype(np.float32)
    c["c_sin"] = np.tile(sin, (2, 1)).astype(np.float32)
    q = np.arange(P)[:, None]
    c["c_mask_a"] = log_mask(copies(q + (QT - 1) * P - np.arange(SEQ)[None, :]))
    dist = q + P - np.arange(2 * P)[None, :]
    c["c_mask_b"] = log_mask((dist >= 0) & (dist < 128))
    t = (np.arange(NS) % TS)[:, None]
    near = (LA - WIN) + TS * np.arange(P)[None, :] + np.arange(4)[:, None]
    far = 16 * np.arange(NFAR)[None, :] + np.arange(4)[:, None]
    rows = np.concatenate([near.ravel(), far.ravel()])[None, :]
    c["c_mask_s"] = log_mask(copies(LA + t - rows))
    new_b = (np.arange(NS) // TS)[None, None, :]
    new_t = (np.arange(NS) % TS)[None, None, :]
    dn = t[:, :, None] - new_t
    same = new_b == np.arange(NB)[None, :, None]
    c["c_mask_sn"] = log_mask(copies(dn) * same).reshape(NS, NB * NS)
    c["c_mask_t"] = log_mask((LB + t - np.arange(LB)[None, :]) < 128)
    c["c_mask_tn"] = log_mask((dn >= 0) * same).reshape(NS, NB * NS)
    c["c_pick"] = ((np.arange(NS) // TS)[:, None] == np.arange(HB)[None, :]).astype(np.float32)
    return c


def trunk(nc, x_prompt, x_sample, cache_a, cache_b, attn_norm, w_in, q_norm_a, k_norm_a, q_norm_b,
          k_norm_b, sinks_b, out_norm_a, out_norm_b, w_out, ffn_norm, w_gate_up, w_down,
          c_ident, c_ones, c_blocks, c_cos, c_sin, c_mask_a, c_mask_b, c_mask_s, c_mask_sn,
          c_mask_t, c_mask_tn, c_pick,
          y_prompt, y_sample, new_a_p, new_b_p, new_a_s, new_b_s):
    x_spill = nc.dram_tensor("x_spill", (P, DC * T), F32).ap()
    with ExitStack() as ctx:
        ctx.enter_context(nc.allow_non_contiguous_dma(reason="small gains are laid on partitions"))

        def tensor(scope, name, shape, dt=F32):
            return scope.enter_context(nc.sbuf_tensor(name, shape, dt))

        def sem(name):
            return ctx.enter_context(nc.semaphore(name))

        class Signal:
            def __init__(self, name, per_layer, starts=0):
                self.sem, self.per_layer, self.starts = sem(name), per_layer, starts

            def at(self, layer, count):
                return layer * self.per_layer + count + self.starts

        ident = tensor(ctx, "ident", [P, P])
        ones = tensor(ctx, "ones", [P, P])
        blocks = tensor(ctx, "blocks", [P, P])
        cos = tensor(ctx, "cos", [P, T])
        sin = tensor(ctx, "sin", [P, T])
        mask_a = tensor(ctx, "mask_a", [P, SEQ])
        mask_b = tensor(ctx, "mask_b", [P, 2 * P])
        gains = tensor(ctx, "gains", [P, NG])
        sinks = tensor(ctx, "sinks", [P, HB])
        eps = tensor(ctx, "eps", [P, 1])
        xm = tensor(ctx, "xm", [P, DC, T])

        mixer = ExitStack()
        q_rows_a = tensor(mixer, "q_rows_a", [P, NP, NB, HA, TS])
        q_rows_b = tensor(mixer, "q_rows_b", [P, NB, HB, TS])
        k_new_a = tensor(mixer, "k_new_a", [P, NP, NS])
        k_new_b = tensor(mixer, "k_new_b", [P, NS])
        kv_rows = tensor(mixer, "kv_rows", [NS, 2, NP + 1, P])

        pairs = ExitStack()
        h_hi = tensor(pairs, "h_hi", [P, DC, T], F32R)
        h_lo = tensor(pairs, "h_lo", [P, DC, T], F32R)
        w_raw = tensor(pairs, "w_raw", [P, DC, P])
        w_hi = tensor(pairs, "w_hi", [P, 2, DC, P], F32R)
        w_lo = tensor(pairs, "w_lo", [P, 2, DC, P], F32R)
        t_buf = [tensor(pairs, f"t_buf{i}", [P, T]) for i in range(3)]
        kt_a = tensor(pairs, "kt_a", [P, T])
        kt_b = tensor(pairs, "kt_b", [P, T])
        q_a = tensor(pairs, "q_a", [P, 2, SEQ])
        q_b = tensor(pairs, "q_b", [P, 2, SEQ])
        v_a = tensor(pairs, "v_a", [P, QT, P])
        v_b = tensor(pairs, "v_b", [P, QT, P])
        stage = tensor(pairs, "stage", [P, T])
        pt = tensor(pairs, "pt", [P, 3, 4 * P])
        stats = tensor(pairs, "stats", [P, 6, 4])
        sink_now = tensor(pairs, "sink_now", [P, 2])
        sink_raw = tensor(pairs, "sink_raw", [P, 2])
        sq1, hf1, rs1 = [t_buf[0], t_buf[1]], [kt_a, kt_b], t_buf[2]
        xy_tile = [q_a, q_b]
        pairs.close()

        samples = ExitStack()
        near = [tensor(samples, f"near{i}", [P, 4, 2 * WA]) for i in range(2)]
        far = [tensor(samples, f"far{i}", [NFAR, 4, 2 * WA]) for i in range(2)]
        last = [tensor(samples, f"last{i}", [P, 2, P]) for i in range(2)]
        kt_s = tensor(samples, "kt_s", [P, NP, WIN + 4 * NFAR])
        kt_t = tensor(samples, "kt_t", [P, P])
        q_now_a = tensor(samples, "q_now_a", [P, NP, NS])
        q_now_b = tensor(samples, "q_now_b", [P, NS])
        mask_s = tensor(samples, "mask_s", [NS, NKEYS])
        mask_t = tensor(samples, "mask_t", [NS, LB + NS])
        mask_sn = tensor(samples, "mask_sn", [NS, NB * NS])
        mask_tn = tensor(samples, "mask_tn", [NS, NB * NS])
        pick = tensor(samples, "pick", [NS, HB])
        p_s = tensor(samples, "p_s", [NS, NKEYS + LB + NS])
        pt_s = tensor(samples, "pt_s", [P, 11, NS])
        st_s = tensor(samples, "st_s", [NS, 16])
        samples.close()
        mixer.close()

        dense = ExitStack()
        g_hi = tensor(dense, "g_hi", [P, DC, T], F32R)
        g_lo = tensor(dense, "g_lo", [P, DC, T], F32R)
        f_raw = tensor(dense, "f_raw", [P, 2 * D])
        f_hi = [tensor(dense, f"f_hi{i}", [P, 2 * D], F32R) for i in range(3)]
        f_lo = [tensor(dense, f"f_lo{i}", [P, 2 * D], F32R) for i in range(3)]
        norms = ExitStack()
        sq2 = [tensor(norms, f"sq2_{i}", [P, T]) for i in range(2)]
        hf2 = [tensor(norms, f"hf2_{i}", [P, T]) for i in range(2)]
        rs2 = tensor(norms, "rs2", [P, T])
        norms.close()
        hidden = ExitStack()
        a_hi = tensor(hidden, "a_hi", [P, 2, T], F32R)
        a_lo = tensor(hidden, "a_lo", [P, 2, T], F32R)
        silu = tensor(hidden, "silu", [P, 2, W])
        hidden.close()
        dense.close()

        ps = ctx.enter_context(nc.psum_tensor("ps", [P, 8, 512], F32))

        consts_in = sem("consts_in")
        eps_set = sem("eps_set")
        x_tile_in = [sem(f"x_tile_in{i}") for i in range(2)]
        x_tile_turned = sem("x_tile_turned")
        x_tile_kept = sem("x_tile_kept")
        y_tile_turned = sem("y_tile_turned")
        y_tile_kept = sem("y_tile_kept")
        y_tile_out = [sem(f"y_tile_out{i}") for i in range(2)]
        met = sem("met")
        waits_alone = sem("waits_alone")

        N_GAINS = 14
        gains_in = Signal("gains_in", 16 * N_GAINS)
        spilled = Signal("spilled", 16)
        zeroed = Signal("zeroed", 6)
        sq_ready = Signal("sq_ready", 24)
        sq_summed = Signal("sq_summed", 24)
        root_ready = Signal("root_ready", 4)
        rs_ready = Signal("rs_ready", 4)
        hf_ready = Signal("hf_ready", 24)
        hi_ready = Signal("hi_ready", 24)
        lo_ready = Signal("lo_ready", 24)

        UNITS = 2 + 4 * NP
        RAW = [16, 32]
        RAW_P = [16, 32, 48, 80]
        w_raw_in = Signal("w_raw_in", 32 + 80 * NP)
        w_hi_ready = Signal("w_hi_ready", UNITS)
        w_split = Signal("w_split", UNITS, starts=1)
        projected = Signal("projected", UNITS)
        K_ROPE, Q_ROPE = 8, 10
        ROPE_P = K_ROPE + 2 * Q_ROPE
        rope = Signal("rope", K_ROPE + ROPE_P * NP, starts=1)
        head_sq = Signal("head_sq", 1 + 3 * NP)
        head_summed = Signal("head_summed", 1 + 3 * NP)
        head_root = Signal("head_root", 1 + 3 * NP)
        v_staged = Signal("v_staged", 1 + NP)
        v_turned = Signal("v_turned", 3 * (1 + NP))
        v_kept = Signal("v_kept", 3 * (1 + NP))
        k_turned = Signal("k_turned", 3 * (1 + NP))
        k_kept = Signal("k_kept", 3 * (1 + NP))
        v_out = Signal("v_out", 16 * (1 + NP))
        k_out = Signal("k_out", 16 * (1 + NP))
        sink_ready = Signal("sink_ready", 2 * NP)

        steps = [(m, i, hh) for m in "ab" for i in range(QT) for hh in range(2)]
        NST = len(steps)
        key_tiles = [list(range(i + 1)) if m == "a" else list(range(max(i - 1, 0), i + 1)) for m, i, hh in steps]
        groups = []
        for s, tiles in enumerate(key_tiles):
            groups += [(s, g, min(g + 4, len(tiles))) for g in range(0, len(tiles), 4)]
        NGR = len(groups)
        groups_of = [[g for g in range(NGR) if groups[g][0] == s] for s in range(NST)]
        exps_to = [sum(1 + (m == "b") for m, _, _ in steps[:s + 1]) for s in range(NST)]
        NEXP = exps_to[-1]
        scores = Signal("scores", NP * NST)
        masked = Signal("masked", NP * NST, starts=1)
        bias_ready = Signal("bias_ready", NP * NST)
        exped = Signal("exped", NP * NEXP)
        sum_ready = Signal("sum_ready", NP * NEXP)
        probs = Signal("probs", NP * NST)
        p_turned = Signal("p_turned", NP * NGR)
        pt_ready = Signal("pt_ready", NP * NGR, starts=1)
        mixed = Signal("mixed", NP * NST)
        mix_kept = Signal("mix_kept", NP * NST, starts=1)

        rows_out = Signal("rows_out", 16 * 4)
        cache_out = Signal("cache_out", 16 * 2 * NB)
        masks_in = Signal("masks_in", 16 * 5)
        sink_s = Signal("sink_s", 3)
        kv_in = [Signal(f"kv_in{i}", 16 * 3 * NB // 2) for i in range(2)]
        s_turned = Signal("s_turned", 9 * NB)
        near_kept = Signal("near_kept", 5 * NB)
        far_kept = Signal("far_kept", 4 * NB)
        s_query = Signal("s_query", 4 * NB)
        s_scores = Signal("s_scores", NB, starts=1)
        s_soft = Signal("s_soft", 10 * NB, starts=1)
        s_exped = Signal("s_exped", 3 * NB)
        s_pturned = Signal("s_pturned", NB)
        s_pkept = Signal("s_pkept", 5 * NB)
        s_mixed = Signal("s_mixed", NB)
        s_mix_kept = Signal("s_mix_kept", 4 * NB, starts=1)

        x_back = Signal("x_back", 16)
        o_raw_in = Signal("o_raw_in", 16 * 3 * DC)
        o_hi_ready = Signal("o_hi_ready", DC)
        o_split = Signal("o_split", DC, starts=1)
        o_done = [Signal(f"o_done{i}", DC // 2, starts=1) for i in range(2)]
        o_added = [Signal(f"o_added{i}", DC // 2, starts=1) for i in range(2)]

        f_raw_in = Signal("f_raw_in", 16 * 3 * FI)
        f_hi_ready = Signal("f_hi_ready", 3 * FI)
        f_split = Signal("f_split", 3 * FI, starts=1)
        HID = 2 * NW
        DOWN = NW * DC
        hid = Signal("hid", HID * FI, starts=1)
        silued = Signal("silued", HID * FI)
        gated = Signal("gated", HID * FI, starts=1)
        act_hi = Signal("act_hi", HID * FI)
        act_lo = Signal("act_lo", HID * FI, starts=1)
        downed = Signal("downed", DOWN * FI, starts=1)
        ffn_added = Signal("ffn_added", DOWN * FI, starts=1)

        MEETS = 5

        def meet(eng, layer, k):
            eng.drain().then_inc(met, 1)
            eng.wait_ge(met, layer * 5 * MEETS + 5 * (k + 1))
            eng.sem_inc(waits_alone, 1)

        def pieces(ap):
            return ap.rearrange("p (n w) -> p n w", n=NW)

        def banks(b):
            return ps[:, b:b + NW, 0:W]

        def rows_of(t):
            return P if t < QT else NS

        NORMS = [(0, DC, 0, D), (0, NP, 8, WA), (NP, NP, 12, WA), (0, DC, 16, D)]

        def product(pe, out, left, right, n):
            mm = None
            for c in range(n):
                for k, (a, b) in enumerate(((0, 0), (1, 0), (0, 1))):
                    mm = pe.matmul(out, left(a, c), right(b, c), start=(c == 0 and k == 0),
                                   stop=(c == n - 1 and k == 2))
            return mm

        block = ctx.enter_context(nc.Block())

        @block.sync
        def _(sp):
            for signal in (w_split, rope, o_split, f_split, masked, pt_ready, mix_kept, hid, gated, downed,
                           ffn_added, act_lo, s_scores, s_soft, s_mix_kept, *o_done, *o_added):
                sp.sem_inc(signal.sem, 1)
            for dst, src in ((ident, c_ident), (ones, c_ones), (blocks, c_blocks), (cos, c_cos),
                             (sin, c_sin), (mask_a, c_mask_a), (mask_b, c_mask_b)):
                sp.dma_start(dst[:], src).then_inc(consts_in, 16)
            for t in range(QT + 1):
                if t >= 2:
                    sp.wait_ge(x_tile_turned, 2 * (t - 1))
                src = x_prompt[0, t * P:(t + 1) * P, :] if t < QT else x_sample.rearrange("b t d -> (b t) d")
                sp.dma_start(xy_tile[t % 2][0:rows_of(t), 0, :], src).then_inc(x_tile_in[t % 2], 16)
            sp.wait_ge(x_tile_kept, 2 * (QT + 1))
            with sp.Fori(0, DEPTH) as l:
                def layer(ap):
                    return ap[ds(l, 1)]

                for hh in range(2):
                    half = slice(hh * HD, (hh + 1) * HD)
                    for g, src in ((GQA, q_norm_a), (GKA, k_norm_a), (GQB, q_norm_b), (GKB, k_norm_b)):
                        sp.dma_start(gains[half, g:g + 1], layer(src).rearrange("l p -> p l")
                                     ).then_inc(gains_in.sem, 16)
                    sp.dma_start(gains[half, GOUT + NP:GOUT + 2 * NP],
                                 layer(out_norm_b)[:, hh * NP * HD:(hh + 1) * NP * HD].rearrange(
                                     "l (c p) -> p (l c)", p=HD)).then_inc(gains_in.sem, 16)
                for g, src, n in ((GATT, attn_norm, DC), (GFFN, ffn_norm, DC), (GOUT, out_norm_a, NP)):
                    sp.dma_start(gains[:, g:g + n], layer(src).rearrange("l (c p) -> p (l c)", p=P)
                                 ).then_inc(gains_in.sem, 16)
                sp.dma_start(sinks[:], layer(sinks_b).broadcast_to((P, HB))).then_inc(gains_in.sem, 16)
                sp.dma_start(x_spill, xm[:].rearrange("p c t -> p (c t)")).then_inc(spilled.sem, 16)
                sp.wait_ge(gains_in.sem, gains_in.at(l, 16 * N_GAINS))
                sp.sem_inc(waits_alone, 1)
                sp.wait_ge(spilled.sem, spilled.at(l, 16))
                sp.sem_inc(waits_alone, 1)
                meet(sp, l, 0)

                def w_load(u, col):
                    sp.wait_ge(w_split.sem, w_split.at(l, u))
                    sp.sem_inc(waits_alone, 1)
                    sp.dma_start(w_raw[:], layer(w_in)[:, :, ds(col, P)].rearrange(
                        "l (c p) n -> p (l c) n", p=P)).then_inc(w_raw_in.sem, 16)

                w_load(0, COL_KB)
                w_load(1, COL_VB)
                sp.wait_ge(v_kept.sem, v_kept.at(l, 3))
                sp.sem_inc(waits_alone, 1)
                sp.dma_start(layer(new_b_p)[:, 0, :, 1].rearrange("l t h d -> (l t) (h d)"),
                             v_b[:, QT - 1, :]).then_inc(v_out.sem, 16)
                sp.wait_ge(k_kept.sem, k_kept.at(l, 3))
                sp.sem_inc(waits_alone, 1)
                sp.dma_start(layer(new_b_p)[:, 0, :, 0].rearrange("l t h d -> (l t) (h d)"),
                             stage[:, (QT - 1) * P:QT * P]).then_inc(k_out.sem, 16)
                with sp.Fori(0, NP) as p:
                    w_load(2 + 4 * p, COL_KA + p * P)
                    w_load(3 + 4 * p, COL_VA + p * P)
                    w_load(4 + 4 * p, COL_QA + p * P)
                    sp.wait_ge(w_split.sem, w_split.at(l, 5 + 4 * p))
                    sp.sem_inc(waits_alone, 1)
                    for hh in range(2):
                        sp.dma_start(w_raw[:, :, hh * HD:(hh + 1) * HD],
                                     layer(w_in)[:, :, ds(COL_QB + 4 * hh * HD + p * HD, HD)].rearrange(
                                         "l (c p) n -> p (l c) n", p=P)).then_inc(w_raw_in.sem, 16)
                    for kv, kept, out, rows in ((1, v_kept, v_out, v_a[:]),
                                                (0, k_kept, k_out, stage[:, 0:SEQ].rearrange("p (j n) -> p j n", j=QT))):
                        sp.wait_ge(kept.sem, kept.at(l, 6 + 3 * p))
                        sp.sem_inc(waits_alone, 1)
                        sp.dma_start(layer(new_a_p)[:, 0, :, kv].rearrange(
                            "l (j q) h d -> q (l j) (h d)", q=P)[:, :, ds(p * P, P)], rows).then_inc(out.sem, 16)
                sp.wait_ge(v_out.sem, v_out.at(l, 16 * (1 + NP)))
                sp.sem_inc(waits_alone, 1)
                sp.wait_ge(k_out.sem, k_out.at(l, 16 * (1 + NP)))
                sp.sem_inc(waits_alone, 1)
                meet(sp, l, 1)

                for kv in range(2):
                    sp.dma_start(layer(new_a_s)[:, :, LA - TS:LA, kv].rearrange("l b t h d -> (l b) t (h d)"),
                                 kv_rows[:, kv, 0:NP, :].rearrange("q c n -> q (c n)")).then_inc(rows_out.sem, 16)
                    sp.dma_start(layer(new_b_s)[:, :, LB - TS:LB, kv].rearrange("l b t h d -> (l b) t (h d)"),
                                 kv_rows[:, kv, NP, :]).then_inc(rows_out.sem, 16)
                for dst, src in ((mask_s[:, 0:WIN + 4 * NFAR], c_mask_s), (mask_t[:, 0:LB], c_mask_t),
                                 (mask_sn[:], c_mask_sn), (mask_tn[:], c_mask_tn), (pick[:], c_pick)):
                    sp.dma_start(dst, src).then_inc(masks_in.sem, 16)

                def kv_load(i, b):
                    rows = layer(cache_a)[:, ds(b, 1)]
                    sp.dma_start(near[i][:], rows[:, :, LA - WIN:LA].rearrange(
                        "l b (k r) z h d -> (l b k) r (z h d)", r=4)).then_inc(kv_in[i].sem, 16)
                    sp.dma_start(far[i][:], rows[:, :, 0:LA - WIN].rearrange(
                        "l b (k r) z h d -> (l b k) r (z h d)", r=16)[:, 0:4, :]).then_inc(kv_in[i].sem, 16)
                    sp.dma_start(last[i][:], layer(cache_b)[:, ds(b, 1)].rearrange(
                        "l b k z h d -> (l b k) z (h d)")).then_inc(kv_in[i].sem, 16)

                kv_load(0, 0)
                kv_load(1, 1)
                with sp.Fori(0, NB // 2 - 1) as bb:
                    for i in range(2):
                        sp.wait_ge(s_mixed.sem, s_mixed.at(l, 2 * bb + i + 1))
                        sp.sem_inc(waits_alone, 1)
                        kv_load(i, 2 * bb + 2 + i)
                sp.wait_ge(rows_out.sem, rows_out.at(l, 64))
                sp.sem_inc(waits_alone, 1)
                meet(sp, l, 2)

                sp.wait_ge(hf_ready.sem, hf_ready.at(l, 16))
                sp.sem_inc(waits_alone, 1)
                sp.dma_start(xm[:].rearrange("p c t -> p (c t)"), x_spill).then_inc(x_back.sem, 16)
                raw = f_raw[:, 0:D].rearrange("p (c n) -> p c n", c=DC)
                with sp.Fori(0, DC) as u:
                    sp.wait_ge(o_split.sem, o_split.at(l, u))
                    sp.sem_inc(waits_alone, 1)
                    wo = layer(w_out)[:, :, ds(u * P, P)]
                    sp.dma_start(raw[:, 0:NP, :], wo[:, 0:WA].rearrange(
                        "l (c p) n -> p (l c) n", p=P)).then_inc(o_raw_in.sem, 16)
                    for hh in range(2):
                        sp.dma_start(raw[hh * HD:(hh + 1) * HD, NP:DC, :],
                                     wo[:, WA + NP * hh * HD:WA + NP * (hh + 1) * HD].rearrange(
                                         "l (c p) n -> p (l c) n", p=HD)).then_inc(o_raw_in.sem, 16)
                sp.wait_ge(x_back.sem, x_back.at(l, 16))
                sp.sem_inc(waits_alone, 1)
                meet(sp, l, 3)

                with sp.Fori(0, FI) as f:
                    for j in range(3):
                        sp.wait_ge(f_split.sem, f_split.at(l, 3 * f + j))
                        sp.sem_inc(waits_alone, 1)
                        if j < 2:
                            sp.dma_start(f_raw[:].rearrange("p (c n) -> p c n", c=DC),
                                         layer(w_gate_up)[:, :, ds(j * FF + f * 2 * P, 2 * P)].rearrange(
                                             "l (c p) n -> p (l c) n", p=P)).then_inc(f_raw_in.sem, 16)
                        else:
                            sp.dma_start(f_raw[:].rearrange("p (a n) -> p a n", a=2),
                                         layer(w_down)[:, ds(f * 2 * P, 2 * P), :].rearrange(
                                             "l (a p) n -> p (l a) n", p=P)).then_inc(f_raw_in.sem, 16)
                meet(sp, l, 4)
            for t in range(QT + 1):
                sp.wait_ge(y_tile_kept, 2 * (t + 1))
                dst = y_prompt[0, t * P:(t + 1) * P, :] if t < QT else y_sample.rearrange("b t d -> (b t) d")
                sp.dma_start(dst, xy_tile[t % 2][0:rows_of(t), 0, :]).then_inc(y_tile_out[t % 2], 16)
            sp.wait_ge(y_tile_out[0], 16 * 5)
            sp.wait_ge(y_tile_out[1], 16 * 4)

        @block.gpsimd
        def _(pool):
            nc.gpsimd.memset(eps[:], EPS).then_inc(eps_set, 1)

            def split(l, k, raw_in, raw_count, hi_ready_, split_, raw, hi, lo):
                pool.wait_ge(raw_in.sem, raw_in.at(l, raw_count))
                pool.sem_inc(waits_alone, 1)
                nc.gpsimd.tensor_copy(hi, raw).then_inc(hi_ready_.sem, 1)
                pool.wait_ge(hi_ready_.sem, hi_ready_.at(l, k + 1))
                pool.sem_inc(waits_alone, 1)
                nc.gpsimd.tensor_tensor(lo, raw, hi.bitcast(F32), ALU.subtract).then_inc(split_.sem, 1)

            with pool.Fori(0, DEPTH) as l:
                meet(pool, l, 0)
                for n, z in enumerate((q_a[HD:P, 0], q_a[0:HD, 1], q_b[HD:P, 0], q_b[0:HD, 1], q_rows_a[:], q_rows_b[:])):
                    nc.gpsimd.memset(z, 0.0).then_inc(zeroed.sem, 1)
                    pool.wait_ge(zeroed.sem, zeroed.at(l, n + 1))
                    pool.sem_inc(waits_alone, 1)

                def split_w(k, raw_count, slot):
                    split(l, k, w_raw_in, raw_count, w_hi_ready, w_split, w_raw[:], w_hi[:, slot], w_lo[:, slot])

                for u in range(2):
                    split_w(u, RAW[u], u)
                with pool.Fori(0, NP) as p:
                    for b in range(2):
                        pool.dma_start(new_a_s[ds(l, 1), ds(2 * p + b, 1), 0:LA - TS].rearrange("l b t z h d -> (l b) (t z h d)"),
                                       cache_a[ds(l, 1), ds(2 * p + b, 1), TS:LA].rearrange("l b t z h d -> (l b) (t z h d)")
                                       ).then_inc(cache_out.sem, 16)
                        pool.dma_start(new_b_s[ds(l, 1), ds(2 * p + b, 1), 0:LB - TS].rearrange("l b t z h d -> (l b) (t z h d)"),
                                       cache_b[ds(l, 1), ds(2 * p + b, 1), TS:LB].rearrange("l b t z h d -> (l b) (t z h d)")
                                       ).then_inc(cache_out.sem, 16)
                    for j in range(4):
                        pool.wait_ge(projected.sem, projected.at(l, 1 + 4 * p + j))
                        pool.sem_inc(waits_alone, 1)
                        split_w(2 + 4 * p + j, 32 + 80 * p + RAW_P[j], j % 2)
                meet(pool, l, 1)
                meet(pool, l, 2)
                with pool.Fori(0, DC // 2) as dd:
                    for i in range(2):
                        pool.wait_ge(o_done[i].sem, o_done[i].at(l, dd))
                        pool.sem_inc(waits_alone, 1)
                        u = 2 * dd + i
                        split(l, u, o_raw_in, 48 * (u + 1), o_hi_ready, o_split,
                              f_raw[:, 0:D], f_hi[i][:, 0:D], f_lo[i][:, 0:D])
                meet(pool, l, 3)
                with pool.Fori(0, FI) as f:
                    for j in range(3):
                        if j < 2:
                            pool.wait_ge(hid.sem, hid.at(l, HID * f))
                            pool.sem_inc(waits_alone, 1)
                        else:
                            pool.wait_ge(downed.sem, downed.at(l, DOWN * f))
                            pool.sem_inc(waits_alone, 1)
                        u = 3 * f + j
                        split(l, u, f_raw_in, 16 * (u + 1), f_hi_ready, f_split, f_raw[:], f_hi[j][:], f_lo[j][:])
                pool.wait_ge(cache_out.sem, cache_out.at(l, 16 * 2 * NB))
                pool.sem_inc(waits_alone, 1)
                meet(pool, l, 4)

        @block.scalar
        def _(act):
            act.wait_ge(eps_set, 1)

            def norm_squares(l, k, sq, rs, bank):
                first, n, before, width = NORMS[k]
                for c in range(n):
                    if c >= 2:
                        act.wait_ge(sq_summed.sem, sq_summed.at(l, before + c - 1))
                    nc.scalar.activation(sq[c % 2][:], xm[:, first + c, :], ACT.Square).then_inc(sq_ready.sem, 1)
                act.wait_ge(sq_summed.sem, sq_summed.at(l, before + n))
                nc.scalar.activation(pieces(rs[:]), banks(bank), ACT.Sqrt, scale=1.0 / width,
                                     bias=eps[:, 0:1]).then_inc(root_ready.sem, 1)

            def norm_hi(l, k, hf, hi):
                first, n, before, width = NORMS[k]
                for c in range(n):
                    act.wait_ge(hf_ready.sem, hf_ready.at(l, before + c + 1))
                    nc.scalar.activation(hi[:, first + c, :], hf[c % 2][:], ACT.Copy).then_inc(hi_ready.sem, 1)

            with act.Fori(0, DEPTH) as l:
                meet(act, l, 0)
                norm_squares(l, 0, sq1, rs1, 0)
                norm_hi(l, 0, hf1, h_hi)

                def head_squares(unit, bank, roped, n):
                    act.wait_ge(projected.sem, projected.at(l, unit + 1))
                    act.wait_ge(rope.sem, rope.at(l, roped))
                    nc.scalar.activation(pieces(t_buf[1][:]), banks(bank), ACT.Square).then_inc(head_sq.sem, 1)

                def head_roots(bank, n):
                    act.wait_ge(head_summed.sem, head_summed.at(l, n))
                    nc.scalar.activation(pieces(t_buf[1][:]), banks(bank), ACT.Sqrt, scale=1.0 / HD,
                                         bias=eps[:, 0:1]).then_inc(head_root.sem, 1)

                def stage_v(unit, n):
                    act.wait_ge(projected.sem, projected.at(l, unit + 1))
                    act.wait_ge(k_out.sem, k_out.at(l, 16 * n))
                    nc.scalar.activation(pieces(stage[:]), banks(3), ACT.Copy).then_inc(v_staged.sem, 1)

                def keep_k(n, rows):
                    for g in range(2):
                        act.wait_ge(k_turned.sem, k_turned.at(l, 3 * n + g + 1))
                        nc.scalar.activation(stage[:, g * 4 * P:(g + 1) * 4 * P], ps[:, 6 + g, :], ACT.Copy
                                             ).then_inc(k_kept.sem, 1)
                    act.wait_ge(k_turned.sem, k_turned.at(l, 3 * n + 3))
                    nc.scalar.activation(rows, ps[0:NS, 2, 384:512], ACT.Copy).then_inc(k_kept.sem, 1)

                act.wait_ge(projected.sem, projected.at(l, 1))
                act.wait_ge(lo_ready.sem, lo_ready.at(l, 8))
                nc.scalar.activation(pieces(t_buf[1][:]), banks(0), ACT.Square).then_inc(head_sq.sem, 1)
                act.wait_ge(projected.sem, projected.at(l, 2))
                nc.scalar.activation(pieces(stage[:]), banks(3), ACT.Copy).then_inc(v_staged.sem, 1)
                head_roots(0, 1)
                keep_k(0, kv_rows[:, 0, NP, :])
                with act.Fori(0, NP) as p:
                    u, r, h = 2 + 4 * p, K_ROPE + ROPE_P * p, 1 + 3 * p
                    head_squares(u, 0, r, h)
                    stage_v(u + 1, p + 1)
                    head_roots(0, h + 1)
                    head_squares(u + 2, 3, r + K_ROPE, h + 1)
                    keep_k(p + 1, kv_rows[:, 0, ds(p, 1), :].rearrange("q c n -> q (c n)"))
                    head_roots(3, h + 2)
                    head_squares(u + 3, 0, r + K_ROPE + Q_ROPE, h + 2)
                    head_roots(0, h + 3)

                    def softmax(s):
                        m, i, hh = steps[s]
                        n = P * len(key_tiles[s])
                        act.wait_ge(bias_ready.sem, bias_ready.at(l, p * NST + s + 1))
                        nc.scalar.activation(t_buf[s % 3][:, 0:n], t_buf[s % 3][:, 0:n], ACT.Exp, scale=SCALE,
                                             bias=stats[:, 1, s % 4:s % 4 + 1],
                                             accum_out=stats[:, 2, s % 4:s % 4 + 1]).then_inc(exped.sem, 1)
                        if m == "b":
                            nc.scalar.activation(stats[:, 4, s % 4:s % 4 + 1], sink_now[:, hh:hh + 1], ACT.Exp,
                                                 bias=stats[:, 1, s % 4:s % 4 + 1]).then_inc(exped.sem, 1)

                    softmax(0)
                    for s in range(NST):
                        if s + 1 < NST:
                            softmax(s + 1)
                        for g in groups_of[s]:
                            _, a, b = groups[g]
                            if g >= 3:
                                act.wait_ge(mixed.sem, mixed.at(l, p * NST + groups[g - 3][0] + 1))
                            act.wait_ge(p_turned.sem, p_turned.at(l, p * NGR + g + 1))
                            nc.scalar.activation(pt[:, g % 3, 0:(b - a) * P], ps[:, 4 + g % 2, 0:(b - a) * P],
                                                 ACT.Copy).then_inc(pt_ready.sem, 1)
                meet(act, l, 1)

                with act.Fori(0, NB) as b:
                    act.wait_ge(s_scores.sem, s_scores.at(l, b))
                    for pr in range(NP):
                        act.wait_ge(s_turned.sem, s_turned.at(l, 9 * b + 2 * pr + 1))
                        nc.scalar.activation(kt_s[:, pr, 0:WIN], ps[:, 2 * (pr % 2), :], ACT.Copy
                                             ).then_inc(near_kept.sem, 1)
                    act.wait_ge(s_turned.sem, s_turned.at(l, 9 * b + 9))
                    nc.scalar.activation(kt_t[:], ps[:, 7, 256:384], ACT.Copy).then_inc(near_kept.sem, 1)
                    act.wait_ge(s_soft.sem, s_soft.at(l, 10 * b + 5))
                    nc.scalar.activation(p_s[:, 0:NKEYS], p_s[:, 0:NKEYS], ACT.Exp, scale=SCALE,
                                         bias=st_s[:, 3:4], accum_out=st_s[:, 5:6]).then_inc(s_exped.sem, 1)
                    nc.scalar.activation(p_s[:, NKEYS:], p_s[:, NKEYS:], ACT.Exp, scale=SCALE,
                                         bias=st_s[:, 4:5], accum_out=st_s[:, 6:7]).then_inc(s_exped.sem, 1)
                    nc.scalar.activation(st_s[:, 7:8], st_s[:, 10:11], ACT.Exp, bias=st_s[:, 4:5]
                                         ).then_inc(s_exped.sem, 1)
                meet(act, l, 2)

                norm_squares(l, 1, sq2, rs2, 0)
                norm_hi(l, 1, hf2, g_hi)
                act.wait_ge(rs_ready.sem, rs_ready.at(l, 2))
                act.wait_ge(lo_ready.sem, lo_ready.at(l, 12))
                norm_squares(l, 2, sq2, rs2, 3)
                norm_hi(l, 2, hf2, g_hi)
                for i in range(2):
                    act.wait_ge(o_added[i].sem, o_added[i].at(l, DC // 2))
                act.wait_ge(lo_ready.sem, lo_ready.at(l, 16))
                norm_squares(l, 3, sq2, rs2, 0)
                norm_hi(l, 3, hf2, g_hi)
                meet(act, l, 3)

                with act.Fori(0, FI) as f:
                    for k in range(HID):
                        a, n = divmod(k, NW)
                        act.wait_ge(hid.sem, hid.at(l, HID * f + k + 1))
                        act.wait_ge(act_lo.sem, act_lo.at(l, HID * f + max(k - 1, 0)))
                        nc.scalar.activation(silu[:, k % 2, :], ps[:, 2 * (k % 2), 0:W], ACT.Silu
                                             ).then_inc(silued.sem, 1)
                        act.wait_ge(gated.sem, gated.at(l, HID * f + k + 1))
                        act.wait_ge(downed.sem, downed.at(l, DOWN * f))
                        nc.scalar.activation(a_hi[:, a, n * W:(n + 1) * W], silu[:, k % 2, :], ACT.Copy
                                             ).then_inc(act_hi.sem, 1)
                meet(act, l, 4)

        @block.vector
        def _(dve):
            swap = [(i + ROT // 2) % ROT if i < ROT else i for i in range(32)]

            for t in range(QT + 1):
                for g in range(2):
                    dve.wait_ge(x_tile_turned, 2 * t + g + 1)
                    w = rows_of(t)
                    nc.vector.tensor_copy(xm[:, 4 * g:4 * g + 4, t * P:t * P + w],
                                          ps[:, (2 * t + g) % 8, :].rearrange("p (c n) -> p c n", c=4)[:, :, 0:w]
                                          ).then_inc(x_tile_kept, 1)

            def norm_chunks(l, k, gain, hf, rs, hi, lo):
                first, n, before, width = NORMS[k]
                dve.wait_ge(root_ready.sem, root_ready.at(l, k + 1))
                nc.vector.reciprocal(rs[:], rs[:]).then_inc(rs_ready.sem, 1)
                dve.wait_ge(rs_ready.sem, rs_ready.at(l, k + 1))
                for c in range(n + 1):
                    if c < n:
                        if c >= 2:
                            dve.wait_ge(lo_ready.sem, lo_ready.at(l, before + c - 1))
                        nc.vector.scalar_tensor_tensor(hf[c % 2][:], xm[:, first + c, :],
                                                       gains[:, gain + first + c:gain + first + c + 1], rs[:],
                                                       ALU.mult, ALU.mult).then_inc(hf_ready.sem, 1)
                    if c >= 1:
                        dve.wait_ge(hi_ready.sem, hi_ready.at(l, before + c))
                        nc.vector.tensor_tensor(lo[:, first + c - 1, :], hf[(c - 1) % 2][:],
                                                hi[:, first + c - 1, :].bitcast(F32), ALU.subtract
                                                ).then_inc(lo_ready.sem, 1)

            with dve.Fori(0, DEPTH) as l:
                meet(dve, l, 0)
                norm_chunks(l, 0, GATT, hf1, rs1, h_hi, h_lo)

                def roped(unit, bank, gain, r, root):
                    dve.wait_ge(projected.sem, projected.at(l, unit + 1))
                    dve.wait_ge(rope.sem, rope.at(l, r))
                    dve.wait_ge(head_sq.sem, head_sq.at(l, root))
                    nc.vector.tensor_scalar(pieces(t_buf[0][:]), banks(bank), gains[:, gain:gain + 1], None,
                                            ALU.mult).then_inc(rope.sem, 1)
                    dve.wait_ge(rope.sem, rope.at(l, r + 1))
                    dve.sem_inc(waits_alone, 1)
                    nc.vector.stream_shuffle(t_buf[2][:], t_buf[0][:], swap).then_inc(rope.sem, 1)
                    dve.wait_ge(rope.sem, rope.at(l, r + 2))
                    nc.vector.tensor_tensor(t_buf[0][:], t_buf[0][:], cos[:], ALU.mult).then_inc(rope.sem, 1)
                    nc.vector.tensor_tensor(t_buf[2][:], t_buf[2][:], sin[:], ALU.mult).then_inc(rope.sem, 1)
                    dve.wait_ge(rope.sem, rope.at(l, r + 4))
                    nc.vector.tensor_tensor(t_buf[0][:], t_buf[0][:], t_buf[2][:], ALU.add).then_inc(rope.sem, 1)
                    dve.wait_ge(head_root.sem, head_root.at(l, root))
                    nc.vector.reciprocal(t_buf[1][:], t_buf[1][:]).then_inc(rope.sem, 1)
                    dve.wait_ge(rope.sem, rope.at(l, r + 6))

                def k_rope(unit, gain, r, root, kt, new):
                    roped(unit, 0, gain, r, root)
                    nc.vector.tensor_tensor(kt[:], t_buf[0][:], t_buf[1][:], ALU.mult).then_inc(rope.sem, 1)
                    dve.wait_ge(rope.sem, rope.at(l, r + 7))
                    nc.vector.tensor_copy(new, kt[:, SEQ:T]).then_inc(rope.sem, 1)

                def q_rope(unit, bank, gain, r, root, q, rows):
                    roped(unit, bank, gain, r, root)
                    for hh in range(2):
                        half = slice(hh * HD, (hh + 1) * HD)
                        nc.vector.tensor_tensor(q[half, hh, :], t_buf[0][half, 0:SEQ], t_buf[1][half, 0:SEQ],
                                                ALU.mult).then_inc(rope.sem, 1)
                    for hh in range(2):
                        half = slice(hh * HD, (hh + 1) * HD)
                        nc.vector.tensor_tensor(rows(half, hh),
                                                t_buf[0][half, SEQ:T].rearrange("p (b t) -> p b t", t=TS),
                                                t_buf[1][half, SEQ:T].rearrange("p (b t) -> p b t", t=TS),
                                                ALU.mult).then_inc(rope.sem, 1)

                def keep_v(n, v, rows):
                    dve.wait_ge(v_out.sem, v_out.at(l, 16 * n))
                    for g in range(2):
                        dve.wait_ge(v_turned.sem, v_turned.at(l, 3 * n + g + 1))
                        nc.vector.tensor_copy(v[:, 4 * g:4 * g + 4, :],
                                              ps[:, 6 + g, :].rearrange("p (j n) -> p j n", j=4)).then_inc(v_kept.sem, 1)
                    dve.wait_ge(v_turned.sem, v_turned.at(l, 3 * n + 3))
                    nc.vector.tensor_copy(rows, ps[0:NS, 5, 384:512]).then_inc(v_kept.sem, 1)

                dve.wait_ge(zeroed.sem, zeroed.at(l, 6))
                dve.wait_ge(lo_ready.sem, lo_ready.at(l, 8))
                k_rope(0, GKB, 0, 1, kt_b, k_new_b[:])
                keep_v(0, v_b, kv_rows[:, 1, NP, :])
                with dve.Fori(0, NP) as p:
                    u, r, h = 2 + 4 * p, K_ROPE + ROPE_P * p, 1 + 3 * p
                    k_rope(u, GKA, r, h + 1, kt_a, k_new_a[:, ds(p, 1), :].rearrange("q c n -> q (c n)"))
                    keep_v(p + 1, v_a, kv_rows[:, 1, ds(p, 1), :].rearrange("q c n -> q (c n)"))
                    q_rope(u + 2, 3, GQA, r + K_ROPE, h + 2, q_a,
                           lambda half, hh: q_rows_a[half, ds(p, 1), :, ds(2 * p + hh, 1), :].rearrange(
                               "q c b h t -> q (c b) (h t)"))
                    q_rope(u + 3, 0, GQB, r + K_ROPE + Q_ROPE, h + 3, q_b,
                           lambda half, hh: q_rows_b[half, :, ds(p + NP * hh, 1), :].rearrange("q b h t -> q b (h t)"))
                    nc.vector.tensor_copy(sink_now[:].rearrange("p (a b) -> p a b", b=1),
                                          sinks[:].rearrange("p (a b) -> p a b", a=2)[:, :, ds(p, 1)]
                                          ).then_inc(sink_ready.sem, 1)
                    dve.wait_ge(sink_ready.sem, sink_ready.at(l, 2 * p + 1))
                    nc.vector.tensor_scalar(sink_raw[:], sink_now[:], 1.0 / SCALE, None, ALU.mult
                                            ).then_inc(sink_ready.sem, 1)
                    dve.wait_ge(sink_ready.sem, sink_ready.at(l, 2 * p + 2))
                    dve.wait_ge(rope.sem, rope.at(l, r + ROPE_P))

                    def mask_and_max(s):
                        m, i, hh = steps[s]
                        n = P * len(key_tiles[s])
                        mask = mask_a[:, SEQ - n:] if m == "a" else mask_b[:, 2 * P - n:]
                        if s >= 3:
                            dve.wait_ge(p_turned.sem, p_turned.at(l, p * NGR + groups_of[s - 3][-1] + 1))
                        dve.wait_ge(scores.sem, scores.at(l, p * NST + s + 1))
                        dve.sem_inc(waits_alone, 1)
                        nc.vector.tensor_tensor_reduce(
                            t_buf[s % 3][:, 0:n],
                            ps[:, 2 * (s % 2):2 * (s % 2) + 2, :].rearrange("p b c -> p (b c)")[:, 0:n], mask,
                            1.0, -3e38 if m == "a" else sink_raw[:, hh:hh + 1], ALU.add, ALU.max,
                            stats[:, 0, s % 4:s % 4 + 1]).then_inc(masked.sem, 1)
                        dve.wait_ge(masked.sem, masked.at(l, p * NST + s + 1))
                        nc.vector.tensor_scalar(stats[:, 1, s % 4:s % 4 + 1], stats[:, 0, s % 4:s % 4 + 1],
                                                -SCALE, None, ALU.mult).then_inc(bias_ready.sem, 1)

                    def normalize(s):
                        m, i, hh = steps[s]
                        n = P * len(key_tiles[s])
                        c = slice(s % 4, s % 4 + 1)
                        dve.wait_ge(exped.sem, exped.at(l, p * NEXP + exps_to[s]))
                        if m == "b":
                            nc.vector.tensor_tensor(stats[:, 2, c], stats[:, 2, c], stats[:, 4, c], ALU.add
                                                    ).then_inc(sum_ready.sem, 1)
                            dve.wait_ge(sum_ready.sem, sum_ready.at(l, p * NEXP + exps_to[s] - 1))
                        nc.vector.reciprocal(stats[:, 3, c], stats[:, 2, c]).then_inc(sum_ready.sem, 1)
                        dve.wait_ge(sum_ready.sem, sum_ready.at(l, p * NEXP + exps_to[s]))
                        nc.vector.tensor_scalar(t_buf[s % 3][:, 0:n], t_buf[s % 3][:, 0:n], stats[:, 3, c], None,
                                                ALU.mult).then_inc(probs.sem, 1)

                    def keep_mix(s):
                        m, i, hh = steps[s]
                        half = slice(hh * HD, (hh + 1) * HD)
                        dve.wait_ge(mixed.sem, mixed.at(l, p * NST + s + 1))
                        nc.vector.tensor_copy(
                            xm[half, ds(p + (NP if m == "b" else 0), 1), i * P:(i + 1) * P].rearrange("q c n -> q (c n)"),
                            ps[half, 6 + s % 2, 0:P]).then_inc(mix_kept.sem, 1)

                    mask_and_max(0)
                    for s in range(NST):
                        if s + 1 < NST:
                            mask_and_max(s + 1)
                        normalize(s)
                        if s >= 2:
                            keep_mix(s - 2)
                    keep_mix(NST - 2)
                    keep_mix(NST - 1)
                meet(dve, l, 1)

                dve.wait_ge(masks_in.sem, masks_in.at(l, 80))
                nc.vector.tensor_tensor(p_s[:, 0:HB], sinks[0:NS, :], pick[:], ALU.mult).then_inc(sink_s.sem, 1)
                dve.wait_ge(sink_s.sem, sink_s.at(l, 1))
                nc.vector.reduce_sum(st_s[:, 10:11], p_s[:, 0:HB], AX.X).then_inc(sink_s.sem, 1)
                dve.wait_ge(sink_s.sem, sink_s.at(l, 2))
                nc.vector.tensor_scalar(st_s[:, 11:12], st_s[:, 10:11], 1.0 / SCALE, None, ALU.mult
                                        ).then_inc(sink_s.sem, 1)
                dve.wait_ge(sink_s.sem, sink_s.at(l, 3))
                dve.sem_inc(waits_alone, 1)
                with dve.Fori(0, NB) as b:
                    dve.wait_ge(s_scores.sem, s_scores.at(l, b))
                    dve.wait_ge(s_soft.sem, s_soft.at(l, 10 * b))
                    nc.vector.tensor_copy(q_now_a[:], q_rows_a[:, :, ds(b, 1)].rearrange("q c b h t -> q c (b h t)")
                                          ).then_inc(s_query.sem, 1)
                    nc.vector.tensor_copy(q_now_b[:], q_rows_b[:, ds(b, 1)].rearrange("q b h t -> q (b h t)")
                                          ).then_inc(s_query.sem, 1)
                    nc.vector.tensor_copy(mask_s[:, WIN + 4 * NFAR:], mask_sn[:, ds(b * NS, NS)]).then_inc(s_query.sem, 1)
                    nc.vector.tensor_copy(mask_t[:, LB:], mask_tn[:, ds(b * NS, NS)]).then_inc(s_query.sem, 1)
                    for pr in range(NP):
                        dve.wait_ge(s_turned.sem, s_turned.at(l, 9 * b + 2 * pr + 2))
                        nc.vector.tensor_copy(kt_s[:, pr, WIN:], ps[:, 2 * (pr % 2) + 1, 0:4 * NFAR]
                                              ).then_inc(far_kept.sem, 1)
                    dve.wait_ge(s_scores.sem, s_scores.at(l, b + 1))
                    dve.wait_ge(s_query.sem, s_query.at(l, 4 * b + 4))
                    dve.sem_inc(waits_alone, 1)
                    nc.vector.tensor_tensor_reduce(p_s[:, 0:WIN], ps[0:NS, 5, :], mask_s[:, 0:WIN], 1.0, -3e38,
                                                   ALU.add, ALU.max, st_s[:, 0:1]).then_inc(s_soft.sem, 1)
                    dve.wait_ge(s_soft.sem, s_soft.at(l, 10 * b + 1))
                    dve.sem_inc(waits_alone, 1)
                    nc.vector.tensor_tensor_reduce(p_s[:, WIN:NKEYS], ps[0:NS, 6, 0:NKEYS - WIN], mask_s[:, WIN:], 1.0,
                                                   st_s[:, 0:1], ALU.add, ALU.max, st_s[:, 1:2]).then_inc(s_soft.sem, 1)
                    nc.vector.tensor_tensor_reduce(p_s[:, NKEYS:], ps[0:NS, 7, 0:LB + NS], mask_t[:], 1.0,
                                                   st_s[:, 11:12], ALU.add, ALU.max, st_s[:, 2:3]).then_inc(s_soft.sem, 1)
                    dve.wait_ge(s_soft.sem, s_soft.at(l, 10 * b + 3))
                    nc.vector.tensor_scalar(st_s[:, 3:4], st_s[:, 1:2], -SCALE, None, ALU.mult).then_inc(s_soft.sem, 1)
                    nc.vector.tensor_scalar(st_s[:, 4:5], st_s[:, 2:3], -SCALE, None, ALU.mult).then_inc(s_soft.sem, 1)
                    dve.wait_ge(s_exped.sem, s_exped.at(l, 3 * b + 3))
                    nc.vector.tensor_tensor(st_s[:, 6:7], st_s[:, 6:7], st_s[:, 7:8], ALU.add).then_inc(s_soft.sem, 1)
                    dve.wait_ge(s_soft.sem, s_soft.at(l, 10 * b + 6))
                    nc.vector.reciprocal(st_s[:, 8:9], st_s[:, 5:6]).then_inc(s_soft.sem, 1)
                    nc.vector.reciprocal(st_s[:, 9:10], st_s[:, 6:7]).then_inc(s_soft.sem, 1)
                    dve.wait_ge(s_soft.sem, s_soft.at(l, 10 * b + 8))
                    nc.vector.tensor_scalar(p_s[:, 0:NKEYS], p_s[:, 0:NKEYS], st_s[:, 8:9], None, ALU.mult
                                            ).then_inc(s_soft.sem, 1)
                    nc.vector.tensor_scalar(p_s[:, NKEYS:], p_s[:, NKEYS:], st_s[:, 9:10], None, ALU.mult
                                            ).then_inc(s_soft.sem, 1)
                    dve.wait_ge(s_pturned.sem, s_pturned.at(l, b + 1))
                    for rows, a, z in ((P, 0, 4), (NFAR, 4, 8), (NS, 8, 9), (P, 9, 10), (NS, 10, 11)):
                        nc.vector.tensor_copy(pt_s[0:rows, a:z, :],
                                              ps[0:rows, 4, a * NS:z * NS].rearrange("p (a n) -> p a n", n=NS)
                                              ).then_inc(s_pkept.sem, 1)
                    dve.wait_ge(s_mixed.sem, s_mixed.at(l, b + 1))
                    for hh in range(2):
                        half = slice(hh * HD, (hh + 1) * HD)
                        nc.vector.tensor_copy(xm[half, 0:NP, ds(SEQ + b * TS, TS)],
                                              ps[half, 4, 384:416].rearrange("p (c n) -> p c n", c=NP)[
                                                  :, :, hh * TS:(hh + 1) * TS]).then_inc(s_mix_kept.sem, 1)
                        nc.vector.tensor_copy(xm[half, NP:2 * NP, ds(SEQ + b * TS, TS)],
                                              ps[half, 4, 416 + hh * 16:432 + hh * 16].rearrange(
                                                  "p (c n) -> p c n", c=NP)).then_inc(s_mix_kept.sem, 1)
                meet(dve, l, 2)

                norm_chunks(l, 1, GOUT, hf2, rs2, g_hi, g_lo)
                norm_chunks(l, 2, GOUT, hf2, rs2, g_hi, g_lo)
                dve.wait_ge(x_back.sem, x_back.at(l, 16))
                dve.sem_inc(waits_alone, 1)
                with dve.Fori(0, DC // 2) as dd:
                    for i in range(2):
                        dve.wait_ge(o_done[i].sem, o_done[i].at(l, dd + 1))
                        chunk = pieces(xm[:, ds(2 * dd + i, 1), :].rearrange("p c t -> p (c t)"))
                        nc.vector.tensor_tensor(chunk, chunk, banks(3 * i), ALU.add).then_inc(o_added[i].sem, 1)
                norm_chunks(l, 3, GFFN, hf2, rs2, g_hi, g_lo)
                meet(dve, l, 3)

                with dve.Fori(0, FI) as f:
                    for k in range(HID):
                        a, n = divmod(k, NW)
                        dve.wait_ge(silued.sem, silued.at(l, HID * f + k + 1))
                        nc.vector.tensor_tensor(silu[:, k % 2, :], silu[:, k % 2, :], ps[:, 2 * (k % 2) + 1, 0:W],
                                                ALU.mult).then_inc(gated.sem, 1)
                        dve.wait_ge(act_hi.sem, act_hi.at(l, HID * f + k + 1))
                        nc.vector.tensor_tensor(a_lo[:, a, n * W:(n + 1) * W], silu[:, k % 2, :],
                                                a_hi[:, a, n * W:(n + 1) * W].bitcast(F32), ALU.subtract
                                                ).then_inc(act_lo.sem, 1)
                    for n in range(NW):
                        for d in range(DC):
                            dve.wait_ge(downed.sem, downed.at(l, DOWN * f + n * DC + d + 1))
                            xs = xm[:, d, n * W:(n + 1) * W]
                            nc.vector.tensor_tensor(xs, xs, ps[:, 4 + (n * DC + d) % 4, 0:W], ALU.add
                                                    ).then_inc(ffn_added.sem, 1)
                meet(dve, l, 4)
            for t in range(QT + 1):
                if t >= 2:
                    dve.wait_ge(y_tile_out[t % 2], 16 * (t // 2))
                for g in range(2):
                    dve.wait_ge(y_tile_turned, 2 * t + g + 1)
                    w = rows_of(t)
                    nc.vector.tensor_copy(xy_tile[t % 2][0:w, 0, g * 512:(g + 1) * 512],
                                          ps[0:w, (2 * t + g) % 8, :]).then_inc(y_tile_kept, 1)

        @block.tensor
        def _(pe):
            pe.wait_ge(consts_in, 16 * 7)
            for t in range(QT + 1):
                pe.wait_ge(x_tile_in[t % 2], 16 * (t // 2 + 1))
                w = rows_of(t)
                for g in range(2):
                    if 2 * t + g >= 8:
                        pe.wait_ge(x_tile_kept, 2 * t + g - 7)
                    for c in range(4):
                        mm = pe.transpose(ps[:, (2 * t + g) % 8, c * P:c * P + w],
                                          xy_tile[t % 2][0:w, 0, (4 * g + c) * P:(4 * g + c + 1) * P], ident[0:w, 0:w])
                    mm.then_inc(x_tile_turned, 1)

            def sum_squares(l, k, sq, bank):
                first, n, before, width = NORMS[k]
                for c in range(n):
                    pe.wait_ge(sq_ready.sem, sq_ready.at(l, before + c + 1))
                    for w in range(NW):
                        mm = pe.matmul(ps[:, bank + w, 0:W], ones[:], sq[c % 2][:, w * W:(w + 1) * W],
                                       start=(c == 0), stop=(c == n - 1))
                    mm.then_inc(sq_summed.sem, 1)

            with pe.Fori(0, DEPTH) as l:
                meet(pe, l, 0)
                sum_squares(l, 0, sq1, 0)
                pe.wait_ge(lo_ready.sem, lo_ready.at(l, 8))
                pe.wait_ge(zeroed.sem, zeroed.at(l, 6))

                def project(u, slot, bank, rest=None):
                    pe.wait_ge(w_split.sem, w_split.at(l, u + 1))
                    for n in range(NW):
                        if rest is not None and n == NW - 1:
                            pe.wait_ge(rest[0].sem, rest[0].at(l, rest[1]))
                        mm = product(pe, ps[:, bank + n, 0:W], lambda a, c: (w_hi, w_lo)[a][:, slot, c, :],
                                     lambda a, c: (h_hi, h_lo)[a][:, c, n * W:(n + 1) * W], DC)
                    mm.then_inc(projected.sem, 1)

                def sum_heads(bank, count, r):
                    pe.wait_ge(head_sq.sem, head_sq.at(l, count))
                    pe.wait_ge(rope.sem, rope.at(l, r + 1))
                    for n in range(NW):
                        mm = pe.matmul(ps[:, bank + n, 0:W], blocks[:], t_buf[1][:, n * W:(n + 1) * W],
                                       start=True, stop=True)
                    mm.then_inc(head_summed.sem, 1)

                def turn(src, rest, done):
                    for g in range(2):
                        for c in range(4):
                            mm = pe.transpose(ps[:, 6 + g, c * P:(c + 1) * P],
                                              src[:, (4 * g + c) * P:(4 * g + c + 1) * P], ident[:])
                        mm.then_inc(done.sem, 1)
                    pe.transpose(ps[0:NS, rest, 384:512], src[:, SEQ:T], ident[:]).then_inc(done.sem, 1)

                project(0, 0, 0)
                project(1, 1, 3)
                sum_heads(0, 1, 0)
                pe.wait_ge(v_staged.sem, v_staged.at(l, 1))
                turn(stage, 5, v_turned)
                pe.wait_ge(rope.sem, rope.at(l, K_ROPE))
                pe.wait_ge(v_kept.sem, v_kept.at(l, 3))
                turn(kt_b, 2, k_turned)
                with pe.Fori(0, NP) as p:
                    u, r, h = 2 + 4 * p, K_ROPE + ROPE_P * p, 1 + 3 * p
                    pe.wait_ge(k_kept.sem, k_kept.at(l, 3 * p + 3))
                    pe.wait_ge(masked.sem, masked.at(l, NST * p))
                    pe.wait_ge(pt_ready.sem, pt_ready.at(l, NGR * p))
                    pe.wait_ge(mix_kept.sem, mix_kept.at(l, NST * p))
                    project(u, 0, 0)
                    project(u + 1, 1, 3)
                    sum_heads(0, h + 1, r)
                    pe.wait_ge(v_staged.sem, v_staged.at(l, p + 2))
                    turn(stage, 5, v_turned)
                    project(u + 2, 0, 3, (v_kept, 3 * p + 6))
                    pe.wait_ge(rope.sem, rope.at(l, r + K_ROPE))
                    pe.wait_ge(v_kept.sem, v_kept.at(l, 3 * p + 6))
                    turn(kt_a, 2, k_turned)
                    project(u + 3, 1, 0, (k_kept, 3 * p + 6))
                    sum_heads(3, h + 2, r + K_ROPE)
                    sum_heads(0, h + 3, r + K_ROPE + Q_ROPE)
                    pe.wait_ge(rope.sem, rope.at(l, r + ROPE_P))
                    pe.wait_ge(k_kept.sem, k_kept.at(l, 3 * p + 6))

                    def score(s):
                        m, i, hh = steps[s]
                        q, kt = (q_a, kt_a) if m == "a" else (q_b, kt_b)
                        n, first = P * len(key_tiles[s]), P * key_tiles[s][0]
                        if s >= 2:
                            pe.wait_ge(masked.sem, masked.at(l, p * NST + s - 1))
                        for c in range(0, n, 512):
                            w = min(512, n - c)
                            mm = pe.matmul(ps[:, 2 * (s % 2) + c // 512, 0:w], q[:, hh, i * P:(i + 1) * P],
                                           kt[:, first + c:first + c + w], start=True, stop=True)
                        mm.then_inc(scores.sem, 1)

                    def turn_probs(s):
                        pe.wait_ge(probs.sem, probs.at(l, p * NST + s + 1))
                        for g in groups_of[s]:
                            _, a, b = groups[g]
                            if g >= 2:
                                pe.wait_ge(pt_ready.sem, pt_ready.at(l, p * NGR + g - 1))
                            for c in range(a, b):
                                mm = pe.transpose(ps[:, 4 + g % 2, (c - a) * P:(c - a + 1) * P],
                                                  t_buf[s % 3][:, c * P:(c + 1) * P], ident[:])
                            mm.then_inc(p_turned.sem, 1)

                    def mix(s):
                        m, i, hh = steps[s]
                        v = v_a if m == "a" else v_b
                        if s >= 2:
                            pe.wait_ge(mix_kept.sem, mix_kept.at(l, p * NST + s - 1))
                        for g in groups_of[s]:
                            _, a, b = groups[g]
                            pe.wait_ge(pt_ready.sem, pt_ready.at(l, p * NGR + g + 1))
                            for c in range(a, b):
                                mm = pe.matmul(ps[:, 6 + s % 2, 0:P], v[:, key_tiles[s][c], :],
                                               pt[:, g % 3, (c - a) * P:(c - a + 1) * P],
                                               start=(c == 0), stop=(c == len(key_tiles[s]) - 1))
                        mm.then_inc(mixed.sem, 1)

                    score(0)
                    for s in range(NST):
                        if s + 1 < NST:
                            score(s + 1)
                        turn_probs(s)
                        if s >= 1:
                            mix(s - 1)
                    mix(NST - 1)
                meet(pe, l, 1)

                with pe.Fori(0, NB // 2) as bb:
                    for i in range(2):
                        b = 2 * bb + i
                        pe.wait_ge(kv_in[i].sem, kv_in[i].at(l, 48 * (bb + 1)))
                        pe.sem_inc(waits_alone, 1)
                        for pr in range(NP):
                            if pr >= 2:
                                pe.wait_ge(near_kept.sem, near_kept.at(l, 5 * b + pr - 1))
                                pe.sem_inc(waits_alone, 1)
                            for c in range(4):
                                mm = pe.transpose(ps[:, 2 * (pr % 2), c * P:(c + 1) * P],
                                                  near[i][:, c, pr * P:(pr + 1) * P], ident[:])
                            mm.then_inc(s_turned.sem, 1)
                            if pr >= 2:
                                pe.wait_ge(far_kept.sem, far_kept.at(l, 4 * b + pr - 1))
                                pe.sem_inc(waits_alone, 1)
                            for c in range(4):
                                mm = pe.transpose(ps[:, 2 * (pr % 2) + 1, c * NFAR:(c + 1) * NFAR],
                                                  far[i][:, c, pr * P:(pr + 1) * P], ident[0:NFAR, 0:NFAR])
                            mm.then_inc(s_turned.sem, 1)
                        pe.transpose(ps[:, 7, 256:384], last[i][:, 0, :], ident[:]).then_inc(s_turned.sem, 1)
                        pe.wait_ge(near_kept.sem, near_kept.at(l, 5 * b + 5))
                        pe.wait_ge(far_kept.sem, far_kept.at(l, 4 * b + 4))
                        pe.wait_ge(s_query.sem, s_query.at(l, 4 * b + 4))
                        for out, keys in ((ps[0:NS, 5, :], lambda pr: kt_s[:, pr, 0:WIN]),
                                          (ps[0:NS, 6, 0:4 * NFAR], lambda pr: kt_s[:, pr, WIN:]),
                                          (ps[0:NS, 6, 4 * NFAR:NKEYS - WIN], lambda pr: k_new_a[:, pr, :])):
                            for pr in range(NP):
                                pe.matmul(out, q_now_a[:, pr, :], keys(pr), start=(pr == 0), stop=(pr == NP - 1))
                        pe.matmul(ps[0:NS, 7, 0:LB], q_now_b[:], kt_t[:], start=True, stop=True)
                        pe.matmul(ps[0:NS, 7, LB:LB + NS], q_now_b[:], k_new_b[:], start=True, stop=True
                                  ).then_inc(s_scores.sem, 1)
                        pe.wait_ge(s_soft.sem, s_soft.at(l, 10 * b + 10))
                        pe.sem_inc(waits_alone, 1)
                        cols = [(c * P, P) for c in range(4)] + [(WIN + c * NFAR, NFAR) for c in range(4)] + \
                               [(WIN + 4 * NFAR, NS), (NKEYS, LB), (NKEYS + LB, NS)]
                        for c, (a, w) in enumerate(cols):
                            mm = pe.transpose(ps[0:w, 4, c * NS:(c + 1) * NS], p_s[:, a:a + w], ident[0:NS, 0:NS])
                        mm.then_inc(s_pturned.sem, 1)
                        pe.wait_ge(s_pkept.sem, s_pkept.at(l, 5 * b + 5))
                        pe.wait_ge(s_mix_kept.sem, s_mix_kept.at(l, 4 * b))
                        for pr in range(NP):
                            out = ps[:, 4, 384 + 8 * pr:392 + 8 * pr]
                            v_cols = slice(WA + pr * P, WA + (pr + 1) * P)
                            for c in range(4):
                                pe.matmul(out, near[i][:, c, v_cols], pt_s[:, c, 8 * pr:8 * pr + 8],
                                          start=(c == 0), stop=False)
                            for c in range(4):
                                pe.matmul(out, far[i][:, c, v_cols], pt_s[0:NFAR, 4 + c, 8 * pr:8 * pr + 8],
                                          start=False, stop=False)
                            pe.matmul(out, kv_rows[:, 1, pr, :], pt_s[0:NS, 8, 8 * pr:8 * pr + 8],
                                      start=False, stop=True)
                        pe.matmul(ps[:, 4, 416:448], last[i][:, 1, :], pt_s[:, 9, :], start=True, stop=False)
                        pe.matmul(ps[:, 4, 416:448], kv_rows[:, 1, NP, :], pt_s[0:NS, 10, :], start=False, stop=True
                                  ).then_inc(s_mixed.sem, 1)
                meet(pe, l, 2)

                sum_squares(l, 1, sq2, 0)
                sum_squares(l, 2, sq2, 3)
                pe.wait_ge(lo_ready.sem, lo_ready.at(l, 16))
                pe.sem_inc(waits_alone, 1)
                with pe.Fori(0, DC // 2) as dd:
                    for i in range(2):
                        pe.wait_ge(o_split.sem, o_split.at(l, 2 * dd + i + 1))
                        pe.wait_ge(o_added[i].sem, o_added[i].at(l, dd))
                        for n in range(NW):
                            mm = product(pe, ps[:, 3 * i + n, 0:W], lambda a, c: (f_hi, f_lo)[a][i][:, c * P:(c + 1) * P],
                                         lambda a, c: (g_hi, g_lo)[a][:, c, n * W:(n + 1) * W], DC)
                        mm.then_inc(o_done[i].sem, 1)
                pe.wait_ge(o_added[0].sem, o_added[0].at(l, DC // 2))
                sum_squares(l, 3, sq2, 0)
                meet(pe, l, 3)

                with pe.Fori(0, FI) as f:
                    pe.wait_ge(f_split.sem, f_split.at(l, 3 * f + 2))
                    for k in range(HID):
                        a, n = divmod(k, NW)
                        pe.wait_ge(gated.sem, gated.at(l, HID * f + max(k - 1, 0)))
                        for j in range(2):
                            mm = product(pe, ps[:, 2 * (k % 2) + j, 0:W],
                                         lambda h, c: (f_hi, f_lo)[h][j][:, c * 2 * P + a * P:c * 2 * P + (a + 1) * P],
                                         lambda h, c: (g_hi, g_lo)[h][:, c, n * W:(n + 1) * W], DC)
                        mm.then_inc(hid.sem, 1)
                    pe.wait_ge(f_split.sem, f_split.at(l, 3 * f + 3))
                    for n in range(NW):
                        pe.wait_ge(act_lo.sem, act_lo.at(l, HID * f + NW + n + 1))
                        for d in range(DC):
                            x = n * DC + d
                            pe.wait_ge(ffn_added.sem, ffn_added.at(l, DOWN * f + max(x - 3, 0)))
                            product(pe, ps[:, 4 + x % 4, 0:W],
                                    lambda h, c: (f_hi, f_lo)[h][2][:, c * D + d * P:c * D + (d + 1) * P],
                                    lambda h, c: (a_hi, a_lo)[h][:, c, n * W:(n + 1) * W], 2
                                    ).then_inc(downed.sem, 1)
                meet(pe, l, 4)
            for t in range(QT + 1):
                w = rows_of(t)
                for g in range(2):
                    if 2 * t + g >= 8:
                        pe.wait_ge(y_tile_kept, 2 * t + g - 7)
                    for c in range(4):
                        mm = pe.transpose(ps[0:w, (2 * t + g) % 8, c * P:(c + 1) * P],
                                          xm[:, 4 * g + c, t * P:t * P + w], ident[:])
                    mm.then_inc(y_tile_turned, 1)


_INS = ["x_prompt", "x_sample", "cache_a", "cache_b", "attn_norm", "w_in", "q_norm_a", "k_norm_a", "q_norm_b",
        "k_norm_b", "sinks_b", "out_norm_a", "out_norm_b", "w_out", "ffn_norm", "w_gate_up", "w_down"]
_OUTS = [(1, SEQ, D), (NB, TS, D), (DEPTH, 1, SEQ, 2, HA, HD), (DEPTH, 1, LB, 2, KVB, HD),
         (DEPTH, NB, LA, 2, HA, HD), (DEPTH, NB, LB, 2, KVB, HD)]


def kernel(**inputs):
    import concourse.bacc as _bacc
    from concourse.bass_utils import run_bass_kernel_spmd as _run

    nc = _bacc.Bacc("TRN2", target_bir_lowering=False, num_devices=1)
    arrays, args = {}, []
    tables = constants()
    for name, a in [(n, np.ascontiguousarray(inputs[n])) for n in _INS] + list(tables.items()):
        arrays[f"in_{name}_dram"] = a
        args.append(nc.dram_tensor(f"in_{name}_dram", a.shape, mybir.dt.from_np(a.dtype), kind="ExternalInput").ap())
    for i, shape in enumerate(_OUTS):
        args.append(nc.dram_tensor(f"out_{i}_dram", shape, F32, kind="ExternalOutput").ap())
    trunk(nc, *args)
    r = _run(nc, [arrays], core_ids=[0])
    return tuple(r.results[0][f"out_{i}_dram"] for i in range(len(_OUTS)))
```

```python
from contextlib import ExitStack
import math

import numpy as np
import concourse.bass as bass
from concourse import mybir

F32 = mybir.dt.float32
F32R = mybir.dt.float32r
ACT = mybir.ActivationFunctionType
ALU = mybir.AluOpType
AX = mybir.AxisListType
ds = bass.ds

P = 128
D = 1024
DC = D // P
SEQ = 1024
QT = SEQ // P
DEPTH = 2
NB, TS = 8, 4
NS = NB * TS
T = SEQ + NS
NW = 3
W = T // NW
HD = 64
HA, HB, KVB = 8, 8, 2
NP = HA // 2
LA, LB = 2048, 128
PAST = 4096
FF = 2816
FI = FF // (2 * P)
ROT = HD // 4
EPS = 1e-6
SCALE = HD ** -0.5
WA = HA * HD
COL_QA, COL_KA, COL_VA, COL_QB, COL_KB, COL_VB = 0, WA, 2 * WA, 3 * WA, 4 * WA, 4 * WA + KVB * HD
NEG = -1e30
WIN = 512
NFAR = (LA - WIN) // 16
NKEYS = WIN + 4 * NFAR + NS
GQA, GKA, GQB, GKB, GATT, GFFN, GOUT = 0, 1, 2, 3, 4, 12, 20
NG = 28
A_STEPS = [(i, hh) for i in range(QT) for hh in range(2)]
NSTEP = len(A_STEPS)


def copies(dist):
    n = np.zeros(dist.shape)
    for w, d in ((128, 1), (512, 4), (2048, 16)):
        n += (dist >= 0) & (dist <= w) & (dist % d == 0)
    return n


def log_mask(n):
    return -np.where(n > 0, np.log(np.maximum(n, 1)) / SCALE, NEG).astype(np.float32)


def constants():
    c = {}
    c["c_ident"] = np.eye(P, dtype=np.float32)
    c["c_ones"] = np.ones((P, P), np.float32)
    c["c_blocks"] = np.kron(np.eye(2), np.ones((HD, HD))).astype(np.float32)
    pos = np.concatenate([np.arange(SEQ), np.tile(PAST + np.arange(TS), NB)]).astype(np.float32)
    inv = np.exp(np.float32(-math.log(500000.0)) * np.arange(0, ROT, 2).astype(np.float32) / np.float32(ROT)).astype(np.float32)
    ang = (inv[:, None] * pos[None, :]).astype(np.float32).astype(np.float64)
    cos, sin = np.ones((HD, T)), np.zeros((HD, T))
    h = ROT // 2
    cos[:h] = cos[h:ROT] = np.cos(ang)
    sin[:h], sin[h:ROT] = -np.sin(ang), np.sin(ang)
    c["c_cos"] = np.tile(cos, (2, 1)).astype(np.float32)
    c["c_sin"] = np.tile(sin, (2, 1)).astype(np.float32)
    q = np.arange(P)[:, None]
    c["c_mask_a"] = log_mask(copies(q + (QT - 1) * P - np.arange(SEQ)[None, :]))
    dist = q + P - np.arange(2 * P)[None, :]
    c["c_mask_b"] = log_mask((dist >= 0) & (dist < 128))
    t = (np.arange(NS) % TS)[:, None]
    near = (LA - WIN) + TS * np.arange(P)[None, :] + np.arange(4)[:, None]
    far = 16 * np.arange(NFAR)[None, :] + np.arange(4)[:, None]
    rows = np.concatenate([near.ravel(), far.ravel()])[None, :]
    c["c_mask_s"] = log_mask(copies(LA + t - rows))
    new_b = (np.arange(NS) // TS)[None, None, :]
    new_t = (np.arange(NS) % TS)[None, None, :]
    dn = t[:, :, None] - new_t
    same = new_b == np.arange(NB)[None, :, None]
    c["c_mask_sn"] = log_mask(copies(dn) * same).reshape(NS, NB * NS)
    c["c_mask_t"] = log_mask((LB + t - np.arange(LB)[None, :]) < 128)
    c["c_mask_tn"] = log_mask((dn >= 0) * same).reshape(NS, NB * NS)
    c["c_pick"] = ((np.arange(NS) // TS)[:, None] == np.arange(HB)[None, :]).astype(np.float32)
    return c


def trunk(nc, x_prompt, x_sample, cache_a, cache_b, attn_norm, w_in, q_norm_a, k_norm_a, q_norm_b,
          k_norm_b, sinks_b, out_norm_a, out_norm_b, w_out, ffn_norm, w_gate_up, w_down,
          c_ident, c_ones, c_blocks, c_cos, c_sin, c_mask_a, c_mask_b, c_mask_s, c_mask_sn,
          c_mask_t, c_mask_tn, c_pick,
          y_prompt, y_sample, new_a_p, new_b_p, new_a_s, new_b_s):
    x_spill = nc.dram_tensor("x_spill", (P, DC * T), F32).ap()
    with ExitStack() as ctx:
        ctx.enter_context(nc.allow_non_contiguous_dma(reason="small gains are laid on partitions"))

        def tensor(scope, name, shape, dt=F32):
            return scope.enter_context(nc.sbuf_tensor(name, shape, dt))

        def sem(name):
            return ctx.enter_context(nc.semaphore(name))

        class Signal:
            def __init__(self, name, per_layer, starts=0):
                self.sem, self.per_layer, self.starts = sem(name), per_layer, starts

            def at(self, layer, count):
                return layer * self.per_layer + count + self.starts

        ident = tensor(ctx, "ident", [P, P])
        ones = tensor(ctx, "ones", [P, P])
        blocks = tensor(ctx, "blocks", [P, P])
        cos = tensor(ctx, "cos", [P, T])
        sin = tensor(ctx, "sin", [P, T])
        mask_a = tensor(ctx, "mask_a", [P, SEQ])
        mask_b = tensor(ctx, "mask_b", [P, 2 * P])
        gains = tensor(ctx, "gains", [P, NG])
        sinks = tensor(ctx, "sinks", [P, HB])
        eps = tensor(ctx, "eps", [P, 1])
        roots = tensor(ctx, "roots", [P, 2, QT + 1])
        xm = tensor(ctx, "xm", [P, DC, T])

        mixer = ExitStack()
        q_rows_a = tensor(mixer, "q_rows_a", [P, NP, NB, HA, TS])
        q_rows_b = tensor(mixer, "q_rows_b", [P, NB, HB, TS])
        k_new_a = tensor(mixer, "k_new_a", [P, NP, NS])
        k_new_b = tensor(mixer, "k_new_b", [P, NS])
        kv_rows = tensor(mixer, "kv_rows", [NS, 2, NP + 1, P])

        pairs = ExitStack()
        h_hi = tensor(pairs, "h_hi", [P, DC, T], F32R)
        h_lo = tensor(pairs, "h_lo", [P, DC, T], F32R)
        w_raw = tensor(pairs, "w_raw", [P, DC, P])
        w_hi = tensor(pairs, "w_hi", [P, 2, DC, P], F32R)
        w_lo = tensor(pairs, "w_lo", [P, 2, DC, P], F32R)
        t_buf = [tensor(pairs, f"t_buf{i}", [P, T if i != 1 else (QT + 1) * P]) for i in range(3)]
        kt_a = tensor(pairs, "kt_a", [P, T])
        kt_b = tensor(pairs, "kt_b", [P, T])
        q_a = tensor(pairs, "q_a", [P, 2, SEQ])
        q_b = tensor(pairs, "q_b", [P, 2, SEQ])
        v_a = tensor(pairs, "v_a", [P, QT, P])
        v_b = tensor(pairs, "v_b", [P, QT, P])
        stage = tensor(pairs, "stage", [P, T])
        pt = tensor(pairs, "pt", [P, 3, 4 * P])
        head_means = tensor(pairs, "head_means", [P, 2, 2 * (QT + 1)])
        stats = tensor(pairs, "stats", [P, 5, 4])
        sink_now = tensor(pairs, "sink_now", [P, 2])
        sink_raw = tensor(pairs, "sink_raw", [P, 2])
        sq1, hf1 = [t_buf[0], t_buf[2]], [kt_a, kt_b]
        xy_tile = [q_a, q_b]
        pairs.close()

        samples = ExitStack()
        near = [tensor(samples, f"near{i}", [P, 4, 2 * WA]) for i in range(2)]
        far = [tensor(samples, f"far{i}", [NFAR, 4, 2 * WA]) for i in range(2)]
        last = [tensor(samples, f"last{i}", [P, 2, P]) for i in range(2)]
        kt_s = tensor(samples, "kt_s", [P, NP, WIN + 4 * NFAR])
        kt_t = tensor(samples, "kt_t", [P, P])
        q_now_a = tensor(samples, "q_now_a", [P, NP, NS])
        q_now_b = tensor(samples, "q_now_b", [P, NS])
        mask_s = tensor(samples, "mask_s", [NS, NKEYS])
        mask_t = tensor(samples, "mask_t", [NS, LB + NS])
        mask_sn = tensor(samples, "mask_sn", [NS, NB * NS])
        mask_tn = tensor(samples, "mask_tn", [NS, NB * NS])
        pick = tensor(samples, "pick", [NS, HB])
        p_s = tensor(samples, "p_s", [NS, NKEYS + LB + NS])
        pt_s = tensor(samples, "pt_s", [P, 11, NS])
        st_s = tensor(samples, "st_s", [NS, 16])
        samples.close()
        mixer.close()

        dense = ExitStack()
        g_hi = tensor(dense, "g_hi", [P, DC, T], F32R)
        g_lo = tensor(dense, "g_lo", [P, DC, T], F32R)
        f_raw = [tensor(dense, f"f_raw{i}", [P, 2 * D]) for i in range(2)]
        f_hi = [tensor(dense, f"f_hi{i}", [P, 2 * D], F32R) for i in range(3)]
        f_lo = [tensor(dense, f"f_lo{i}", [P, 2 * D], F32R) for i in range(3)]
        norms = ExitStack()
        sq2 = [tensor(norms, f"sq2_{i}", [P, T]) for i in range(2)]
        hf2 = [tensor(norms, f"hf2_{i}", [P, T]) for i in range(2)]
        norms.close()
        hidden = ExitStack()
        a_hi = tensor(hidden, "a_hi", [P, 2, T], F32R)
        a_lo = tensor(hidden, "a_lo", [P, 2, T], F32R)
        silu = tensor(hidden, "silu", [P, 2, W])
        hidden.close()
        dense.close()

        ps = ctx.enter_context(nc.psum_tensor("ps", [P, 8, 512], F32))

        consts_in = sem("consts_in")
        eps_set = sem("eps_set")
        x_tile_in = [sem(f"x_tile_in{i}") for i in range(2)]
        x_tile_turned = sem("x_tile_turned")
        x_tile_kept = sem("x_tile_kept")
        y_tile_turned = sem("y_tile_turned")
        y_tile_kept = sem("y_tile_kept")
        y_tile_out = [sem(f"y_tile_out{i}") for i in range(2)]
        met = sem("met")
        waits_alone = sem("waits_alone")

        N_GAINS = 14
        gains_in = Signal("gains_in", 16 * N_GAINS)
        spilled = Signal("spilled", 16)
        zeroed = Signal("zeroed", 6)
        sq_ready = Signal("sq_ready", 24)
        sq_summed = Signal("sq_summed", 24)
        root_ready = Signal("root_ready", 8)
        rs_ready = Signal("rs_ready", 8)
        rs_spread = Signal("rs_spread", 4)
        hf_ready = Signal("hf_ready", 24)
        hi_ready = Signal("hi_ready", 24)
        lo_ready = Signal("lo_ready", 24)

        UNITS = 2 + 4 * NP
        RAW = [16, 32]
        RAW_P = [16, 32, 48, 80]
        w_raw_in = Signal("w_raw_in", 32 + 80 * NP)
        w_hi_ready = Signal("w_hi_ready", UNITS)
        w_split = Signal("w_split", UNITS, starts=1)
        projected = Signal("projected", UNITS)
        K_ROPE, Q_ROPE = 11, 13
        ROPE_P = K_ROPE + 2 * Q_ROPE
        rope = Signal("rope", K_ROPE + ROPE_P * NP, starts=1)
        head_sq = Signal("head_sq", 1 + 3 * NP)
        head_summed = Signal("head_summed", 1 + 3 * NP)
        head_root = Signal("head_root", 2 * (1 + 3 * NP))
        head_spread = Signal("head_spread", 1 + 3 * NP)
        v_staged = Signal("v_staged", 1 + NP)
        v_turned = Signal("v_turned", 3 * (1 + NP))
        v_kept = Signal("v_kept", 3 * (1 + NP))
        k_turned = Signal("k_turned", 3 * (1 + NP))
        k_kept = Signal("k_kept", 3 * (1 + NP))
        v_out = Signal("v_out", 16 * (1 + NP))
        k_out = Signal("k_out", 16 * (1 + NP))
        sink_ready = Signal("sink_ready", 2 * NP)

        steps = [(m, i, hh) for m in "ab" for i in range(QT) for hh in range(2)]
        NST = len(steps)
        key_tiles = [list(range(i + 1)) if m == "a" else list(range(max(i - 1, 0), i + 1)) for m, i, hh in steps]
        groups = []
        for s, tiles in enumerate(key_tiles):
            groups += [(s, g, min(g + 4, len(tiles))) for g in range(0, len(tiles), 4)]
        NGR = len(groups)
        groups_of = [[g for g in range(NGR) if groups[g][0] == s] for s in range(NST)]
        exps_to = [sum(1 + (m == "b") for m, _, _ in steps[:s + 1]) for s in range(NST)]
        NEXP = exps_to[-1]
        scores = Signal("scores", NP * NST)
        masked = Signal("masked", NP * NST, starts=1)
        exped = Signal("exped", NP * NEXP)
        sum_ready = Signal("sum_ready", NP * NEXP)
        probs = Signal("probs", NP * NST)
        p_turned = Signal("p_turned", NP * NGR)
        pt_ready = Signal("pt_ready", NP * NGR, starts=1)
        mixed = Signal("mixed", NP * NST)
        mix_kept = Signal("mix_kept", NP * NST, starts=1)

        rows_out = Signal("rows_out", 16 * 4)
        cache_out = Signal("cache_out", 16 * 2 * NB)
        masks_in = Signal("masks_in", 16 * 5)
        sink_s = Signal("sink_s", 3)
        kv_in = [Signal(f"kv_in{i}", 16 * 3 * NB // 2) for i in range(2)]
        s_turned = Signal("s_turned", 9 * NB)
        near_kept = Signal("near_kept", 5 * NB)
        far_kept = Signal("far_kept", 4 * NB)
        s_query = Signal("s_query", 4 * NB)
        s_scores = Signal("s_scores", NB, starts=1)
        s_soft = Signal("s_soft", 8 * NB, starts=1)
        s_exped = Signal("s_exped", 3 * NB)
        s_pturned = Signal("s_pturned", NB)
        s_pkept = Signal("s_pkept", 5 * NB)
        s_mixed = Signal("s_mixed", NB)
        s_mix_kept = Signal("s_mix_kept", 4 * NB, starts=1)

        x_back = Signal("x_back", 16)
        o_raw_in = Signal("o_raw_in", 16 * 3 * DC)
        o_hi_ready = Signal("o_hi_ready", DC)
        o_split = Signal("o_split", DC, starts=1)
        o_done = [Signal(f"o_done{i}", DC // 2, starts=1) for i in range(2)]
        o_added = [Signal(f"o_added{i}", DC // 2, starts=1) for i in range(2)]

        f_raw_in = [Signal(f"f_raw_in{j}", 16 * FI) for j in range(3)]
        f_hi_ready = Signal("f_hi_ready", 3 * FI)
        f_split = Signal("f_split", 3 * FI, starts=1)
        HID = 2 * NW
        DOWN = NW * DC
        hid = Signal("hid", HID * FI, starts=1)
        silued = Signal("silued", HID * FI)
        gated = Signal("gated", HID * FI, starts=1)
        act_hi = Signal("act_hi", HID * FI)
        act_lo = Signal("act_lo", HID * FI, starts=1)
        downed = Signal("downed", DOWN * FI, starts=1)
        ffn_added = Signal("ffn_added", DOWN * FI, starts=1)

        MEETS = 5

        def meet(eng, layer, k):
            eng.drain().then_inc(met, 1)
            eng.wait_ge(met, layer * 5 * MEETS + 5 * (k + 1))
            eng.sem_inc(waits_alone, 1)

        def pieces(ap):
            return ap.rearrange("p (n w) -> p n w", n=NW)

        def banks(b):
            return ps[:, b:b + NW, 0:W]

        def flat(b):
            return ps[:, b:b + NW, :].rearrange("p b c -> p (b c)")[:, 0:T]

        def rows_of(t):
            return P if t < QT else NS

        NORMS = [(0, DC, 0, D), (0, NP, 8, WA), (NP, NP, 12, WA), (0, DC, 16, D)]

        def product(pe, out, left, right, n):
            mm = None
            for c in range(n):
                for k, (a, b) in enumerate(((0, 0), (1, 0), (0, 1))):
                    mm = pe.matmul(out, left(a, c), right(b, c), start=(c == 0 and k == 0),
                                   stop=(c == n - 1 and k == 2))
            return mm

        block = ctx.enter_context(nc.Block())

        @block.sync
        def _(sp):
            for signal in (w_split, rope, o_split, f_split, masked, pt_ready, mix_kept, hid, gated, downed,
                           ffn_added, act_lo, s_scores, s_soft, s_mix_kept, *o_done, *o_added):
                sp.sem_inc(signal.sem, 1)
            for dst, src in ((ident, c_ident), (ones, c_ones), (blocks, c_blocks), (cos, c_cos),
                             (sin, c_sin), (mask_a, c_mask_a), (mask_b, c_mask_b)):
                sp.dma_start(dst[:], src).then_inc(consts_in, 16)
            for t in range(QT + 1):
                if t >= 2:
                    sp.wait_ge(x_tile_turned, 2 * (t - 1))
                src = x_prompt[0, t * P:(t + 1) * P, :] if t < QT else x_sample.rearrange("b t d -> (b t) d")
                sp.dma_start(xy_tile[t % 2][0:rows_of(t), 0, :], src).then_inc(x_tile_in[t % 2], 16)
            sp.wait_ge(x_tile_kept, 2 * (QT + 1))
            with sp.Fori(0, DEPTH) as l:
                def layer(ap):
                    return ap[ds(l, 1)]

                for hh in range(2):
                    half = slice(hh * HD, (hh + 1) * HD)
                    for g, src in ((GQA, q_norm_a), (GKA, k_norm_a), (GQB, q_norm_b), (GKB, k_norm_b)):
                        sp.dma_start(gains[half, g:g + 1], layer(src).rearrange("l p -> p l")
                                     ).then_inc(gains_in.sem, 16)
                    sp.dma_start(gains[half, GOUT + NP:GOUT + 2 * NP],
                                 layer(out_norm_b)[:, hh * NP * HD:(hh + 1) * NP * HD].rearrange(
                                     "l (c p) -> p (l c)", p=HD)).then_inc(gains_in.sem, 16)
                for g, src, n in ((GATT, attn_norm, DC), (GFFN, ffn_norm, DC), (GOUT, out_norm_a, NP)):
                    sp.dma_start(gains[:, g:g + n], layer(src).rearrange("l (c p) -> p (l c)", p=P)
                                 ).then_inc(gains_in.sem, 16)
                sp.dma_start(sinks[:], layer(sinks_b).broadcast_to((P, HB))).then_inc(gains_in.sem, 16)
                sp.dma_start(x_spill, xm[:].rearrange("p c t -> p (c t)")).then_inc(spilled.sem, 16)
                sp.wait_ge(gains_in.sem, gains_in.at(l, 16 * N_GAINS))
                sp.sem_inc(waits_alone, 1)
                sp.wait_ge(spilled.sem, spilled.at(l, 16))
                sp.sem_inc(waits_alone, 1)
                meet(sp, l, 0)

                def w_load(u, col):
                    sp.wait_ge(w_split.sem, w_split.at(l, u))
                    sp.sem_inc(waits_alone, 1)
                    sp.dma_start(w_raw[:], layer(w_in)[:, :, ds(col, P)].rearrange(
                        "l (c p) n -> p (l c) n", p=P)).then_inc(w_raw_in.sem, 16)

                w_load(0, COL_KB)
                w_load(1, COL_VB)
                sp.wait_ge(v_kept.sem, v_kept.at(l, 3))
                sp.sem_inc(waits_alone, 1)
                sp.dma_start(layer(new_b_p)[:, 0, :, 1].rearrange("l t h d -> (l t) (h d)"),
                             v_b[:, QT - 1, :]).then_inc(v_out.sem, 16)
                sp.wait_ge(k_kept.sem, k_kept.at(l, 3))
                sp.sem_inc(waits_alone, 1)
                sp.dma_start(layer(new_b_p)[:, 0, :, 0].rearrange("l t h d -> (l t) (h d)"),
                             stage[:, (QT - 1) * P:QT * P]).then_inc(k_out.sem, 16)
                with sp.Fori(0, NP) as p:
                    w_load(2 + 4 * p, COL_KA + p * P)
                    w_load(3 + 4 * p, COL_VA + p * P)
                    w_load(4 + 4 * p, COL_QA + p * P)
                    sp.wait_ge(w_split.sem, w_split.at(l, 5 + 4 * p))
                    sp.sem_inc(waits_alone, 1)
                    for hh in range(2):
                        sp.dma_start(w_raw[:, :, hh * HD:(hh + 1) * HD],
                                     layer(w_in)[:, :, ds(COL_QB + 4 * hh * HD + p * HD, HD)].rearrange(
                                         "l (c p) n -> p (l c) n", p=P)).then_inc(w_raw_in.sem, 16)
                    for kv, kept, out, rows in ((1, v_kept, v_out, v_a[:]),
                                                (0, k_kept, k_out, stage[:, 0:SEQ].rearrange("p (j n) -> p j n", j=QT))):
                        sp.wait_ge(kept.sem, kept.at(l, 6 + 3 * p))
                        sp.sem_inc(waits_alone, 1)
                        sp.dma_start(layer(new_a_p)[:, 0, :, kv].rearrange(
                            "l (j q) h d -> q (l j) (h d)", q=P)[:, :, ds(p * P, P)], rows).then_inc(out.sem, 16)
                sp.wait_ge(v_out.sem, v_out.at(l, 16 * (1 + NP)))
                sp.sem_inc(waits_alone, 1)
                sp.wait_ge(k_out.sem, k_out.at(l, 16 * (1 + NP)))
                sp.sem_inc(waits_alone, 1)
                meet(sp, l, 1)

                for kv in range(2):
                    sp.dma_start(layer(new_a_s)[:, :, LA - TS:LA, kv].rearrange("l b t h d -> (l b) t (h d)"),
                                 kv_rows[:, kv, 0:NP, :].rearrange("q c n -> q (c n)")).then_inc(rows_out.sem, 16)
                    sp.dma_start(layer(new_b_s)[:, :, LB - TS:LB, kv].rearrange("l b t h d -> (l b) t (h d)"),
                                 kv_rows[:, kv, NP, :]).then_inc(rows_out.sem, 16)
                for dst, src in ((mask_s[:, 0:WIN + 4 * NFAR], c_mask_s), (mask_t[:, 0:LB], c_mask_t),
                                 (mask_sn[:], c_mask_sn), (mask_tn[:], c_mask_tn), (pick[:], c_pick)):
                    sp.dma_start(dst, src).then_inc(masks_in.sem, 16)

                def kv_load(i, b):
                    rows = layer(cache_a)[:, ds(b, 1)]
                    sp.dma_start(near[i][:], rows[:, :, LA - WIN:LA].rearrange(
                        "l b (k r) z h d -> (l b k) r (z h d)", r=4)).then_inc(kv_in[i].sem, 16)
                    sp.dma_start(far[i][:], rows[:, :, 0:LA - WIN].rearrange(
                        "l b (k r) z h d -> (l b k) r (z h d)", r=16)[:, 0:4, :]).then_inc(kv_in[i].sem, 16)
                    sp.dma_start(last[i][:], layer(cache_b)[:, ds(b, 1)].rearrange(
                        "l b k z h d -> (l b k) z (h d)")).then_inc(kv_in[i].sem, 16)

                kv_load(0, 0)
                kv_load(1, 1)
                with sp.Fori(0, NB // 2 - 1) as bb:
                    for i in range(2):
                        sp.wait_ge(s_mixed.sem, s_mixed.at(l, 2 * bb + i + 1))
                        sp.sem_inc(waits_alone, 1)
                        kv_load(i, 2 * bb + 2 + i)
                sp.wait_ge(rows_out.sem, rows_out.at(l, 64))
                sp.sem_inc(waits_alone, 1)
                meet(sp, l, 2)

                sp.wait_ge(hf_ready.sem, hf_ready.at(l, 16))
                sp.sem_inc(waits_alone, 1)
                sp.dma_start(xm[:].rearrange("p c t -> p (c t)"), x_spill).then_inc(x_back.sem, 16)
                raw = f_raw[0][:, 0:D].rearrange("p (c n) -> p c n", c=DC)
                with sp.Fori(0, DC) as u:
                    sp.wait_ge(o_split.sem, o_split.at(l, u))
                    sp.sem_inc(waits_alone, 1)
                    wo = layer(w_out)[:, :, ds(u * P, P)]
                    sp.dma_start(raw[:, 0:NP, :], wo[:, 0:WA].rearrange(
                        "l (c p) n -> p (l c) n", p=P)).then_inc(o_raw_in.sem, 16)
                    for hh in range(2):
                        sp.dma_start(raw[hh * HD:(hh + 1) * HD, NP:DC, :],
                                     wo[:, WA + NP * hh * HD:WA + NP * (hh + 1) * HD].rearrange(
                                         "l (c p) n -> p (l c) n", p=HD)).then_inc(o_raw_in.sem, 16)
                sp.wait_ge(x_back.sem, x_back.at(l, 16))
                sp.sem_inc(waits_alone, 1)
                meet(sp, l, 3)

                with sp.Fori(0, FI) as f:
                    for j in range(3):
                        before = 3 * f + j if j == 0 else 3 * f + j - 1
                        sp.wait_ge(f_split.sem, f_split.at(l, before))
                        sp.sem_inc(waits_alone, 1)
                        if j < 2:
                            sp.dma_start(f_raw[j % 2][:].rearrange("p (c n) -> p c n", c=DC),
                                         layer(w_gate_up)[:, :, ds(j * FF + f * 2 * P, 2 * P)].rearrange(
                                             "l (c p) n -> p (l c) n", p=P)).then_inc(f_raw_in[j].sem, 16)
                        else:
                            sp.dma_start(f_raw[0][:].rearrange("p (a n) -> p a n", a=2),
                                         layer(w_down)[:, ds(f * 2 * P, 2 * P), :].rearrange(
                                             "l (a p) n -> p (l a) n", p=P)).then_inc(f_raw_in[j].sem, 16)
                meet(sp, l, 4)
            for t in range(QT + 1):
                sp.wait_ge(y_tile_kept, 2 * (t + 1))
                dst = y_prompt[0, t * P:(t + 1) * P, :] if t < QT else y_sample.rearrange("b t d -> (b t) d")
                sp.dma_start(dst, xy_tile[t % 2][0:rows_of(t), 0, :]).then_inc(y_tile_out[t % 2], 16)
            sp.wait_ge(y_tile_out[0], 16 * 5)
            sp.wait_ge(y_tile_out[1], 16 * 4)

        @block.gpsimd
        def _(pool):
            nc.gpsimd.memset(eps[:], EPS).then_inc(eps_set, 1)

            def split(l, k, raw_in, raw_count, hi_ready_, split_, raw, hi, lo):
                pool.wait_ge(raw_in.sem, raw_in.at(l, raw_count))
                pool.sem_inc(waits_alone, 1)
                nc.gpsimd.tensor_copy(hi, raw).then_inc(hi_ready_.sem, 1)
                pool.wait_ge(hi_ready_.sem, hi_ready_.at(l, k + 1))
                pool.sem_inc(waits_alone, 1)
                nc.gpsimd.tensor_tensor(lo, raw, hi.bitcast(F32), ALU.subtract).then_inc(split_.sem, 1)

            with pool.Fori(0, DEPTH) as l:
                meet(pool, l, 0)
                for n, z in enumerate((q_a[HD:P, 0], q_a[0:HD, 1], q_b[HD:P, 0], q_b[0:HD, 1], q_rows_a[:], q_rows_b[:])):
                    nc.gpsimd.memset(z, 0.0).then_inc(zeroed.sem, 1)
                    pool.wait_ge(zeroed.sem, zeroed.at(l, n + 1))
                    pool.sem_inc(waits_alone, 1)

                def split_w(k, raw_count, slot):
                    split(l, k, w_raw_in, raw_count, w_hi_ready, w_split, w_raw[:], w_hi[:, slot], w_lo[:, slot])

                for u in range(2):
                    split_w(u, RAW[u], u)
                with pool.Fori(0, NP) as p:
                    for b in range(2):
                        pool.dma_start(new_a_s[ds(l, 1), ds(2 * p + b, 1), 0:LA - TS].rearrange("l b t z h d -> (l b) (t z h d)"),
                                       cache_a[ds(l, 1), ds(2 * p + b, 1), TS:LA].rearrange("l b t z h d -> (l b) (t z h d)")
                                       ).then_inc(cache_out.sem, 16)
                        pool.dma_start(new_b_s[ds(l, 1), ds(2 * p + b, 1), 0:LB - TS].rearrange("l b t z h d -> (l b) (t z h d)"),
                                       cache_b[ds(l, 1), ds(2 * p + b, 1), TS:LB].rearrange("l b t z h d -> (l b) (t z h d)")
                                       ).then_inc(cache_out.sem, 16)
                    for j in range(4):
                        pool.wait_ge(projected.sem, projected.at(l, 1 + 4 * p + j))
                        pool.sem_inc(waits_alone, 1)
                        split_w(2 + 4 * p + j, 32 + 80 * p + RAW_P[j], j % 2)
                meet(pool, l, 1)
                meet(pool, l, 2)
                with pool.Fori(0, DC // 2) as dd:
                    for i in range(2):
                        pool.wait_ge(o_done[i].sem, o_done[i].at(l, dd))
                        pool.sem_inc(waits_alone, 1)
                        u = 2 * dd + i
                        split(l, u, o_raw_in, 48 * (u + 1), o_hi_ready, o_split,
                              f_raw[0][:, 0:D], f_hi[i][:, 0:D], f_lo[i][:, 0:D])
                meet(pool, l, 3)
                with pool.Fori(0, FI) as f:
                    for j in range(3):
                        if j < 2:
                            pool.wait_ge(hid.sem, hid.at(l, HID * f))
                            pool.sem_inc(waits_alone, 1)
                        else:
                            pool.wait_ge(downed.sem, downed.at(l, DOWN * f))
                            pool.sem_inc(waits_alone, 1)
                        u = 3 * f + j
                        split(l, u, f_raw_in[j], 16 * (f + 1), f_hi_ready, f_split, f_raw[j % 2][:], f_hi[j][:], f_lo[j][:])
                pool.wait_ge(cache_out.sem, cache_out.at(l, 16 * 2 * NB))
                pool.sem_inc(waits_alone, 1)
                meet(pool, l, 4)

        @block.scalar
        def _(act):
            act.wait_ge(eps_set, 1)

            def norm_squares(l, k, sq):
                first, n, before, width = NORMS[k]
                for c in range(n):
                    if c >= 2:
                        act.wait_ge(sq_summed.sem, sq_summed.at(l, before + c - 1))
                    nc.scalar.activation(sq[c % 2][:], xm[:, first + c, :], ACT.Square).then_inc(sq_ready.sem, 1)

            def norm_roots(l, k):
                first, n, before, width = NORMS[k]
                act.wait_ge(sq_summed.sem, sq_summed.at(l, before + n))
                for rows, a, b in ((P, 0, QT), (NS, QT, QT + 1)):
                    nc.scalar.activation(roots[0:rows, k % 2, a:b], ps[0:rows, 6 + k % 2, a:b], ACT.Sqrt,
                                         scale=1.0 / width, bias=eps[0:rows, 0:1]).then_inc(root_ready.sem, 1)

            def norm_hi(l, k, hf, hi):
                first, n, before, width = NORMS[k]
                for c in range(n):
                    act.wait_ge(hf_ready.sem, hf_ready.at(l, before + c + 1))
                    nc.scalar.activation(hi[:, first + c, :], hf[c % 2][:], ACT.Copy).then_inc(hi_ready.sem, 1)

            with act.Fori(0, DEPTH) as l:
                meet(act, l, 0)
                norm_squares(l, 0, sq1)
                norm_roots(l, 0)
                norm_hi(l, 0, hf1, h_hi)

                def head_squares(unit, bank, n):
                    act.wait_ge(projected.sem, projected.at(l, unit + 1))
                    act.wait_ge(head_spread.sem, head_spread.at(l, n))
                    nc.scalar.activation(pieces(t_buf[1][:, 0:T]), banks(bank), ACT.Square).then_inc(head_sq.sem, 1)

                def roots_of_heads(n, r):
                    act.wait_ge(rope.sem, rope.at(l, r + 7))
                    for rows, a, b in ((P, 0, QT), (NS, QT, QT + 1)):
                        nc.scalar.activation(
                            t_buf[1][0:rows, a * P:b * P].rearrange("p (t d) -> p t d", d=HD),
                            head_means[0:rows, 1, 2 * a:2 * b].rearrange("p (t o) -> p t o", o=1).broadcast_to(
                                (rows, 2 * (b - a), HD)), ACT.Sqrt).then_inc(head_root.sem, 1)

                def stage_v(unit, n):
                    act.wait_ge(projected.sem, projected.at(l, unit + 1))
                    act.wait_ge(k_out.sem, k_out.at(l, 16 * n))
                    nc.scalar.activation(pieces(stage[:]), banks(3), ACT.Copy).then_inc(v_staged.sem, 1)

                def keep_k(n, rows):
                    for g in range(2):
                        act.wait_ge(k_turned.sem, k_turned.at(l, 3 * n + g + 1))
                        nc.scalar.activation(stage[:, g * 4 * P:(g + 1) * 4 * P], ps[:, 6 + g, :], ACT.Copy
                                             ).then_inc(k_kept.sem, 1)
                    act.wait_ge(k_turned.sem, k_turned.at(l, 3 * n + 3))
                    nc.scalar.activation(rows, ps[0:NS, 2, 384:512], ACT.Copy).then_inc(k_kept.sem, 1)

                act.wait_ge(projected.sem, projected.at(l, 1))
                act.wait_ge(lo_ready.sem, lo_ready.at(l, 8))
                nc.scalar.activation(pieces(t_buf[1][:, 0:T]), banks(0), ACT.Square).then_inc(head_sq.sem, 1)
                act.wait_ge(projected.sem, projected.at(l, 2))
                nc.scalar.activation(pieces(stage[:]), banks(3), ACT.Copy).then_inc(v_staged.sem, 1)
                roots_of_heads(0, 0)
                keep_k(0, kv_rows[:, 0, NP, :])
                with act.Fori(0, NP) as p:
                    u, r, h = 2 + 4 * p, K_ROPE + ROPE_P * p, 1 + 3 * p
                    head_squares(u, 0, h)
                    stage_v(u + 1, p + 1)
                    roots_of_heads(h, r)
                    head_squares(u + 2, 3, h + 1)
                    keep_k(p + 1, kv_rows[:, 0, ds(p, 1), :].rearrange("q c n -> q (c n)"))
                    roots_of_heads(h + 1, r + K_ROPE)
                    head_squares(u + 3, 0, h + 2)
                    roots_of_heads(h + 2, r + K_ROPE + Q_ROPE)

                    def softmax(s):
                        m, i, hh = steps[s]
                        n = P * len(key_tiles[s])
                        act.wait_ge(masked.sem, masked.at(l, p * NST + s + 1))
                        nc.scalar.activation(t_buf[s % 3][:, 0:n], t_buf[s % 3][:, 0:n], ACT.Exp, scale=-1.0,
                                             bias=stats[:, 0, s % 4:s % 4 + 1],
                                             accum_out=stats[:, 2, s % 4:s % 4 + 1]).then_inc(exped.sem, 1)
                        if m == "b":
                            nc.scalar.activation(stats[:, 4, s % 4:s % 4 + 1], sink_now[:, hh:hh + 1], ACT.Exp,
                                                 bias=stats[:, 0, s % 4:s % 4 + 1]).then_inc(exped.sem, 1)

                    softmax(0)
                    softmax(1)
                    for s in range(NST):
                        if s + 2 < NST:
                            softmax(s + 2)
                        for g in groups_of[s]:
                            _, a, b = groups[g]
                            if g >= 3:
                                act.wait_ge(mixed.sem, mixed.at(l, p * NST + groups[g - 3][0] + 1))
                            act.wait_ge(p_turned.sem, p_turned.at(l, p * NGR + g + 1))
                            nc.scalar.activation(pt[:, g % 3, 0:(b - a) * P], ps[:, 4 + g % 2, 0:(b - a) * P],
                                                 ACT.Copy).then_inc(pt_ready.sem, 1)
                meet(act, l, 1)

                with act.Fori(0, NB) as b:
                    act.wait_ge(s_scores.sem, s_scores.at(l, b))
                    for pr in range(NP):
                        act.wait_ge(s_turned.sem, s_turned.at(l, 9 * b + 2 * pr + 1))
                        nc.scalar.activation(kt_s[:, pr, 0:WIN], ps[:, 2 * (pr % 2), :], ACT.Copy
                                             ).then_inc(near_kept.sem, 1)
                    act.wait_ge(s_turned.sem, s_turned.at(l, 9 * b + 9))
                    nc.scalar.activation(kt_t[:], ps[:, 7, 256:384], ACT.Copy).then_inc(near_kept.sem, 1)
                    act.wait_ge(s_soft.sem, s_soft.at(l, 8 * b + 3))
                    nc.scalar.activation(p_s[:, 0:NKEYS], p_s[:, 0:NKEYS], ACT.Exp, scale=-1.0,
                                         bias=st_s[:, 1:2], accum_out=st_s[:, 5:6]).then_inc(s_exped.sem, 1)
                    nc.scalar.activation(p_s[:, NKEYS:], p_s[:, NKEYS:], ACT.Exp, scale=-1.0,
                                         bias=st_s[:, 2:3], accum_out=st_s[:, 6:7]).then_inc(s_exped.sem, 1)
                    nc.scalar.activation(st_s[:, 7:8], st_s[:, 10:11], ACT.Exp, bias=st_s[:, 2:3]
                                         ).then_inc(s_exped.sem, 1)
                meet(act, l, 2)

                norm_squares(l, 1, sq2)
                norm_roots(l, 1)
                for c in range(NP):
                    if c >= 1:
                        act.wait_ge(sq_summed.sem, sq_summed.at(l, 12 + c - 1))
                    else:
                        act.wait_ge(sq_summed.sem, sq_summed.at(l, 12))
                    nc.scalar.activation(sq2[c % 2][:], xm[:, NP + c, :], ACT.Square).then_inc(sq_ready.sem, 1)
                norm_roots(l, 2)
                norm_hi(l, 1, hf2, g_hi)
                norm_hi(l, 2, hf2, g_hi)
                for i in range(2):
                    act.wait_ge(o_added[i].sem, o_added[i].at(l, DC // 2))
                norm_squares(l, 3, sq2)
                norm_roots(l, 3)
                norm_hi(l, 3, hf2, g_hi)
                meet(act, l, 3)

                with act.Fori(0, FI) as f:
                    for k in range(HID):
                        a, n = divmod(k, NW)
                        act.wait_ge(hid.sem, hid.at(l, HID * f + k + 1))
                        act.wait_ge(act_lo.sem, act_lo.at(l, HID * f + max(k - 1, 0)))
                        nc.scalar.activation(silu[:, k % 2, :], ps[:, 2 * (k % 2), 0:W], ACT.Silu
                                             ).then_inc(silued.sem, 1)
                        act.wait_ge(gated.sem, gated.at(l, HID * f + k + 1))
                        act.wait_ge(downed.sem, downed.at(l, DOWN * f))
                        nc.scalar.activation(a_hi[:, a, n * W:(n + 1) * W], silu[:, k % 2, :], ACT.Copy
                                             ).then_inc(act_hi.sem, 1)
                meet(act, l, 4)

        @block.vector
        def _(dve):
            swap = [(i + ROT // 2) % ROT if i < ROT else i for i in range(32)]

            for t in range(QT + 1):
                for g in range(2):
                    dve.wait_ge(x_tile_turned, 2 * t + g + 1)
                    w = rows_of(t)
                    nc.vector.tensor_copy(xm[:, 4 * g:4 * g + 4, t * P:t * P + w],
                                          ps[:, (2 * t + g) % 8, :].rearrange("p (c n) -> p c n", c=4)[:, :, 0:w]
                                          ).then_inc(x_tile_kept, 1)

            def norm_reciprocals(l, k):
                dve.wait_ge(root_ready.sem, root_ready.at(l, 2 * k + 2))
                for rows, a, b in ((P, 0, QT), (NS, QT, QT + 1)):
                    nc.vector.reciprocal(roots[0:rows, k % 2, a:b], roots[0:rows, k % 2, a:b]).then_inc(rs_ready.sem, 1)

            def norm_chunks(l, k, gain, hf, bank, hi, lo):
                first, n, before, width = NORMS[k]
                dve.wait_ge(rs_spread.sem, rs_spread.at(l, k + 1))
                for c in range(n + 1):
                    if c < n:
                        if before + c >= 2:
                            dve.wait_ge(lo_ready.sem, lo_ready.at(l, before + c - 1))
                        nc.vector.scalar_tensor_tensor(hf[c % 2][:], xm[:, first + c, :],
                                                       gains[:, gain + first + c:gain + first + c + 1], flat(bank),
                                                       ALU.mult, ALU.mult).then_inc(hf_ready.sem, 1)
                    if c >= 1:
                        dve.wait_ge(hi_ready.sem, hi_ready.at(l, before + c))
                        nc.vector.tensor_tensor(lo[:, first + c - 1, :], hf[(c - 1) % 2][:],
                                                hi[:, first + c - 1, :].bitcast(F32), ALU.subtract
                                                ).then_inc(lo_ready.sem, 1)

            with dve.Fori(0, DEPTH) as l:
                meet(dve, l, 0)
                norm_reciprocals(l, 0)
                norm_chunks(l, 0, GATT, hf1, 0, h_hi, h_lo)

                def roped(unit, bank, gain, r, root):
                    dve.wait_ge(projected.sem, projected.at(l, unit + 1))
                    dve.wait_ge(rope.sem, rope.at(l, r))
                    dve.wait_ge(head_sq.sem, head_sq.at(l, root + 1))
                    nc.vector.tensor_scalar(pieces(t_buf[0][:]), banks(bank), gains[:, gain:gain + 1], None,
                                            ALU.mult).then_inc(rope.sem, 1)
                    dve.wait_ge(rope.sem, rope.at(l, r + 1))
                    dve.sem_inc(waits_alone, 1)
                    nc.vector.stream_shuffle(t_buf[2][:], t_buf[0][:], swap).then_inc(rope.sem, 1)
                    dve.wait_ge(rope.sem, rope.at(l, r + 2))
                    nc.vector.tensor_tensor(t_buf[0][:], t_buf[0][:], cos[:], ALU.mult).then_inc(rope.sem, 1)
                    dve.wait_ge(head_summed.sem, head_summed.at(l, root + 1))
                    for rows, a, b in ((P, 0, 2 * QT), (NS, 2 * QT, 2 * QT + 2)):
                        nc.vector.tensor_scalar(head_means[0:rows, 0, a:b], ps[0:rows, bank, a:b], 1.0 / HD, EPS,
                                                ALU.mult, ALU.add).then_inc(rope.sem, 1)
                    dve.wait_ge(rope.sem, rope.at(l, r + 5))
                    for rows, a, b in ((P, 0, 2 * QT), (NS, 2 * QT, 2 * QT + 2)):
                        nc.vector.reciprocal(head_means[0:rows, 1, a:b], head_means[0:rows, 0, a:b]).then_inc(rope.sem, 1)
                    nc.vector.tensor_tensor(t_buf[2][:], t_buf[2][:], sin[:], ALU.mult).then_inc(rope.sem, 1)
                    dve.wait_ge(rope.sem, rope.at(l, r + 8))
                    nc.vector.tensor_tensor(t_buf[0][:], t_buf[0][:], t_buf[2][:], ALU.add).then_inc(rope.sem, 1)
                    dve.wait_ge(head_spread.sem, head_spread.at(l, root + 1))
                    dve.wait_ge(rope.sem, rope.at(l, r + 9))

                def k_rope(unit, gain, r, root, kt, new):
                    roped(unit, 0, gain, r, root)
                    nc.vector.tensor_tensor(kt[:], t_buf[0][:], flat(0), ALU.mult).then_inc(rope.sem, 1)
                    dve.wait_ge(rope.sem, rope.at(l, r + 10))
                    nc.vector.tensor_copy(new, kt[:, SEQ:T]).then_inc(rope.sem, 1)

                def q_rope(unit, bank, gain, r, root, q, rows):
                    roped(unit, bank, gain, r, root)
                    for hh in range(2):
                        half = slice(hh * HD, (hh + 1) * HD)
                        nc.vector.scalar_tensor_tensor(q[half, hh, :], t_buf[0][half, 0:SEQ], -1.0,
                                                       flat(bank)[half, 0:SEQ], ALU.mult, ALU.mult).then_inc(rope.sem, 1)
                    for hh in range(2):
                        half = slice(hh * HD, (hh + 1) * HD)
                        nc.vector.scalar_tensor_tensor(rows(half, hh),
                                                       t_buf[0][half, SEQ:T].rearrange("p (b t) -> p b t", t=TS), -1.0,
                                                       flat(bank)[half, SEQ:T].rearrange("p (b t) -> p b t", t=TS),
                                                       ALU.mult, ALU.mult).then_inc(rope.sem, 1)

                def keep_v(n, v, rows):
                    dve.wait_ge(v_out.sem, v_out.at(l, 16 * n))
                    for g in range(2):
                        dve.wait_ge(v_turned.sem, v_turned.at(l, 3 * n + g + 1))
                        nc.vector.tensor_copy(v[:, 4 * g:4 * g + 4, :],
                                              ps[:, 6 + g, :].rearrange("p (j n) -> p j n", j=4)).then_inc(v_kept.sem, 1)
                    dve.wait_ge(v_turned.sem, v_turned.at(l, 3 * n + 3))
                    nc.vector.tensor_copy(rows, ps[0:NS, 5, 384:512]).then_inc(v_kept.sem, 1)

                dve.wait_ge(zeroed.sem, zeroed.at(l, 6))
                dve.wait_ge(lo_ready.sem, lo_ready.at(l, 8))
                k_rope(0, GKB, 0, 0, kt_b, k_new_b[:])
                keep_v(0, v_b, kv_rows[:, 1, NP, :])
                with dve.Fori(0, NP) as p:
                    u, r, h = 2 + 4 * p, K_ROPE + ROPE_P * p, 1 + 3 * p
                    k_rope(u, GKA, r, h, kt_a, k_new_a[:, ds(p, 1), :].rearrange("q c n -> q (c n)"))
                    keep_v(p + 1, v_a, kv_rows[:, 1, ds(p, 1), :].rearrange("q c n -> q (c n)"))
                    q_rope(u + 2, 3, GQA, r + K_ROPE, h + 1, q_a,
                           lambda half, hh: q_rows_a[half, ds(p, 1), :, ds(2 * p + hh, 1), :].rearrange(
                               "q c b h t -> q (c b) (h t)"))
                    q_rope(u + 3, 0, GQB, r + K_ROPE + Q_ROPE, h + 2, q_b,
                           lambda half, hh: q_rows_b[half, :, ds(p + NP * hh, 1), :].rearrange("q b h t -> q b (h t)"))
                    nc.vector.tensor_copy(sink_now[:].rearrange("p (a b) -> p a b", b=1),
                                          sinks[:].rearrange("p (a b) -> p a b", a=2)[:, :, ds(p, 1)]
                                          ).then_inc(sink_ready.sem, 1)
                    dve.wait_ge(sink_ready.sem, sink_ready.at(l, 2 * p + 1))
                    nc.vector.tensor_scalar(sink_raw[:], sink_now[:], -1.0, None, ALU.mult
                                            ).then_inc(sink_ready.sem, 1)
                    dve.wait_ge(sink_ready.sem, sink_ready.at(l, 2 * p + 2))
                    dve.wait_ge(rope.sem, rope.at(l, r + ROPE_P))

                    def mask_and_max(s):
                        m, i, hh = steps[s]
                        n = P * len(key_tiles[s])
                        mask = mask_a[:, SEQ - n:] if m == "a" else mask_b[:, 2 * P - n:]
                        if s >= 3:
                            dve.wait_ge(p_turned.sem, p_turned.at(l, p * NGR + groups_of[s - 3][-1] + 1))
                        dve.wait_ge(scores.sem, scores.at(l, p * NST + s + 1))
                        dve.sem_inc(waits_alone, 1)
                        nc.vector.tensor_tensor_reduce(
                            t_buf[s % 3][:, 0:n],
                            ps[:, 2 * (s % 2):2 * (s % 2) + 2, :].rearrange("p b c -> p (b c)")[:, 0:n], mask,
                            SCALE, 3e38 if m == "a" else sink_raw[:, hh:hh + 1], ALU.add, ALU.min,
                            stats[:, 0, s % 4:s % 4 + 1]).then_inc(masked.sem, 1)

                    def normalize(s):
                        m, i, hh = steps[s]
                        n = P * len(key_tiles[s])
                        c = slice(s % 4, s % 4 + 1)
                        dve.wait_ge(exped.sem, exped.at(l, p * NEXP + exps_to[s]))
                        if m == "b":
                            nc.vector.tensor_tensor(stats[:, 2, c], stats[:, 2, c], stats[:, 4, c], ALU.add
                                                    ).then_inc(sum_ready.sem, 1)
                            dve.wait_ge(sum_ready.sem, sum_ready.at(l, p * NEXP + exps_to[s] - 1))
                        nc.vector.reciprocal(stats[:, 3, c], stats[:, 2, c]).then_inc(sum_ready.sem, 1)
                        dve.wait_ge(sum_ready.sem, sum_ready.at(l, p * NEXP + exps_to[s]))
                        nc.vector.tensor_scalar(t_buf[s % 3][:, 0:n], t_buf[s % 3][:, 0:n], stats[:, 3, c], None,
                                                ALU.mult).then_inc(probs.sem, 1)

                    def keep_mix(s):
                        m, i, hh = steps[s]
                        half = slice(hh * HD, (hh + 1) * HD)
                        dve.wait_ge(mixed.sem, mixed.at(l, p * NST + s + 1))
                        nc.vector.tensor_copy(
                            xm[half, ds(p + (NP if m == "b" else 0), 1), i * P:(i + 1) * P].rearrange("q c n -> q (c n)"),
                            ps[half, 6 + s % 2, 0:P]).then_inc(mix_kept.sem, 1)

                    mask_and_max(0)
                    mask_and_max(1)
                    for s in range(NST):
                        if s + 2 < NST:
                            mask_and_max(s + 2)
                        normalize(s)
                        if s >= 2:
                            keep_mix(s - 2)
                    keep_mix(NST - 2)
                    keep_mix(NST - 1)
                meet(dve, l, 1)

                dve.wait_ge(masks_in.sem, masks_in.at(l, 80))
                nc.vector.tensor_tensor(p_s[:, 0:HB], sinks[0:NS, :], pick[:], ALU.mult).then_inc(sink_s.sem, 1)
                dve.wait_ge(sink_s.sem, sink_s.at(l, 1))
                nc.vector.reduce_sum(st_s[:, 10:11], p_s[:, 0:HB], AX.X).then_inc(sink_s.sem, 1)
                dve.wait_ge(sink_s.sem, sink_s.at(l, 2))
                nc.vector.tensor_scalar(st_s[:, 11:12], st_s[:, 10:11], -1.0, None, ALU.mult
                                        ).then_inc(sink_s.sem, 1)
                dve.wait_ge(sink_s.sem, sink_s.at(l, 3))
                dve.sem_inc(waits_alone, 1)
                with dve.Fori(0, NB) as b:
                    dve.wait_ge(s_scores.sem, s_scores.at(l, b))
                    dve.wait_ge(s_soft.sem, s_soft.at(l, 8 * b))
                    nc.vector.tensor_copy(q_now_a[:], q_rows_a[:, :, ds(b, 1)].rearrange("q c b h t -> q c (b h t)")
                                          ).then_inc(s_query.sem, 1)
                    nc.vector.tensor_copy(q_now_b[:], q_rows_b[:, ds(b, 1)].rearrange("q b h t -> q (b h t)")
                                          ).then_inc(s_query.sem, 1)
                    nc.vector.tensor_copy(mask_s[:, WIN + 4 * NFAR:], mask_sn[:, ds(b * NS, NS)]).then_inc(s_query.sem, 1)
                    nc.vector.tensor_copy(mask_t[:, LB:], mask_tn[:, ds(b * NS, NS)]).then_inc(s_query.sem, 1)
                    for pr in range(NP):
                        dve.wait_ge(s_turned.sem, s_turned.at(l, 9 * b + 2 * pr + 2))
                        nc.vector.tensor_copy(kt_s[:, pr, WIN:], ps[:, 2 * (pr % 2) + 1, 0:4 * NFAR]
                                              ).then_inc(far_kept.sem, 1)
                    dve.wait_ge(s_scores.sem, s_scores.at(l, b + 1))
                    dve.wait_ge(s_query.sem, s_query.at(l, 4 * b + 4))
                    dve.sem_inc(waits_alone, 1)
                    nc.vector.tensor_tensor_reduce(p_s[:, 0:WIN], ps[0:NS, 5, :], mask_s[:, 0:WIN], SCALE, 3e38,
                                                   ALU.add, ALU.min, st_s[:, 0:1]).then_inc(s_soft.sem, 1)
                    dve.wait_ge(s_soft.sem, s_soft.at(l, 8 * b + 1))
                    dve.sem_inc(waits_alone, 1)
                    nc.vector.tensor_tensor_reduce(p_s[:, WIN:NKEYS], ps[0:NS, 6, 0:NKEYS - WIN], mask_s[:, WIN:], SCALE,
                                                   st_s[:, 0:1], ALU.add, ALU.min, st_s[:, 1:2]).then_inc(s_soft.sem, 1)
                    nc.vector.tensor_tensor_reduce(p_s[:, NKEYS:], ps[0:NS, 7, 0:LB + NS], mask_t[:], SCALE,
                                                   st_s[:, 11:12], ALU.add, ALU.min, st_s[:, 2:3]).then_inc(s_soft.sem, 1)
                    dve.wait_ge(s_exped.sem, s_exped.at(l, 3 * b + 3))
                    nc.vector.tensor_tensor(st_s[:, 6:7], st_s[:, 6:7], st_s[:, 7:8], ALU.add).then_inc(s_soft.sem, 1)
                    dve.wait_ge(s_soft.sem, s_soft.at(l, 8 * b + 4))
                    nc.vector.reciprocal(st_s[:, 8:9], st_s[:, 5:6]).then_inc(s_soft.sem, 1)
                    nc.vector.reciprocal(st_s[:, 9:10], st_s[:, 6:7]).then_inc(s_soft.sem, 1)
                    dve.wait_ge(s_soft.sem, s_soft.at(l, 8 * b + 6))
                    nc.vector.tensor_scalar(p_s[:, 0:NKEYS], p_s[:, 0:NKEYS], st_s[:, 8:9], None, ALU.mult
                                            ).then_inc(s_soft.sem, 1)
                    nc.vector.tensor_scalar(p_s[:, NKEYS:], p_s[:, NKEYS:], st_s[:, 9:10], None, ALU.mult
                                            ).then_inc(s_soft.sem, 1)
                    dve.wait_ge(s_pturned.sem, s_pturned.at(l, b + 1))
                    for rows, a, z in ((P, 0, 4), (NFAR, 4, 8), (NS, 8, 9), (P, 9, 10), (NS, 10, 11)):
                        nc.vector.tensor_copy(pt_s[0:rows, a:z, :],
                                              ps[0:rows, 4, a * NS:z * NS].rearrange("p (a n) -> p a n", n=NS)
                                              ).then_inc(s_pkept.sem, 1)
                    dve.wait_ge(s_mixed.sem, s_mixed.at(l, b + 1))
                    for hh in range(2):
                        half = slice(hh * HD, (hh + 1) * HD)
                        nc.vector.tensor_copy(xm[half, 0:NP, ds(SEQ + b * TS, TS)],
                                              ps[half, 4, 384:416].rearrange("p (c n) -> p c n", c=NP)[
                                                  :, :, hh * TS:(hh + 1) * TS]).then_inc(s_mix_kept.sem, 1)
                        nc.vector.tensor_copy(xm[half, NP:2 * NP, ds(SEQ + b * TS, TS)],
                                              ps[half, 4, 416 + hh * 16:432 + hh * 16].rearrange(
                                                  "p (c n) -> p c n", c=NP)).then_inc(s_mix_kept.sem, 1)
                meet(dve, l, 2)

                norm_reciprocals(l, 1)
                norm_reciprocals(l, 2)
                norm_chunks(l, 1, GOUT, hf2, 0, g_hi, g_lo)
                norm_chunks(l, 2, GOUT, hf2, 3, g_hi, g_lo)
                dve.wait_ge(x_back.sem, x_back.at(l, 16))
                dve.sem_inc(waits_alone, 1)
                with dve.Fori(0, DC // 2) as dd:
                    for i in range(2):
                        dve.wait_ge(o_done[i].sem, o_done[i].at(l, dd + 1))
                        chunk = pieces(xm[:, ds(2 * dd + i, 1), :].rearrange("p c t -> p (c t)"))
                        nc.vector.tensor_tensor(chunk, chunk, banks(3 * i), ALU.add).then_inc(o_added[i].sem, 1)
                norm_reciprocals(l, 3)
                norm_chunks(l, 3, GFFN, hf2, 0, g_hi, g_lo)
                meet(dve, l, 3)

                with dve.Fori(0, FI) as f:
                    for k in range(HID):
                        a, n = divmod(k, NW)
                        dve.wait_ge(silued.sem, silued.at(l, HID * f + k + 1))
                        nc.vector.tensor_tensor(silu[:, k % 2, :], silu[:, k % 2, :], ps[:, 2 * (k % 2) + 1, 0:W],
                                                ALU.mult).then_inc(gated.sem, 1)
                        dve.wait_ge(act_hi.sem, act_hi.at(l, HID * f + k + 1))
                        nc.vector.tensor_tensor(a_lo[:, a, n * W:(n + 1) * W], silu[:, k % 2, :],
                                                a_hi[:, a, n * W:(n + 1) * W].bitcast(F32), ALU.subtract
                                                ).then_inc(act_lo.sem, 1)
                    for n in range(NW):
                        for d in range(DC):
                            dve.wait_ge(downed.sem, downed.at(l, DOWN * f + n * DC + d + 1))
                            xs = xm[:, d, n * W:(n + 1) * W]
                            nc.vector.tensor_tensor(xs, xs, ps[:, 4 + (n * DC + d) % 4, 0:W], ALU.add
                                                    ).then_inc(ffn_added.sem, 1)
                meet(dve, l, 4)
            for t in range(QT + 1):
                if t >= 2:
                    dve.wait_ge(y_tile_out[t % 2], 16 * (t // 2))
                for g in range(2):
                    dve.wait_ge(y_tile_turned, 2 * t + g + 1)
                    w = rows_of(t)
                    nc.vector.tensor_copy(xy_tile[t % 2][0:w, 0, g * 512:(g + 1) * 512],
                                          ps[0:w, (2 * t + g) % 8, :]).then_inc(y_tile_kept, 1)

        @block.tensor
        def _(pe):
            pe.wait_ge(consts_in, 16 * 7)
            for t in range(QT + 1):
                pe.wait_ge(x_tile_in[t % 2], 16 * (t // 2 + 1))
                w = rows_of(t)
                for g in range(2):
                    if 2 * t + g >= 8:
                        pe.wait_ge(x_tile_kept, 2 * t + g - 7)
                    for c in range(4):
                        mm = pe.transpose(ps[:, (2 * t + g) % 8, c * P:c * P + w],
                                          xy_tile[t % 2][0:w, 0, (4 * g + c) * P:(4 * g + c + 1) * P], ident[0:w, 0:w])
                    mm.then_inc(x_tile_turned, 1)

            def sum_squares(l, k, sq):
                first, n, before, width = NORMS[k]
                for c in range(n):
                    pe.wait_ge(sq_ready.sem, sq_ready.at(l, before + c + 1))
                    for t in range(QT + 1):
                        mm = pe.matmul(ps[0:rows_of(t), 6 + k % 2, t:t + 1], sq[c % 2][:, t * P:t * P + rows_of(t)],
                                       ones[:, 0:1], start=(c == 0 and t == 0), stop=(c == n - 1),
                                       skip_group_check=True)
                    mm.then_inc(sq_summed.sem, 1)

            def spread_roots(l, k, bank):
                pe.wait_ge(rs_ready.sem, rs_ready.at(l, 2 * k + 2))
                pe.sem_inc(waits_alone, 1)
                for t in range(QT + 1):
                    w = rows_of(t)
                    mm = pe.transpose(ps[:, bank + t // 4, (t % 4) * P:(t % 4) * P + w],
                                      roots[0:w, k % 2, t:t + 1].broadcast_to((w, P)), ident[0:w, 0:w])
                mm.then_inc(rs_spread.sem, 1)

            with pe.Fori(0, DEPTH) as l:
                meet(pe, l, 0)
                sum_squares(l, 0, sq1)
                spread_roots(l, 0, 0)
                pe.wait_ge(lo_ready.sem, lo_ready.at(l, 8))
                pe.wait_ge(zeroed.sem, zeroed.at(l, 6))

                def project(u, slot, bank, rest=None):
                    pe.wait_ge(w_split.sem, w_split.at(l, u + 1))
                    for n in range(NW):
                        if rest is not None and n == NW - 1:
                            pe.wait_ge(rest[0].sem, rest[0].at(l, rest[1]))
                        mm = product(pe, ps[:, bank + n, 0:W], lambda a, c: (w_hi, w_lo)[a][:, slot, c, :],
                                     lambda a, c: (h_hi, h_lo)[a][:, c, n * W:(n + 1) * W], DC)
                    mm.then_inc(projected.sem, 1)

                def sum_heads(bank, n, r):
                    pe.wait_ge(head_sq.sem, head_sq.at(l, n + 1))
                    pe.wait_ge(rope.sem, rope.at(l, r + 1))
                    for t in range(QT + 1):
                        mm = pe.matmul(ps[0:rows_of(t), bank, 2 * t:2 * t + 2], t_buf[1][:, t * P:t * P + rows_of(t)],
                                       blocks[:, 0:P:HD], start=True, stop=True)
                    mm.then_inc(head_summed.sem, 1)

                def spread_heads(bank, n):
                    pe.wait_ge(head_root.sem, head_root.at(l, 2 * n + 2))
                    pe.sem_inc(waits_alone, 1)
                    for t in range(QT + 1):
                        w = rows_of(t)
                        mm = pe.transpose(ps[:, bank + t // 4, (t % 4) * P:(t % 4) * P + w],
                                          t_buf[1][0:w, t * P:(t + 1) * P], ident[0:w, 0:w])
                    mm.then_inc(head_spread.sem, 1)

                def turn(src, rest, done):
                    for g in range(2):
                        for c in range(4):
                            mm = pe.transpose(ps[:, 6 + g, c * P:(c + 1) * P],
                                              src[:, (4 * g + c) * P:(4 * g + c + 1) * P], ident[:])
                        mm.then_inc(done.sem, 1)
                    pe.transpose(ps[0:NS, rest, 384:512], src[:, SEQ:T], ident[:]).then_inc(done.sem, 1)

                project(0, 0, 0)
                project(1, 1, 3)
                sum_heads(0, 0, 0)
                pe.wait_ge(v_staged.sem, v_staged.at(l, 1))
                turn(stage, 5, v_turned)
                spread_heads(0, 0)
                pe.wait_ge(rope.sem, rope.at(l, K_ROPE))
                pe.wait_ge(v_kept.sem, v_kept.at(l, 3))
                turn(kt_b, 2, k_turned)
                with pe.Fori(0, NP) as p:
                    u, r, h = 2 + 4 * p, K_ROPE + ROPE_P * p, 1 + 3 * p
                    pe.wait_ge(k_kept.sem, k_kept.at(l, 3 * p + 3))
                    pe.wait_ge(masked.sem, masked.at(l, NST * p))
                    pe.wait_ge(pt_ready.sem, pt_ready.at(l, NGR * p))
                    pe.wait_ge(mix_kept.sem, mix_kept.at(l, NST * p))
                    project(u, 0, 0)
                    project(u + 1, 1, 3)
                    sum_heads(0, h, r)
                    pe.wait_ge(v_staged.sem, v_staged.at(l, p + 2))
                    turn(stage, 5, v_turned)
                    spread_heads(0, h)
                    project(u + 2, 0, 3, (v_kept, 3 * p + 6))
                    pe.wait_ge(rope.sem, rope.at(l, r + K_ROPE))
                    pe.wait_ge(v_kept.sem, v_kept.at(l, 3 * p + 6))
                    turn(kt_a, 2, k_turned)
                    sum_heads(3, h + 1, r + K_ROPE)
                    project(u + 3, 1, 0, (k_kept, 3 * p + 6))
                    spread_heads(3, h + 1)
                    sum_heads(0, h + 2, r + K_ROPE + Q_ROPE)
                    spread_heads(0, h + 2)
                    pe.wait_ge(rope.sem, rope.at(l, r + ROPE_P))
                    pe.wait_ge(k_kept.sem, k_kept.at(l, 3 * p + 6))

                    def score(s):
                        m, i, hh = steps[s]
                        q, kt = (q_a, kt_a) if m == "a" else (q_b, kt_b)
                        n, first = P * len(key_tiles[s]), P * key_tiles[s][0]
                        if s >= 2:
                            pe.wait_ge(masked.sem, masked.at(l, p * NST + s - 1))
                        for c in range(0, n, 512):
                            w = min(512, n - c)
                            mm = pe.matmul(ps[:, 2 * (s % 2) + c // 512, 0:w], q[:, hh, i * P:(i + 1) * P],
                                           kt[:, first + c:first + c + w], start=True, stop=True)
                        mm.then_inc(scores.sem, 1)

                    def turn_probs(s):
                        pe.wait_ge(probs.sem, probs.at(l, p * NST + s + 1))
                        for g in groups_of[s]:
                            _, a, b = groups[g]
                            if g >= 2:
                                pe.wait_ge(pt_ready.sem, pt_ready.at(l, p * NGR + g - 1))
                            for c in range(a, b):
                                mm = pe.transpose(ps[:, 4 + g % 2, (c - a) * P:(c - a + 1) * P],
                                                  t_buf[s % 3][:, c * P:(c + 1) * P], ident[:])
                            mm.then_inc(p_turned.sem, 1)

                    def mix(s):
                        m, i, hh = steps[s]
                        v = v_a if m == "a" else v_b
                        if s >= 2:
                            pe.wait_ge(mix_kept.sem, mix_kept.at(l, p * NST + s - 1))
                        for g in groups_of[s]:
                            _, a, b = groups[g]
                            pe.wait_ge(pt_ready.sem, pt_ready.at(l, p * NGR + g + 1))
                            for c in range(a, b):
                                mm = pe.matmul(ps[:, 6 + s % 2, 0:P], v[:, key_tiles[s][c], :],
                                               pt[:, g % 3, (c - a) * P:(c - a + 1) * P],
                                               start=(c == 0), stop=(c == len(key_tiles[s]) - 1))
                        mm.then_inc(mixed.sem, 1)

                    score(0)
                    score(1)
                    for s in range(NST):
                        if s + 2 < NST:
                            score(s + 2)
                        turn_probs(s)
                        if s >= 1:
                            mix(s - 1)
                    mix(NST - 1)
                meet(pe, l, 1)

                with pe.Fori(0, NB // 2) as bb:
                    for i in range(2):
                        b = 2 * bb + i
                        pe.wait_ge(kv_in[i].sem, kv_in[i].at(l, 48 * (bb + 1)))
                        pe.sem_inc(waits_alone, 1)
                        for pr in range(NP):
                            if pr >= 2:
                                pe.wait_ge(near_kept.sem, near_kept.at(l, 5 * b + pr - 1))
                                pe.sem_inc(waits_alone, 1)
                            for c in range(4):
                                mm = pe.transpose(ps[:, 2 * (pr % 2), c * P:(c + 1) * P],
                                                  near[i][:, c, pr * P:(pr + 1) * P], ident[:])
                            mm.then_inc(s_turned.sem, 1)
                            if pr >= 2:
                                pe.wait_ge(far_kept.sem, far_kept.at(l, 4 * b + pr - 1))
                                pe.sem_inc(waits_alone, 1)
                            for c in range(4):
                                mm = pe.transpose(ps[:, 2 * (pr % 2) + 1, c * NFAR:(c + 1) * NFAR],
                                                  far[i][:, c, pr * P:(pr + 1) * P], ident[0:NFAR, 0:NFAR])
                            mm.then_inc(s_turned.sem, 1)
                        pe.transpose(ps[:, 7, 256:384], last[i][:, 0, :], ident[:]).then_inc(s_turned.sem, 1)
                        pe.wait_ge(near_kept.sem, near_kept.at(l, 5 * b + 5))
                        pe.wait_ge(far_kept.sem, far_kept.at(l, 4 * b + 4))
                        pe.wait_ge(s_query.sem, s_query.at(l, 4 * b + 4))
                        for out, keys in ((ps[0:NS, 5, :], lambda pr: kt_s[:, pr, 0:WIN]),
                                          (ps[0:NS, 6, 0:4 * NFAR], lambda pr: kt_s[:, pr, WIN:]),
                                          (ps[0:NS, 6, 4 * NFAR:NKEYS - WIN], lambda pr: k_new_a[:, pr, :])):
                            for pr in range(NP):
                                pe.matmul(out, q_now_a[:, pr, :], keys(pr), start=(pr == 0), stop=(pr == NP - 1))
                        pe.matmul(ps[0:NS, 7, 0:LB], q_now_b[:], kt_t[:], start=True, stop=True)
                        pe.matmul(ps[0:NS, 7, LB:LB + NS], q_now_b[:], k_new_b[:], start=True, stop=True
                                  ).then_inc(s_scores.sem, 1)
                        pe.wait_ge(s_soft.sem, s_soft.at(l, 8 * b + 8))
                        pe.sem_inc(waits_alone, 1)
                        cols = [(c * P, P) for c in range(4)] + [(WIN + c * NFAR, NFAR) for c in range(4)] + \
                               [(WIN + 4 * NFAR, NS), (NKEYS, LB), (NKEYS + LB, NS)]
                        for c, (a, w) in enumerate(cols):
                            mm = pe.transpose(ps[0:w, 4, c * NS:(c + 1) * NS], p_s[:, a:a + w], ident[0:NS, 0:NS])
                        mm.then_inc(s_pturned.sem, 1)
                        pe.wait_ge(s_pkept.sem, s_pkept.at(l, 5 * b + 5))
                        pe.wait_ge(s_mix_kept.sem, s_mix_kept.at(l, 4 * b))
                        for pr in range(NP):
                            out = ps[:, 4, 384 + 8 * pr:392 + 8 * pr]
                            v_cols = slice(WA + pr * P, WA + (pr + 1) * P)
                            for c in range(4):
                                pe.matmul(out, near[i][:, c, v_cols], pt_s[:, c, 8 * pr:8 * pr + 8],
                                          start=(c == 0), stop=False)
                            for c in range(4):
                                pe.matmul(out, far[i][:, c, v_cols], pt_s[0:NFAR, 4 + c, 8 * pr:8 * pr + 8],
                                          start=False, stop=False)
                            pe.matmul(out, kv_rows[:, 1, pr, :], pt_s[0:NS, 8, 8 * pr:8 * pr + 8],
                                      start=False, stop=True)
                        pe.matmul(ps[:, 4, 416:448], last[i][:, 1, :], pt_s[:, 9, :], start=True, stop=False)
                        pe.matmul(ps[:, 4, 416:448], kv_rows[:, 1, NP, :], pt_s[0:NS, 10, :], start=False, stop=True
                                  ).then_inc(s_mixed.sem, 1)
                meet(pe, l, 2)

                sum_squares(l, 1, sq2)
                sum_squares(l, 2, sq2)
                spread_roots(l, 1, 0)
                spread_roots(l, 2, 3)
                pe.wait_ge(lo_ready.sem, lo_ready.at(l, 16))
                pe.sem_inc(waits_alone, 1)
                with pe.Fori(0, DC // 2) as dd:
                    for i in range(2):
                        pe.wait_ge(o_split.sem, o_split.at(l, 2 * dd + i + 1))
                        pe.wait_ge(o_added[i].sem, o_added[i].at(l, dd))
                        for n in range(NW):
                            mm = product(pe, ps[:, 3 * i + n, 0:W], lambda a, c: (f_hi, f_lo)[a][i][:, c * P:(c + 1) * P],
                                         lambda a, c: (g_hi, g_lo)[a][:, c, n * W:(n + 1) * W], DC)
                        mm.then_inc(o_done[i].sem, 1)
                pe.wait_ge(o_added[0].sem, o_added[0].at(l, DC // 2))
                sum_squares(l, 3, sq2)
                spread_roots(l, 3, 0)
                meet(pe, l, 3)

                with pe.Fori(0, FI) as f:
                    pe.wait_ge(f_split.sem, f_split.at(l, 3 * f + 2))
                    for k in range(HID):
                        a, n = divmod(k, NW)
                        pe.wait_ge(gated.sem, gated.at(l, HID * f + max(k - 1, 0)))
                        for j in range(2):
                            mm = product(pe, ps[:, 2 * (k % 2) + j, 0:W],
                                         lambda h, c: (f_hi, f_lo)[h][j][:, c * 2 * P + a * P:c * 2 * P + (a + 1) * P],
                                         lambda h, c: (g_hi, g_lo)[h][:, c, n * W:(n + 1) * W], DC)
                        mm.then_inc(hid.sem, 1)
                    pe.wait_ge(f_split.sem, f_split.at(l, 3 * f + 3))
                    for n in range(NW):
                        pe.wait_ge(act_lo.sem, act_lo.at(l, HID * f + NW + n + 1))
                        for d in range(DC):
                            x = n * DC + d
                            pe.wait_ge(ffn_added.sem, ffn_added.at(l, DOWN * f + max(x - 3, 0)))
                            product(pe, ps[:, 4 + x % 4, 0:W],
                                    lambda h, c: (f_hi, f_lo)[h][2][:, c * D + d * P:c * D + (d + 1) * P],
                                    lambda h, c: (a_hi, a_lo)[h][:, c, n * W:(n + 1) * W], 2
                                    ).then_inc(downed.sem, 1)
                meet(pe, l, 4)
            for t in range(QT + 1):
                w = rows_of(t)
                for g in range(2):
                    if 2 * t + g >= 8:
                        pe.wait_ge(y_tile_kept, 2 * t + g - 7)
                    for c in range(4):
                        mm = pe.transpose(ps[0:w, (2 * t + g) % 8, c * P:(c + 1) * P],
                                          xm[:, 4 * g + c, t * P:t * P + w], ident[:])
                    mm.then_inc(y_tile_turned, 1)


_INS = ["x_prompt", "x_sample", "cache_a", "cache_b", "attn_norm", "w_in", "q_norm_a", "k_norm_a", "q_norm_b",
        "k_norm_b", "sinks_b", "out_norm_a", "out_norm_b", "w_out", "ffn_norm", "w_gate_up", "w_down"]
_OUTS = [(1, SEQ, D), (NB, TS, D), (DEPTH, 1, SEQ, 2, HA, HD), (DEPTH, 1, LB, 2, KVB, HD),
         (DEPTH, NB, LA, 2, HA, HD), (DEPTH, NB, LB, 2, KVB, HD)]


def kernel(**inputs):
    import concourse.bacc as _bacc
    from concourse.bass_utils import run_bass_kernel_spmd as _run

    nc = _bacc.Bacc("TRN2", target_bir_lowering=False, num_devices=1)
    arrays, args = {}, []
    tables = constants()
    for name, a in [(n, np.ascontiguousarray(inputs[n])) for n in _INS] + list(tables.items()):
        arrays[f"in_{name}_dram"] = a
        args.append(nc.dram_tensor(f"in_{name}_dram", a.shape, mybir.dt.from_np(a.dtype), kind="ExternalInput").ap())
    for i, shape in enumerate(_OUTS):
        args.append(nc.dram_tensor(f"out_{i}_dram", shape, F32, kind="ExternalOutput").ap())
    trunk(nc, *args)
    r = _run(nc, [arrays], core_ids=[0])
    return tuple(r.results[0][f"out_{i}_dram"] for i in range(len(_OUTS)))
```

```python
from contextlib import ExitStack
import math

import numpy as np
import concourse.bass as bass
from concourse import mybir

F32 = mybir.dt.float32
F32R = mybir.dt.float32r
ACT = mybir.ActivationFunctionType
ALU = mybir.AluOpType
AX = mybir.AxisListType
ds = bass.ds

P = 128
D = 1024
DC = D // P
SEQ = 1024
QT = SEQ // P
DEPTH = 2
NB, TS = 8, 4
NS = NB * TS
T = SEQ + NS
NW = 3
W = T // NW
HD = 64
HA, HB, KVB = 8, 8, 2
NP = HA // 2
LA, LB = 2048, 128
PAST = 4096
FF = 2816
FI = FF // (2 * P)
ROT = HD // 4
EPS = 1e-6
SCALE = HD ** -0.5
WA = HA * HD
COL_QA, COL_KA, COL_VA, COL_QB, COL_KB, COL_VB = 0, WA, 2 * WA, 3 * WA, 4 * WA, 4 * WA + KVB * HD
NEG = -1e30
WIN = 512
NFAR = (LA - WIN) // 16
NKEYS = WIN + 4 * NFAR + NS
GQA, GKA, GQB, GKB, GATT, GFFN, GOUT = 0, 1, 2, 3, 4, 12, 20
NG = 28
A_STEPS = [(i, hh) for i in range(QT) for hh in range(2)]
NSTEP = len(A_STEPS)


def copies(dist):
    n = np.zeros(dist.shape)
    for w, d in ((128, 1), (512, 4), (2048, 16)):
        n += (dist >= 0) & (dist <= w) & (dist % d == 0)
    return n


def log_mask(n):
    return -np.where(n > 0, np.log(np.maximum(n, 1)) / SCALE, NEG).astype(np.float32)


def constants():
    c = {}
    c["c_ident"] = np.eye(P, dtype=np.float32)
    c["c_ones"] = np.ones((P, P), np.float32)
    c["c_blocks"] = np.kron(np.eye(2), np.ones((HD, HD))).astype(np.float32)
    pos = np.concatenate([np.arange(SEQ), np.tile(PAST + np.arange(TS), NB)]).astype(np.float32)
    inv = np.exp(np.float32(-math.log(500000.0)) * np.arange(0, ROT, 2).astype(np.float32) / np.float32(ROT)).astype(np.float32)
    ang = (inv[:, None] * pos[None, :]).astype(np.float32).astype(np.float64)
    cos, sin = np.ones((HD, T)), np.zeros((HD, T))
    h = ROT // 2
    cos[:h] = cos[h:ROT] = np.cos(ang)
    sin[:h], sin[h:ROT] = -np.sin(ang), np.sin(ang)
    c["c_cos"] = np.tile(cos, (2, 1)).astype(np.float32)
    c["c_sin"] = np.tile(sin, (2, 1)).astype(np.float32)
    q = np.arange(P)[:, None]
    c["c_mask_a"] = log_mask(copies(q + (QT - 1) * P - np.arange(SEQ)[None, :]))
    dist = q + P - np.arange(2 * P)[None, :]
    c["c_mask_b"] = log_mask((dist >= 0) & (dist < 128))
    t = (np.arange(NS) % TS)[:, None]
    near = (LA - WIN) + TS * np.arange(P)[None, :] + np.arange(4)[:, None]
    far = 16 * np.arange(NFAR)[None, :] + np.arange(4)[:, None]
    rows = np.concatenate([near.ravel(), far.ravel()])[None, :]
    c["c_mask_s"] = log_mask(copies(LA + t - rows))
    new_b = (np.arange(NS) // TS)[None, None, :]
    new_t = (np.arange(NS) % TS)[None, None, :]
    dn = t[:, :, None] - new_t
    same = new_b == np.arange(NB)[None, :, None]
    c["c_mask_sn"] = log_mask(copies(dn) * same).reshape(NS, NB * NS)
    c["c_mask_t"] = log_mask((LB + t - np.arange(LB)[None, :]) < 128)
    c["c_mask_tn"] = log_mask((dn >= 0) * same).reshape(NS, NB * NS)
    c["c_pick"] = ((np.arange(NS) // TS)[:, None] == np.arange(HB)[None, :]).astype(np.float32)
    return c


def trunk(nc, x_prompt, x_sample, cache_a, cache_b, attn_norm, w_in, q_norm_a, k_norm_a, q_norm_b,
          k_norm_b, sinks_b, out_norm_a, out_norm_b, w_out, ffn_norm, w_gate_up, w_down,
          c_ident, c_ones, c_blocks, c_cos, c_sin, c_mask_a, c_mask_b, c_mask_s, c_mask_sn,
          c_mask_t, c_mask_tn, c_pick,
          y_prompt, y_sample, new_a_p, new_b_p, new_a_s, new_b_s):
    x_spill = nc.dram_tensor("x_spill", (P, DC * T), F32).ap()
    with ExitStack() as ctx:
        ctx.enter_context(nc.allow_non_contiguous_dma(reason="small gains are laid on partitions"))

        def tensor(scope, name, shape, dt=F32):
            return scope.enter_context(nc.sbuf_tensor(name, shape, dt))

        def sem(name):
            return ctx.enter_context(nc.semaphore(name))

        class Signal:
            def __init__(self, name, per_layer, starts=0):
                self.sem, self.per_layer, self.starts = sem(name), per_layer, starts

            def at(self, layer, count):
                return layer * self.per_layer + count + self.starts

        ident = tensor(ctx, "ident", [P, P])
        ones = tensor(ctx, "ones", [P, P])
        blocks = tensor(ctx, "blocks", [P, P])
        cos = tensor(ctx, "cos", [P, T])
        sin = tensor(ctx, "sin", [P, T])
        mask_a = tensor(ctx, "mask_a", [P, SEQ])
        mask_b = tensor(ctx, "mask_b", [P, 2 * P])
        gains_all = tensor(ctx, "gains_all", [P, DEPTH * NG])
        sinks_all = tensor(ctx, "sinks_all", [P, DEPTH * HB])
        gains = tensor(ctx, "gains", [P, NG])
        sinks = tensor(ctx, "sinks", [P, HB])
        eps = tensor(ctx, "eps", [P, 1])
        roots = tensor(ctx, "roots", [P, 2, QT + 1])
        xm = tensor(ctx, "xm", [P, DC, T])

        mixer = ExitStack()
        q_rows_a = tensor(mixer, "q_rows_a", [P, NP, NB, HA, TS])
        q_rows_b = tensor(mixer, "q_rows_b", [P, NB, HB, TS])
        k_new_a = tensor(mixer, "k_new_a", [P, NP, NS])
        k_new_b = tensor(mixer, "k_new_b", [P, NS])
        kv_rows = tensor(mixer, "kv_rows", [NS, 2, NP + 1, P])

        pairs = ExitStack()
        h_hi = tensor(pairs, "h_hi", [P, DC, T], F32R)
        h_lo = tensor(pairs, "h_lo", [P, DC, T], F32R)
        w_raw = tensor(pairs, "w_raw", [P, DC, P])
        w_hi = tensor(pairs, "w_hi", [P, 2, DC, P], F32R)
        w_lo = tensor(pairs, "w_lo", [P, 2, DC, P], F32R)
        t_buf = [tensor(pairs, f"t_buf{i}", [P, T if i != 1 else (QT + 1) * P]) for i in range(3)]
        kt_a = tensor(pairs, "kt_a", [P, T])
        kt_b = tensor(pairs, "kt_b", [P, T])
        q_a = tensor(pairs, "q_a", [P, 2, SEQ])
        q_b = tensor(pairs, "q_b", [P, 2, SEQ])
        v_a = tensor(pairs, "v_a", [P, QT, P])
        v_b = tensor(pairs, "v_b", [P, QT, P])
        stage = tensor(pairs, "stage", [P, T])
        pt = tensor(pairs, "pt", [P, 3, 4 * P])
        head_means = tensor(pairs, "head_means", [P, 2, 2 * (QT + 1)])
        stats = tensor(pairs, "stats", [P, 5, 4])
        sink_now = tensor(pairs, "sink_now", [P, 2])
        sink_raw = tensor(pairs, "sink_raw", [P, 2])
        sq1, hf1 = [t_buf[0], t_buf[2]], [kt_a, kt_b]
        xy_tile = [q_a, q_b]
        pairs.close()

        samples = ExitStack()
        near = [tensor(samples, f"near{i}", [P, 4, 2 * WA]) for i in range(2)]
        far = [tensor(samples, f"far{i}", [NFAR, 4, 2 * WA]) for i in range(2)]
        last = [tensor(samples, f"last{i}", [P, 2, P]) for i in range(2)]
        mask_s = tensor(samples, "mask_s", [NS, NKEYS])
        mask_t = tensor(samples, "mask_t", [NS, LB + NS])
        mask_sn = tensor(samples, "mask_sn", [NS, NB * NS])
        mask_tn = tensor(samples, "mask_tn", [NS, NB * NS])
        pick = tensor(samples, "pick", [NS, HB])
        kt_s = tensor(samples, "kt_s", [P, NP, WIN + 4 * NFAR])
        kt_t = tensor(samples, "kt_t", [P, P])
        q_now_a = tensor(samples, "q_now_a", [P, NP, NS])
        q_now_b = tensor(samples, "q_now_b", [P, NS])
        p_s = tensor(samples, "p_s", [NS, NKEYS + LB + NS])
        pt_s = tensor(samples, "pt_s", [P, 11, NS])
        st_s = tensor(samples, "st_s", [NS, 16])
        samples.close()
        mixer.close()

        dense = ExitStack()
        g_hi = tensor(dense, "g_hi", [P, DC, T], F32R)
        g_lo = tensor(dense, "g_lo", [P, DC, T], F32R)
        norms = ExitStack()
        sq2 = [tensor(norms, f"sq2_{i}", [P, T]) for i in range(2)]
        hf2 = [tensor(norms, f"hf2_{i}", [P, T]) for i in range(2)]
        norms.close()
        hidden = ExitStack()
        a_hi = tensor(hidden, "a_hi", [P, 2, T], F32R)
        a_lo = tensor(hidden, "a_lo", [P, 2, T], F32R)
        silu = tensor(hidden, "silu", [P, 2, W])
        f_hi, f_lo = [None] * 3, [None] * 3
        for j in (2, 0, 1):
            f_hi[j] = tensor(hidden, f"f_hi{j}", [P, 2 * D], F32R)
            f_lo[j] = tensor(hidden, f"f_lo{j}", [P, 2 * D], F32R)
        f_raw = [tensor(hidden, f"f_raw{i}", [P, 2 * D]) for i in range(2)]
        hidden.close()
        dense.close()

        ps = ctx.enter_context(nc.psum_tensor("ps", [P, 8, 512], F32))

        consts_in = sem("consts_in")
        eps_set = sem("eps_set")
        x_tile_in = [sem(f"x_tile_in{i}") for i in range(2)]
        x_tile_turned = sem("x_tile_turned")
        x_tile_kept = sem("x_tile_kept")
        y_tile_turned = sem("y_tile_turned")
        y_tile_kept = sem("y_tile_kept")
        y_tile_out = [sem(f"y_tile_out{i}") for i in range(2)]
        met = sem("met")
        waits_alone = sem("waits_alone")

        N_GAINS = 8 + 6 * DEPTH
        gains_in = sem("gains_in")
        gains_now = Signal("gains_now", 2)
        spilled = Signal("spilled", 16)
        zeroed = Signal("zeroed", 6)
        sq_ready = Signal("sq_ready", 24)
        sq_summed = Signal("sq_summed", 24)
        root_ready = Signal("root_ready", 8)
        rs_ready = Signal("rs_ready", 8)
        rs_spread = Signal("rs_spread", 4)
        hf_ready = Signal("hf_ready", 24)
        hi_ready = Signal("hi_ready", 24)
        lo_ready = Signal("lo_ready", 24)

        UNITS = 2 + 4 * NP
        RAW = [16, 32]
        RAW_P = [16, 32, 64, 80]
        w_raw_in = Signal("w_raw_in", 32 + 80 * NP)
        w_hi_ready = Signal("w_hi_ready", UNITS)
        w_split = Signal("w_split", UNITS, starts=1)
        projected = Signal("projected", UNITS)
        K_ROPE, Q_ROPE = 11, 13
        ROPE_P = K_ROPE + 2 * Q_ROPE
        rope = Signal("rope", K_ROPE + ROPE_P * NP, starts=1)
        head_sq = Signal("head_sq", 1 + 3 * NP)
        head_summed = Signal("head_summed", 1 + 3 * NP)
        head_root = Signal("head_root", 2 * (1 + 3 * NP))
        head_spread = Signal("head_spread", 1 + 3 * NP)
        v_staged = Signal("v_staged", 1 + NP)
        v_turned = Signal("v_turned", 3 * (1 + NP))
        v_kept = Signal("v_kept", 3 * (1 + NP))
        k_turned = Signal("k_turned", 3 * (1 + NP))
        k_kept = Signal("k_kept", 3 * (1 + NP))
        v_out = Signal("v_out", 16 * (1 + NP))
        k_out = Signal("k_out", 16 * (1 + NP))
        sink_ready = Signal("sink_ready", 2 * NP)

        steps = [(m, i, hh) for m in "ab" for i in range(QT) for hh in range(2)]
        NST = len(steps)
        key_tiles = [list(range(i + 1)) if m == "a" else list(range(max(i - 1, 0), i + 1)) for m, i, hh in steps]
        groups = []
        for s, tiles in enumerate(key_tiles):
            groups += [(s, g, min(g + 4, len(tiles))) for g in range(0, len(tiles), 4)]
        NGR = len(groups)
        groups_of = [[g for g in range(NGR) if groups[g][0] == s] for s in range(NST)]
        exps_to = [sum(1 + (m == "b") for m, _, _ in steps[:s + 1]) for s in range(NST)]
        NEXP = exps_to[-1]
        scores = Signal("scores", NP * NST)
        masked = Signal("masked", NP * NST, starts=1)
        exped = Signal("exped", NP * NEXP)
        sum_ready = Signal("sum_ready", NP * NEXP)
        probs = Signal("probs", NP * NST)
        p_turned = Signal("p_turned", NP * NGR)
        pt_ready = Signal("pt_ready", NP * NGR, starts=1)
        mixed = Signal("mixed", NP * NST)
        mix_kept = Signal("mix_kept", NP * NST, starts=1)

        rows_out = Signal("rows_out", 16 * 4)
        cache_out = Signal("cache_out", 16 * 2 * NB)
        masks_in = Signal("masks_in", 16 * 5)
        sink_s = Signal("sink_s", 3)
        k_in = [Signal(f"k_in{i}", 16 * 3 * NB // 2) for i in range(2)]
        v_in = [Signal(f"v_in{i}", 16 * 3 * NB // 2) for i in range(2)]
        s_turned = Signal("s_turned", 8 * NB)
        near_kept = Signal("near_kept", 4 * NB)
        far_kept = Signal("far_kept", 5 * NB)
        s_query = Signal("s_query", 4 * NB)
        s_scores = Signal("s_scores", NB, starts=1)
        s_soft = Signal("s_soft", 8 * NB, starts=1)
        s_exped = Signal("s_exped", 3 * NB)
        s_pturned = Signal("s_pturned", NB)
        s_pkept = Signal("s_pkept", 5 * NB)
        s_mixed = Signal("s_mixed", 2 * NB)
        s_rows = Signal("s_rows", NB)
        s_mix_turned = Signal("s_mix_turned", NB)
        s_mix_kept = Signal("s_mix_kept", 4 * NB, starts=1)

        x_back = Signal("x_back", 16)
        o_raw_in = [Signal(f"o_raw_in{i}", 16 * 3 * DC // 2) for i in range(2)]
        o_hi_ready = Signal("o_hi_ready", DC)
        o_split = Signal("o_split", DC, starts=1)
        o_done = [Signal(f"o_done{i}", DC // 2, starts=1) for i in range(2)]
        o_added = [Signal(f"o_added{i}", DC // 2, starts=1) for i in range(2)]

        f_raw_in = [Signal(f"f_raw_in{j}", 16 * FI) for j in range(3)]
        f_hi_ready = Signal("f_hi_ready", 3 * FI)
        f_split = Signal("f_split", 3 * FI, starts=1)
        HID = 2 * NW
        DOWN = NW * DC
        hid = Signal("hid", HID * FI, starts=1)
        silued = Signal("silued", HID * FI)
        gated = Signal("gated", HID * FI, starts=1)
        act_hi = Signal("act_hi", HID * FI)
        act_lo = Signal("act_lo", HID * FI, starts=1)
        downed = Signal("downed", DOWN * FI, starts=1)
        ffn_added = Signal("ffn_added", DOWN * FI, starts=1)

        MEETS = 3

        def meet(eng, layer, k):
            eng.drain().then_inc(met, 1)
            eng.wait_ge(met, 5 + layer * 5 * MEETS + 5 * (k + 1))
            eng.sem_inc(waits_alone, 1)

        def pieces(ap):
            return ap.rearrange("p (n w) -> p n w", n=NW)

        def banks(b):
            return ps[:, b:b + NW, 0:W]

        def flat(b):
            return ps[:, b:b + NW, :].rearrange("p b c -> p (b c)")[:, 0:T]

        def rows_of(t):
            return P if t < QT else NS

        NORMS = [(0, DC, 0, D), (0, NP, 8, WA), (NP, NP, 12, WA), (0, DC, 16, D)]

        def product(pe, out, left, right, n):
            mm = None
            for c in range(n):
                for k, (a, b) in enumerate(((0, 0), (1, 0), (0, 1))):
                    mm = pe.matmul(out, left(a, c), right(b, c), start=(c == 0 and k == 0),
                                   stop=(c == n - 1 and k == 2))
            return mm

        block = ctx.enter_context(nc.Block())

        @block.sync
        def _(sp):
            for signal in (w_split, rope, o_split, f_split, masked, pt_ready, mix_kept, hid, gated, downed,
                           ffn_added, act_lo, s_scores, s_soft, s_mix_kept, *o_done, *o_added):
                sp.sem_inc(signal.sem, 1)
            for dst, src in ((ident, c_ident), (ones, c_ones), (blocks, c_blocks), (cos, c_cos),
                             (sin, c_sin), (mask_a, c_mask_a), (mask_b, c_mask_b)):
                sp.dma_start(dst[:], src).then_inc(consts_in, 16)
            for hh in range(2):
                half = slice(hh * HD, (hh + 1) * HD)
                by_layer = gains_all[half, :].rearrange("p (l g) -> p l g", l=DEPTH)
                for g, src in ((GQA, q_norm_a), (GKA, k_norm_a), (GQB, q_norm_b), (GKB, k_norm_b)):
                    sp.dma_start(by_layer[:, :, g], src.rearrange("l p -> p l")).then_inc(gains_in, 16)
                for l in range(DEPTH):
                    sp.dma_start(by_layer[:, l, GOUT + NP:GOUT + 2 * NP],
                                 out_norm_b[l, hh * NP * HD:(hh + 1) * NP * HD].rearrange(
                                     "(c p) -> p c", p=HD)).then_inc(gains_in, 16)
            for l in range(DEPTH):
                for g, src, n in ((GATT, attn_norm, DC), (GFFN, ffn_norm, DC), (GOUT, out_norm_a, NP)):
                    sp.dma_start(gains_all[:, l * NG + g:l * NG + g + n], src[l].rearrange("(c p) -> p c", p=P)
                                 ).then_inc(gains_in, 16)
                sp.dma_start(sinks_all[:, l * HB:(l + 1) * HB], sinks_b[l:l + 1].broadcast_to((P, HB))
                             ).then_inc(gains_in, 16)
            for t in range(QT + 1):
                if t >= 2:
                    sp.wait_ge(x_tile_turned, 2 * (t - 1))
                src = x_prompt[0, t * P:(t + 1) * P, :] if t < QT else x_sample.rearrange("b t d -> (b t) d")
                sp.dma_start(xy_tile[t % 2][0:rows_of(t), 0, :], src).then_inc(x_tile_in[t % 2], 16)
            sp.wait_ge(x_tile_kept, 2 * (QT + 1))
            sp.wait_ge(gains_in, 16 * N_GAINS)
            sp.drain().then_inc(met, 1)
            sp.wait_ge(met, 5)
            with sp.Fori(0, DEPTH) as l:
                def layer(ap):
                    return ap[ds(l, 1)]

                def w_load(u, col):
                    sp.wait_ge(w_split.sem, w_split.at(l, u))
                    sp.sem_inc(waits_alone, 1)
                    sp.dma_start(w_raw[:], layer(w_in)[:, :, ds(col, P)].rearrange(
                        "l (c p) n -> p (l c) n", p=P)).then_inc(w_raw_in.sem, 16)

                w_load(0, COL_KB)
                sp.dma_start(x_spill, xm[:].rearrange("p c t -> p (c t)")).then_inc(spilled.sem, 16)
                w_load(1, COL_VB)
                sp.wait_ge(k_kept.sem, k_kept.at(l, 3))
                sp.sem_inc(waits_alone, 1)
                sp.dma_start(layer(new_b_p)[:, 0, :, 0].rearrange("l t h d -> (l t) (h d)"),
                             stage[:, (QT - 1) * P:QT * P]).then_inc(k_out.sem, 16)
                sp.wait_ge(v_kept.sem, v_kept.at(l, 3))
                sp.sem_inc(waits_alone, 1)
                sp.dma_start(layer(new_b_p)[:, 0, :, 1].rearrange("l t h d -> (l t) (h d)"),
                             v_b[:, QT - 1, :]).then_inc(v_out.sem, 16)
                with sp.Fori(0, NP) as p:
                    w_load(2 + 4 * p, COL_KA + p * P)
                    w_load(3 + 4 * p, COL_QA + p * P)
                    sp.wait_ge(w_split.sem, w_split.at(l, 4 + 4 * p))
                    sp.sem_inc(waits_alone, 1)
                    for hh in range(2):
                        sp.dma_start(w_raw[:, :, hh * HD:(hh + 1) * HD],
                                     layer(w_in)[:, :, ds(COL_QB + 4 * hh * HD + p * HD, HD)].rearrange(
                                         "l (c p) n -> p (l c) n", p=P)).then_inc(w_raw_in.sem, 16)
                    w_load(5 + 4 * p, COL_VA + p * P)
                    for kv, kept, out, rows in ((0, k_kept, k_out, stage[:, 0:SEQ].rearrange("p (j n) -> p j n", j=QT)),
                                                (1, v_kept, v_out, v_a[:])):
                        sp.wait_ge(kept.sem, kept.at(l, 6 + 3 * p))
                        sp.sem_inc(waits_alone, 1)
                        sp.dma_start(layer(new_a_p)[:, 0, :, kv].rearrange(
                            "l (j q) h d -> q (l j) (h d)", q=P)[:, :, ds(p * P, P)], rows).then_inc(out.sem, 16)
                sp.wait_ge(projected.sem, projected.at(l, UNITS))
                sp.sem_inc(waits_alone, 1)
                for dst, src in ((mask_s[:, 0:WIN + 4 * NFAR], c_mask_s), (mask_t[:, 0:LB], c_mask_t),
                                 (mask_sn[:], c_mask_sn), (mask_tn[:], c_mask_tn), (pick[:], c_pick)):
                    sp.dma_start(dst, src).then_inc(masks_in.sem, 16)

                def kv_load(kv, i, b):
                    arrived, side = (k_in, v_in)[kv][i].sem, slice(kv * WA, (kv + 1) * WA)
                    rows = layer(cache_a)[:, ds(b, 1), :, kv]
                    sp.dma_start(near[i][:, :, side], rows[:, :, LA - WIN:LA].rearrange(
                        "l b (k r) h d -> (l b k) r (h d)", r=4)).then_inc(arrived, 16)
                    sp.dma_start(far[i][:, :, side], rows[:, :, 0:LA - WIN].rearrange(
                        "l b (k r) h d -> (l b k) r (h d)", r=16)[:, 0:4, :]).then_inc(arrived, 16)
                    sp.dma_start(last[i][:, kv, :], layer(cache_b)[:, ds(b, 1), :, kv].rearrange(
                        "l b k h d -> (l b k) (h d)")).then_inc(arrived, 16)

                for i in range(2):
                    for kv in range(2):
                        kv_load(kv, i, i)
                sp.wait_ge(v_out.sem, v_out.at(l, 16 * (1 + NP)))
                sp.sem_inc(waits_alone, 1)
                sp.wait_ge(k_out.sem, k_out.at(l, 16 * (1 + NP)))
                sp.sem_inc(waits_alone, 1)
                meet(sp, l, 0)

                for kv in range(2):
                    sp.dma_start(layer(new_a_s)[:, :, LA - TS:LA, kv].rearrange("l b t h d -> (l b) t (h d)"),
                                 kv_rows[:, kv, 0:NP, :].rearrange("q c n -> q (c n)")).then_inc(rows_out.sem, 16)
                    sp.dma_start(layer(new_b_s)[:, :, LB - TS:LB, kv].rearrange("l b t h d -> (l b) t (h d)"),
                                 kv_rows[:, kv, NP, :]).then_inc(rows_out.sem, 16)
                def o_load(i, u):
                    raw = f_raw[i][:, 0:D].rearrange("p (c n) -> p c n", c=DC)
                    wo = layer(w_out)[:, :, ds(u * P, P)]
                    sp.dma_start(raw[:, 0:NP, :], wo[:, 0:WA].rearrange(
                        "l (c p) n -> p (l c) n", p=P)).then_inc(o_raw_in[i].sem, 16)
                    for hh in range(2):
                        sp.dma_start(raw[hh * HD:(hh + 1) * HD, NP:DC, :],
                                     wo[:, WA + NP * hh * HD:WA + NP * (hh + 1) * HD].rearrange(
                                         "l (c p) n -> p (l c) n", p=HD)).then_inc(o_raw_in[i].sem, 16)

                o_load(0, 0)
                o_load(1, 1)
                with sp.Fori(0, NB // 2 - 1) as bb:
                    for i in range(2):
                        sp.wait_ge(s_turned.sem, s_turned.at(l, 8 * (2 * bb + i + 1)))
                        sp.sem_inc(waits_alone, 1)
                        kv_load(0, i, 2 * bb + 2 + i)
                        sp.wait_ge(s_mixed.sem, s_mixed.at(l, 2 * (2 * bb + i + 1)))
                        sp.sem_inc(waits_alone, 1)
                        kv_load(1, i, 2 * bb + 2 + i)
                sp.wait_ge(rows_out.sem, rows_out.at(l, 64))
                sp.sem_inc(waits_alone, 1)
                meet(sp, l, 1)

                sp.wait_ge(hf_ready.sem, hf_ready.at(l, 16))
                sp.sem_inc(waits_alone, 1)
                sp.dma_start(xm[:].rearrange("p c t -> p (c t)"), x_spill).then_inc(x_back.sem, 16)
                with sp.Fori(1, DC // 2) as dd:
                    for i in range(2):
                        sp.wait_ge(o_split.sem, o_split.at(l, 2 * dd + i - 1))
                        sp.sem_inc(waits_alone, 1)
                        o_load(i, 2 * dd + i)
                sp.wait_ge(x_back.sem, x_back.at(l, 16))
                sp.sem_inc(waits_alone, 1)

                sp.wait_ge(o_split.sem, o_split.at(l, DC))
                sp.sem_inc(waits_alone, 1)
                with sp.Fori(0, FI) as f:
                    for j in range(3):
                        before = 3 * f + j if j == 0 else 3 * f + j - 1
                        sp.wait_ge(f_split.sem, f_split.at(l, before))
                        sp.sem_inc(waits_alone, 1)
                        if j < 2:
                            sp.dma_start(f_raw[j % 2][:].rearrange("p (c n) -> p c n", c=DC),
                                         layer(w_gate_up)[:, :, ds(j * FF + f * 2 * P, 2 * P)].rearrange(
                                             "l (c p) n -> p (l c) n", p=P)).then_inc(f_raw_in[j].sem, 16)
                        else:
                            sp.dma_start(f_raw[0][:].rearrange("p (a n) -> p a n", a=2),
                                         layer(w_down)[:, ds(f * 2 * P, 2 * P), :].rearrange(
                                             "l (a p) n -> p (l a) n", p=P)).then_inc(f_raw_in[j].sem, 16)
                meet(sp, l, 2)
            for t in range(QT + 1):
                sp.wait_ge(y_tile_kept, 2 * (t + 1))
                dst = y_prompt[0, t * P:(t + 1) * P, :] if t < QT else y_sample.rearrange("b t d -> (b t) d")
                sp.dma_start(dst, xy_tile[t % 2][0:rows_of(t), 0, :]).then_inc(y_tile_out[t % 2], 16)
            sp.wait_ge(y_tile_out[0], 16 * 5)
            sp.wait_ge(y_tile_out[1], 16 * 4)

        @block.gpsimd
        def _(pool):
            nc.gpsimd.memset(eps[:], EPS).then_inc(eps_set, 1)

            def split(l, k, raw_in, raw_count, hi_ready_, split_, raw, hi, lo):
                pool.wait_ge(raw_in.sem, raw_in.at(l, raw_count))
                pool.sem_inc(waits_alone, 1)
                nc.gpsimd.tensor_copy(hi, raw).then_inc(hi_ready_.sem, 1)
                pool.wait_ge(hi_ready_.sem, hi_ready_.at(l, k + 1))
                pool.sem_inc(waits_alone, 1)
                nc.gpsimd.tensor_tensor(lo, raw, hi.bitcast(F32), ALU.subtract).then_inc(split_.sem, 1)

            pool.drain().then_inc(met, 1)
            pool.wait_ge(met, 5)
            with pool.Fori(0, DEPTH) as l:
                for n, z in enumerate((q_a[HD:P, 0], q_a[0:HD, 1], q_b[HD:P, 0], q_b[0:HD, 1], q_rows_a[:], q_rows_b[:])):
                    nc.gpsimd.memset(z, 0.0).then_inc(zeroed.sem, 1)
                    pool.wait_ge(zeroed.sem, zeroed.at(l, n + 1))
                    pool.sem_inc(waits_alone, 1)

                def split_w(k, raw_count, slot):
                    split(l, k, w_raw_in, raw_count, w_hi_ready, w_split, w_raw[:], w_hi[:, slot], w_lo[:, slot])

                for u in range(2):
                    split_w(u, RAW[u], u)
                with pool.Fori(0, NP) as p:
                    for b in range(2):
                        pool.dma_start(new_a_s[ds(l, 1), ds(2 * p + b, 1), 0:LA - TS].rearrange("l b t z h d -> (l b) (t z h d)"),
                                       cache_a[ds(l, 1), ds(2 * p + b, 1), TS:LA].rearrange("l b t z h d -> (l b) (t z h d)")
                                       ).then_inc(cache_out.sem, 16)
                        pool.dma_start(new_b_s[ds(l, 1), ds(2 * p + b, 1), 0:LB - TS].rearrange("l b t z h d -> (l b) (t z h d)"),
                                       cache_b[ds(l, 1), ds(2 * p + b, 1), TS:LB].rearrange("l b t z h d -> (l b) (t z h d)")
                                       ).then_inc(cache_out.sem, 16)
                    for j in range(4):
                        pool.wait_ge(projected.sem, projected.at(l, 1 + 4 * p + j))
                        pool.sem_inc(waits_alone, 1)
                        split_w(2 + 4 * p + j, 32 + 80 * p + RAW_P[j], j % 2)
                meet(pool, l, 0)

                def split_o(i, dd):
                    split(l, 2 * dd + i, o_raw_in[i], 48 * (dd + 1), o_hi_ready, o_split,
                          f_raw[i][:, 0:D], f_hi[i][:, D:], f_lo[i][:, D:])

                split_o(0, 0)
                split_o(1, 0)
                meet(pool, l, 1)
                with pool.Fori(1, DC // 2) as dd:
                    for i in range(2):
                        pool.wait_ge(o_done[i].sem, o_done[i].at(l, dd))
                        pool.sem_inc(waits_alone, 1)
                        split_o(i, dd)
                with pool.Fori(0, FI) as f:
                    for j in range(3):
                        pool.wait_ge(f_hi_ready.sem, f_hi_ready.at(l, 3 * f + j + 1))
                        pool.sem_inc(waits_alone, 1)
                        nc.gpsimd.tensor_tensor(f_lo[j][:], f_raw[j % 2][:], f_hi[j][:].bitcast(F32), ALU.subtract
                                                ).then_inc(f_split.sem, 1)
                pool.wait_ge(cache_out.sem, cache_out.at(l, 16 * 2 * NB))
                pool.sem_inc(waits_alone, 1)
                meet(pool, l, 2)

        @block.scalar
        def _(act):
            act.wait_ge(eps_set, 1)

            def norm_squares(l, k, sq):
                first, n, before, width = NORMS[k]
                for c in range(n):
                    if c >= 2:
                        act.wait_ge(sq_summed.sem, sq_summed.at(l, before + c - 1))
                    nc.scalar.activation(sq[c % 2][:], xm[:, first + c, :], ACT.Square).then_inc(sq_ready.sem, 1)

            def norm_roots(l, k):
                first, n, before, width = NORMS[k]
                act.wait_ge(sq_summed.sem, sq_summed.at(l, before + n))
                for rows, a, b in ((P, 0, QT), (NS, QT, QT + 1)):
                    nc.scalar.activation(roots[0:rows, k % 2, a:b], ps[0:rows, 6 + k % 2, a:b], ACT.Sqrt,
                                         scale=1.0 / width, bias=eps[0:rows, 0:1]).then_inc(root_ready.sem, 1)

            def norm_hi(l, k, hf, hi):
                first, n, before, width = NORMS[k]
                for c in range(n):
                    act.wait_ge(hf_ready.sem, hf_ready.at(l, before + c + 1))
                    nc.scalar.activation(hi[:, first + c, :], hf[c % 2][:], ACT.Copy).then_inc(hi_ready.sem, 1)

            act.drain().then_inc(met, 1)
            act.wait_ge(met, 5)
            with act.Fori(0, DEPTH) as l:
                norm_squares(l, 0, sq1)
                norm_roots(l, 0)
                norm_hi(l, 0, hf1, h_hi)

                def head_squares(unit, bank, n):
                    act.wait_ge(projected.sem, projected.at(l, unit + 1))
                    act.wait_ge(head_spread.sem, head_spread.at(l, n))
                    nc.scalar.activation(pieces(t_buf[1][:, 0:T]), banks(bank), ACT.Square).then_inc(head_sq.sem, 1)

                def roots_of_heads(n, r):
                    act.wait_ge(rope.sem, rope.at(l, r + 7))
                    for rows, a, b in ((P, 0, QT), (NS, QT, QT + 1)):
                        nc.scalar.activation(
                            t_buf[1][0:rows, a * P:b * P].rearrange("p (t d) -> p t d", d=HD),
                            head_means[0:rows, 1, 2 * a:2 * b].rearrange("p (t o) -> p t o", o=1).broadcast_to(
                                (rows, 2 * (b - a), HD)), ACT.Sqrt).then_inc(head_root.sem, 1)

                def stage_v(unit, n):
                    act.wait_ge(projected.sem, projected.at(l, unit + 1))
                    act.wait_ge(k_out.sem, k_out.at(l, 16 * (n + 1)))
                    nc.scalar.activation(pieces(stage[:]), banks(3), ACT.Copy).then_inc(v_staged.sem, 1)

                def keep_k(n, rows):
                    act.wait_ge(v_turned.sem, v_turned.at(l, 3 * n))
                    for g in range(2):
                        act.wait_ge(k_turned.sem, k_turned.at(l, 3 * n + g + 1))
                        nc.scalar.activation(stage[:, g * 4 * P:(g + 1) * 4 * P], ps[:, 6 + g, :], ACT.Copy
                                             ).then_inc(k_kept.sem, 1)
                    act.wait_ge(k_turned.sem, k_turned.at(l, 3 * n + 3))
                    nc.scalar.activation(rows, ps[0:NS, 2, 384:512], ACT.Copy).then_inc(k_kept.sem, 1)

                act.wait_ge(projected.sem, projected.at(l, 1))
                act.wait_ge(lo_ready.sem, lo_ready.at(l, 8))
                nc.scalar.activation(pieces(t_buf[1][:, 0:T]), banks(0), ACT.Square).then_inc(head_sq.sem, 1)
                roots_of_heads(0, 0)
                keep_k(0, kv_rows[:, 0, NP, :])
                stage_v(1, 0)
                with act.Fori(0, NP) as p:
                    u, r, h = 2 + 4 * p, K_ROPE + ROPE_P * p, 1 + 3 * p
                    head_squares(u, 0, h)
                    roots_of_heads(h, r)
                    head_squares(u + 1, 3, h + 1)
                    keep_k(p + 1, kv_rows[:, 0, ds(p, 1), :].rearrange("q c n -> q (c n)"))
                    roots_of_heads(h + 1, r + K_ROPE)
                    head_squares(u + 2, 0, h + 2)
                    roots_of_heads(h + 2, r + K_ROPE + Q_ROPE)
                    stage_v(u + 3, p + 1)

                    def softmax(s):
                        m, i, hh = steps[s]
                        n = P * len(key_tiles[s])
                        act.wait_ge(masked.sem, masked.at(l, p * NST + s + 1))
                        nc.scalar.activation(t_buf[s % 3][:, 0:n], t_buf[s % 3][:, 0:n], ACT.Exp, scale=-1.0,
                                             bias=stats[:, 0, s % 4:s % 4 + 1],
                                             accum_out=stats[:, 2, s % 4:s % 4 + 1]).then_inc(exped.sem, 1)
                        if m == "b":
                            nc.scalar.activation(stats[:, 4, s % 4:s % 4 + 1], sink_now[:, hh:hh + 1], ACT.Exp,
                                                 bias=stats[:, 0, s % 4:s % 4 + 1]).then_inc(exped.sem, 1)

                    softmax(0)
                    softmax(1)
                    for s in range(NST):
                        for g in groups_of[s]:
                            _, a, b = groups[g]
                            if g >= 3:
                                act.wait_ge(mixed.sem, mixed.at(l, p * NST + groups[g - 3][0] + 1))
                            act.wait_ge(p_turned.sem, p_turned.at(l, p * NGR + g + 1))
                            nc.scalar.activation(pt[:, g % 3, 0:(b - a) * P], ps[:, 4 + g % 2, 0:(b - a) * P],
                                                 ACT.Copy).then_inc(pt_ready.sem, 1)
                        if s + 2 < NST:
                            softmax(s + 2)
                meet(act, l, 0)

                def keep_near(b, prs):
                    for pr in prs:
                        act.wait_ge(s_turned.sem, s_turned.at(l, 8 * b + 2 * pr + 1))
                        nc.scalar.activation(kt_s[:, pr, 0:WIN], ps[:, 2 * (pr % 2), :], ACT.Copy
                                             ).then_inc(near_kept.sem, 1)

                def exps(b, following):
                    if following:
                        act.wait_ge(s_scores.sem, s_scores.at(l, b + 1))
                        keep_near(b + 1, range(1))
                    act.wait_ge(s_soft.sem, s_soft.at(l, 8 * b + 3))
                    nc.scalar.activation(p_s[:, 0:NKEYS], p_s[:, 0:NKEYS], ACT.Exp, scale=-1.0,
                                         bias=st_s[:, 1:2], accum_out=st_s[:, 5:6]).then_inc(s_exped.sem, 1)
                    nc.scalar.activation(p_s[:, NKEYS:], p_s[:, NKEYS:], ACT.Exp, scale=-1.0,
                                         bias=st_s[:, 2:3], accum_out=st_s[:, 6:7]).then_inc(s_exped.sem, 1)
                    nc.scalar.activation(st_s[:, 7:8], st_s[:, 10:11], ACT.Exp, bias=st_s[:, 2:3]
                                         ).then_inc(s_exped.sem, 1)
                    if following:
                        keep_near(b + 1, range(1, NP))

                keep_near(0, range(NP))
                with act.Fori(0, NB - 1) as b:
                    exps(b, True)
                exps(NB - 1, False)
                meet(act, l, 1)

                norm_squares(l, 1, sq2)
                norm_roots(l, 1)
                for c in range(NP):
                    if c >= 1:
                        act.wait_ge(sq_summed.sem, sq_summed.at(l, 12 + c - 1))
                    else:
                        act.wait_ge(sq_summed.sem, sq_summed.at(l, 12))
                    nc.scalar.activation(sq2[c % 2][:], xm[:, NP + c, :], ACT.Square).then_inc(sq_ready.sem, 1)
                norm_roots(l, 2)
                norm_hi(l, 1, hf2, g_hi)
                norm_hi(l, 2, hf2, g_hi)
                for i in range(2):
                    act.wait_ge(o_added[i].sem, o_added[i].at(l, DC // 2))
                norm_squares(l, 3, sq2)
                norm_roots(l, 3)
                norm_hi(l, 3, hf2, g_hi)

                def round_weights(j, f):
                    act.wait_ge(f_raw_in[j].sem, f_raw_in[j].at(l, 16 * (f + 1)))
                    if j < 2:
                        act.wait_ge(hid.sem, hid.at(l, HID * f))
                    else:
                        act.wait_ge(downed.sem, downed.at(l, DOWN * f))
                    nc.scalar.activation(f_hi[j][:], f_raw[j % 2][:], ACT.Copy).then_inc(f_hi_ready.sem, 1)

                def hidden_piece(f, k):
                    a, n = divmod(k, NW)
                    act.wait_ge(hid.sem, hid.at(l, HID * f + k + 1))
                    act.wait_ge(act_lo.sem, act_lo.at(l, HID * f + max(k - 1, 0)))
                    nc.scalar.activation(silu[:, k % 2, :], ps[:, 2 * (k % 2), 0:W], ACT.Silu
                                         ).then_inc(silued.sem, 1)
                    act.wait_ge(gated.sem, gated.at(l, HID * f + k + 1))
                    act.wait_ge(downed.sem, downed.at(l, DOWN * f))
                    nc.scalar.activation(a_hi[:, a, n * W:(n + 1) * W], silu[:, k % 2, :], ACT.Copy
                                         ).then_inc(act_hi.sem, 1)

                for i in range(2):
                    act.wait_ge(o_done[i].sem, o_done[i].at(l, DC // 2))
                round_weights(0, 0)
                round_weights(1, 0)
                with act.Fori(0, FI - 1) as f:
                    hidden_piece(f, 0)
                    hidden_piece(f, 1)
                    round_weights(2, f)
                    for k in range(2, HID):
                        hidden_piece(f, k)
                    round_weights(0, f + 1)
                    round_weights(1, f + 1)
                for k in range(HID):
                    hidden_piece(FI - 1, k)
                    if k == 1:
                        round_weights(2, FI - 1)
                meet(act, l, 2)

        @block.vector
        def _(dve):
            swap = [(i + ROT // 2) % ROT if i < ROT else i for i in range(32)]

            for t in range(QT + 1):
                for g in range(2):
                    dve.wait_ge(x_tile_turned, 2 * t + g + 1)
                    w = rows_of(t)
                    nc.vector.tensor_copy(xm[:, 4 * g:4 * g + 4, t * P:t * P + w],
                                          ps[:, (2 * t + g) % 8, :].rearrange("p (c n) -> p c n", c=4)[:, :, 0:w]
                                          ).then_inc(x_tile_kept, 1)

            def norm_reciprocals(l, k):
                dve.wait_ge(root_ready.sem, root_ready.at(l, 2 * k + 2))
                for rows, a, b in ((P, 0, QT), (NS, QT, QT + 1)):
                    nc.vector.reciprocal(roots[0:rows, k % 2, a:b], roots[0:rows, k % 2, a:b]).then_inc(rs_ready.sem, 1)

            def norm_chunks(l, k, gain, hf, bank, hi, lo):
                first, n, before, width = NORMS[k]
                dve.wait_ge(rs_spread.sem, rs_spread.at(l, k + 1))
                for c in range(n + 1):
                    if c < n:
                        if before + c >= 2:
                            dve.wait_ge(lo_ready.sem, lo_ready.at(l, before + c - 1))
                        nc.vector.scalar_tensor_tensor(hf[c % 2][:], xm[:, first + c, :],
                                                       gains[:, gain + first + c:gain + first + c + 1], flat(bank),
                                                       ALU.mult, ALU.mult).then_inc(hf_ready.sem, 1)
                    if c >= 1:
                        dve.wait_ge(hi_ready.sem, hi_ready.at(l, before + c))
                        nc.vector.tensor_tensor(lo[:, first + c - 1, :], hf[(c - 1) % 2][:],
                                                hi[:, first + c - 1, :].bitcast(F32), ALU.subtract
                                                ).then_inc(lo_ready.sem, 1)

            dve.drain().then_inc(met, 1)
            dve.wait_ge(met, 5)
            with dve.Fori(0, DEPTH) as l:
                nc.vector.tensor_copy(gains[:], gains_all[:, ds(l * NG, NG)]).then_inc(gains_now.sem, 1)
                nc.vector.tensor_copy(sinks[:], sinks_all[:, ds(l * HB, HB)]).then_inc(gains_now.sem, 1)
                norm_reciprocals(l, 0)
                dve.wait_ge(gains_now.sem, gains_now.at(l, 2))
                norm_chunks(l, 0, GATT, hf1, 0, h_hi, h_lo)

                def roped(unit, bank, gain, r, root):
                    dve.wait_ge(projected.sem, projected.at(l, unit + 1))
                    dve.wait_ge(rope.sem, rope.at(l, r))
                    dve.wait_ge(head_sq.sem, head_sq.at(l, root + 1))
                    nc.vector.tensor_scalar(pieces(t_buf[0][:]), banks(bank), gains[:, gain:gain + 1], None,
                                            ALU.mult).then_inc(rope.sem, 1)
                    dve.wait_ge(rope.sem, rope.at(l, r + 1))
                    dve.sem_inc(waits_alone, 1)
                    nc.vector.stream_shuffle(t_buf[2][:], t_buf[0][:], swap).then_inc(rope.sem, 1)
                    dve.wait_ge(rope.sem, rope.at(l, r + 2))
                    nc.vector.tensor_tensor(t_buf[0][:], t_buf[0][:], cos[:], ALU.mult).then_inc(rope.sem, 1)
                    dve.wait_ge(head_summed.sem, head_summed.at(l, root + 1))
                    for rows, a, b in ((P, 0, 2 * QT), (NS, 2 * QT, 2 * QT + 2)):
                        nc.vector.tensor_scalar(head_means[0:rows, 0, a:b], ps[0:rows, bank, a:b], 1.0 / HD, EPS,
                                                ALU.mult, ALU.add).then_inc(rope.sem, 1)
                    dve.wait_ge(rope.sem, rope.at(l, r + 5))
                    for rows, a, b in ((P, 0, 2 * QT), (NS, 2 * QT, 2 * QT + 2)):
                        nc.vector.reciprocal(head_means[0:rows, 1, a:b], head_means[0:rows, 0, a:b]).then_inc(rope.sem, 1)
                    nc.vector.tensor_tensor(t_buf[2][:], t_buf[2][:], sin[:], ALU.mult).then_inc(rope.sem, 1)
                    dve.wait_ge(rope.sem, rope.at(l, r + 8))
                    nc.vector.tensor_tensor(t_buf[0][:], t_buf[0][:], t_buf[2][:], ALU.add).then_inc(rope.sem, 1)
                    dve.wait_ge(head_spread.sem, head_spread.at(l, root + 1))
                    dve.wait_ge(rope.sem, rope.at(l, r + 9))

                def k_rope(unit, gain, r, root, kt, new):
                    roped(unit, 0, gain, r, root)
                    nc.vector.tensor_tensor(kt[:], t_buf[0][:], flat(0), ALU.mult).then_inc(rope.sem, 1)
                    dve.wait_ge(rope.sem, rope.at(l, r + 10))
                    nc.vector.tensor_copy(new, kt[:, SEQ:T]).then_inc(rope.sem, 1)

                def q_rope(unit, bank, gain, r, root, q, rows):
                    roped(unit, bank, gain, r, root)
                    for hh in range(2):
                        half = slice(hh * HD, (hh + 1) * HD)
                        nc.vector.scalar_tensor_tensor(q[half, hh, :], t_buf[0][half, 0:SEQ], -1.0,
                                                       flat(bank)[half, 0:SEQ], ALU.mult, ALU.mult).then_inc(rope.sem, 1)
                    for hh in range(2):
                        half = slice(hh * HD, (hh + 1) * HD)
                        nc.vector.scalar_tensor_tensor(rows(half, hh),
                                                       t_buf[0][half, SEQ:T].rearrange("p (b t) -> p b t", t=TS), -1.0,
                                                       flat(bank)[half, SEQ:T].rearrange("p (b t) -> p b t", t=TS),
                                                       ALU.mult, ALU.mult).then_inc(rope.sem, 1)

                def keep_v(n, v, rows):
                    dve.wait_ge(v_out.sem, v_out.at(l, 16 * n))
                    for g in range(2):
                        dve.wait_ge(v_turned.sem, v_turned.at(l, 3 * n + g + 1))
                        nc.vector.tensor_copy(v[:, 4 * g:4 * g + 4, :],
                                              ps[:, 6 + g, :].rearrange("p (j n) -> p j n", j=4)).then_inc(v_kept.sem, 1)
                    dve.wait_ge(v_turned.sem, v_turned.at(l, 3 * n + 3))
                    nc.vector.tensor_copy(rows, ps[0:NS, 5, 384:512]).then_inc(v_kept.sem, 1)

                dve.wait_ge(zeroed.sem, zeroed.at(l, 6))
                dve.wait_ge(lo_ready.sem, lo_ready.at(l, 8))
                k_rope(0, GKB, 0, 0, kt_b, k_new_b[:])
                keep_v(0, v_b, kv_rows[:, 1, NP, :])
                dve.wait_ge(spilled.sem, spilled.at(l, 16))
                dve.sem_inc(waits_alone, 1)
                with dve.Fori(0, NP) as p:
                    u, r, h = 2 + 4 * p, K_ROPE + ROPE_P * p, 1 + 3 * p
                    k_rope(u, GKA, r, h, kt_a, k_new_a[:, ds(p, 1), :].rearrange("q c n -> q (c n)"))
                    q_rope(u + 1, 3, GQA, r + K_ROPE, h + 1, q_a,
                           lambda half, hh: q_rows_a[half, ds(p, 1), :, ds(2 * p + hh, 1), :].rearrange(
                               "q c b h t -> q (c b) (h t)"))
                    q_rope(u + 2, 0, GQB, r + K_ROPE + Q_ROPE, h + 2, q_b,
                           lambda half, hh: q_rows_b[half, :, ds(p + NP * hh, 1), :].rearrange("q b h t -> q b (h t)"))
                    nc.vector.tensor_copy(sink_now[:].rearrange("p (a b) -> p a b", b=1),
                                          sinks[:].rearrange("p (a b) -> p a b", a=2)[:, :, ds(p, 1)]
                                          ).then_inc(sink_ready.sem, 1)
                    dve.wait_ge(sink_ready.sem, sink_ready.at(l, 2 * p + 1))
                    nc.vector.tensor_scalar(sink_raw[:], sink_now[:], -1.0, None, ALU.mult
                                            ).then_inc(sink_ready.sem, 1)
                    dve.wait_ge(sink_ready.sem, sink_ready.at(l, 2 * p + 2))
                    dve.wait_ge(rope.sem, rope.at(l, r + ROPE_P))

                    def mask_and_max(s):
                        m, i, hh = steps[s]
                        n = P * len(key_tiles[s])
                        mask = mask_a[:, SEQ - n:] if m == "a" else mask_b[:, 2 * P - n:]
                        if s >= 3:
                            dve.wait_ge(p_turned.sem, p_turned.at(l, p * NGR + groups_of[s - 3][-1] + 1))
                        dve.wait_ge(scores.sem, scores.at(l, p * NST + s + 1))
                        dve.sem_inc(waits_alone, 1)
                        nc.vector.tensor_tensor_reduce(
                            t_buf[s % 3][:, 0:n],
                            ps[:, 2 * (s % 2):2 * (s % 2) + 2, :].rearrange("p b c -> p (b c)")[:, 0:n], mask,
                            SCALE, 3e38 if m == "a" else sink_raw[:, hh:hh + 1], ALU.add, ALU.min,
                            stats[:, 0, s % 4:s % 4 + 1]).then_inc(masked.sem, 1)

                    def normalize(s):
                        m, i, hh = steps[s]
                        n = P * len(key_tiles[s])
                        c = slice(s % 4, s % 4 + 1)
                        dve.wait_ge(exped.sem, exped.at(l, p * NEXP + exps_to[s]))
                        if m == "b":
                            nc.vector.tensor_tensor(stats[:, 2, c], stats[:, 2, c], stats[:, 4, c], ALU.add
                                                    ).then_inc(sum_ready.sem, 1)
                            dve.wait_ge(sum_ready.sem, sum_ready.at(l, p * NEXP + exps_to[s] - 1))
                        nc.vector.reciprocal(stats[:, 3, c], stats[:, 2, c]).then_inc(sum_ready.sem, 1)
                        dve.wait_ge(sum_ready.sem, sum_ready.at(l, p * NEXP + exps_to[s]))
                        nc.vector.tensor_scalar(t_buf[s % 3][:, 0:n], t_buf[s % 3][:, 0:n], stats[:, 3, c], None,
                                                ALU.mult).then_inc(probs.sem, 1)

                    def keep_mix(s):
                        m, i, hh = steps[s]
                        half = slice(hh * HD, (hh + 1) * HD)
                        dve.wait_ge(mixed.sem, mixed.at(l, p * NST + s + 1))
                        nc.vector.tensor_copy(
                            xm[half, ds(p + (NP if m == "b" else 0), 1), i * P:(i + 1) * P].rearrange("q c n -> q (c n)"),
                            ps[half, 6 + s % 2, 0:P]).then_inc(mix_kept.sem, 1)

                    mask_and_max(0)
                    mask_and_max(1)
                    keep_v(p + 1, v_a, kv_rows[:, 1, ds(p, 1), :].rearrange("q c n -> q (c n)"))
                    for s in range(NST):
                        normalize(s)
                        if s + 2 < NST:
                            mask_and_max(s + 2)
                        if s >= 2:
                            keep_mix(s - 2)
                    keep_mix(NST - 2)
                    keep_mix(NST - 1)
                meet(dve, l, 0)

                dve.wait_ge(masks_in.sem, masks_in.at(l, 80))
                nc.vector.tensor_tensor(p_s[:, 0:HB], sinks[0:NS, :], pick[:], ALU.mult).then_inc(sink_s.sem, 1)
                dve.wait_ge(sink_s.sem, sink_s.at(l, 1))
                nc.vector.reduce_sum(st_s[:, 10:11], p_s[:, 0:HB], AX.X).then_inc(sink_s.sem, 1)
                dve.wait_ge(sink_s.sem, sink_s.at(l, 2))
                nc.vector.tensor_scalar(st_s[:, 11:12], st_s[:, 10:11], -1.0, None, ALU.mult
                                        ).then_inc(sink_s.sem, 1)
                dve.wait_ge(sink_s.sem, sink_s.at(l, 3))
                dve.sem_inc(waits_alone, 1)
                def queries(b, used):
                    dve.wait_ge(s_scores.sem, s_scores.at(l, b))
                    dve.wait_ge(s_soft.sem, s_soft.at(l, used))
                    nc.vector.tensor_copy(q_now_a[:], q_rows_a[:, :, ds(b, 1)].rearrange("q c b h t -> q c (b h t)")
                                          ).then_inc(s_query.sem, 1)
                    nc.vector.tensor_copy(q_now_b[:], q_rows_b[:, ds(b, 1)].rearrange("q b h t -> q (b h t)")
                                          ).then_inc(s_query.sem, 1)
                    nc.vector.tensor_copy(mask_s[:, WIN + 4 * NFAR:], mask_sn[:, ds(b * NS, NS)]).then_inc(s_query.sem, 1)
                    nc.vector.tensor_copy(mask_t[:, LB:], mask_tn[:, ds(b * NS, NS)]).then_inc(s_query.sem, 1)

                def keep_far(b, prs):
                    for pr in prs:
                        dve.wait_ge(s_turned.sem, s_turned.at(l, 8 * b + 2 * pr + 2))
                        nc.vector.tensor_copy(kt_s[:, pr, WIN:], ps[:, 2 * (pr % 2) + 1, 0:4 * NFAR]
                                              ).then_inc(far_kept.sem, 1)
                        if pr == NP - 1:
                            nc.vector.tensor_copy(kt_t[:], ps[:, 3, 384:512]).then_inc(far_kept.sem, 1)

                def softmax_sample(b, following):
                    dve.wait_ge(s_scores.sem, s_scores.at(l, b + 1))
                    dve.wait_ge(s_query.sem, s_query.at(l, 4 * b + 4))
                    dve.sem_inc(waits_alone, 1)
                    nc.vector.tensor_tensor_reduce(p_s[:, 0:WIN], ps[0:NS, 5, :], mask_s[:, 0:WIN], SCALE, 3e38,
                                                   ALU.add, ALU.min, st_s[:, 0:1]).then_inc(s_soft.sem, 1)
                    dve.wait_ge(s_soft.sem, s_soft.at(l, 8 * b + 1))
                    dve.sem_inc(waits_alone, 1)
                    nc.vector.tensor_tensor_reduce(p_s[:, WIN:NKEYS], ps[0:NS, 6, 0:NKEYS - WIN], mask_s[:, WIN:], SCALE,
                                                   st_s[:, 0:1], ALU.add, ALU.min, st_s[:, 1:2]).then_inc(s_soft.sem, 1)
                    nc.vector.tensor_tensor_reduce(p_s[:, NKEYS:], ps[0:NS, 7, 0:LB + NS], mask_t[:], SCALE,
                                                   st_s[:, 11:12], ALU.add, ALU.min, st_s[:, 2:3]).then_inc(s_soft.sem, 1)
                    if following:
                        queries(b + 1, 8 * b + 3)
                        keep_far(b + 1, range(1))
                    dve.wait_ge(s_exped.sem, s_exped.at(l, 3 * b + 3))
                    nc.vector.tensor_tensor(st_s[:, 6:7], st_s[:, 6:7], st_s[:, 7:8], ALU.add).then_inc(s_soft.sem, 1)
                    dve.wait_ge(s_soft.sem, s_soft.at(l, 8 * b + 4))
                    nc.vector.reciprocal(st_s[:, 8:9], st_s[:, 5:6]).then_inc(s_soft.sem, 1)
                    nc.vector.reciprocal(st_s[:, 9:10], st_s[:, 6:7]).then_inc(s_soft.sem, 1)
                    dve.wait_ge(s_soft.sem, s_soft.at(l, 8 * b + 6))
                    nc.vector.tensor_scalar(p_s[:, 0:NKEYS], p_s[:, 0:NKEYS], st_s[:, 8:9], None, ALU.mult
                                            ).then_inc(s_soft.sem, 1)
                    nc.vector.tensor_scalar(p_s[:, NKEYS:], p_s[:, NKEYS:], st_s[:, 9:10], None, ALU.mult
                                            ).then_inc(s_soft.sem, 1)
                    if following:
                        keep_far(b + 1, range(1, NP))
                    dve.wait_ge(s_pturned.sem, s_pturned.at(l, b + 1))
                    for rows, a, z in ((P, 0, 4), (NFAR, 4, 8), (NS, 8, 9), (P, 9, 10), (NS, 10, 11)):
                        nc.vector.tensor_copy(pt_s[0:rows, a:z, :],
                                              ps[0:rows, 4, a * NS:z * NS].rearrange("p (a n) -> p a n", n=NS)
                                              ).then_inc(s_pkept.sem, 1)
                    dve.wait_ge(s_mixed.sem, s_mixed.at(l, 2 * b + 1))
                    nc.vector.tensor_copy(p_s[:, 0:WA], ps[0:NS, 5, :]).then_inc(s_rows.sem, 1)
                    dve.wait_ge(s_mixed.sem, s_mixed.at(l, 2 * b + 2))
                    for hh in range(2):
                        half = slice(hh * HD, (hh + 1) * HD)
                        nc.vector.tensor_copy(xm[half, NP:2 * NP, ds(SEQ + b * TS, TS)],
                                              ps[half, 6, hh * 16:(hh + 1) * 16].rearrange(
                                                  "p (c n) -> p c n", c=NP)).then_inc(s_mix_kept.sem, 1)
                    dve.wait_ge(s_mix_turned.sem, s_mix_turned.at(l, b + 1))
                    step = NS + 2 * TS
                    for hh in range(2):
                        half = slice(hh * HD, (hh + 1) * HD)
                        nc.vector.tensor_copy(xm[half, 0:NP, ds(SEQ + b * TS, TS)],
                                              ps[half, 7, hh * TS:hh * TS + NP * step].rearrange(
                                                  "p (c n) -> p c n", c=NP)[:, :, 0:TS]).then_inc(s_mix_kept.sem, 1)

                queries(0, 0)
                keep_far(0, range(NP))
                with dve.Fori(0, NB - 1) as b:
                    softmax_sample(b, True)
                softmax_sample(NB - 1, False)
                meet(dve, l, 1)

                norm_reciprocals(l, 1)
                norm_reciprocals(l, 2)
                norm_chunks(l, 1, GOUT, hf2, 0, g_hi, g_lo)
                norm_chunks(l, 2, GOUT, hf2, 3, g_hi, g_lo)
                dve.wait_ge(x_back.sem, x_back.at(l, 16))
                dve.sem_inc(waits_alone, 1)
                with dve.Fori(0, DC // 2) as dd:
                    for i in range(2):
                        dve.wait_ge(o_done[i].sem, o_done[i].at(l, dd + 1))
                        chunk = pieces(xm[:, ds(2 * dd + i, 1), :].rearrange("p c t -> p (c t)"))
                        nc.vector.tensor_tensor(chunk, chunk, banks(3 * i), ALU.add).then_inc(o_added[i].sem, 1)
                norm_reciprocals(l, 3)
                norm_chunks(l, 3, GFFN, hf2, 0, g_hi, g_lo)

                with dve.Fori(0, FI) as f:
                    for k in range(HID):
                        a, n = divmod(k, NW)
                        dve.wait_ge(silued.sem, silued.at(l, HID * f + k + 1))
                        nc.vector.tensor_tensor(silu[:, k % 2, :], silu[:, k % 2, :], ps[:, 2 * (k % 2) + 1, 0:W],
                                                ALU.mult).then_inc(gated.sem, 1)
                        dve.wait_ge(act_hi.sem, act_hi.at(l, HID * f + k + 1))
                        nc.vector.tensor_tensor(a_lo[:, a, n * W:(n + 1) * W], silu[:, k % 2, :],
                                                a_hi[:, a, n * W:(n + 1) * W].bitcast(F32), ALU.subtract
                                                ).then_inc(act_lo.sem, 1)
                    for n in range(NW):
                        for d in range(DC):
                            dve.wait_ge(downed.sem, downed.at(l, DOWN * f + n * DC + d + 1))
                            xs = xm[:, d, n * W:(n + 1) * W]
                            nc.vector.tensor_tensor(xs, xs, ps[:, 4 + (n * DC + d) % 4, 0:W], ALU.add
                                                    ).then_inc(ffn_added.sem, 1)
                meet(dve, l, 2)
            for t in range(QT + 1):
                if t >= 2:
                    dve.wait_ge(y_tile_out[t % 2], 16 * (t // 2))
                for g in range(2):
                    dve.wait_ge(y_tile_turned, 2 * t + g + 1)
                    w = rows_of(t)
                    nc.vector.tensor_copy(xy_tile[t % 2][0:w, 0, g * 512:(g + 1) * 512],
                                          ps[0:w, (2 * t + g) % 8, :]).then_inc(y_tile_kept, 1)

        @block.tensor
        def _(pe):
            pe.wait_ge(consts_in, 16 * 7)
            for t in range(QT + 1):
                pe.wait_ge(x_tile_in[t % 2], 16 * (t // 2 + 1))
                w = rows_of(t)
                for g in range(2):
                    if 2 * t + g >= 8:
                        pe.wait_ge(x_tile_kept, 2 * t + g - 7)
                    for c in range(4):
                        mm = pe.transpose(ps[:, (2 * t + g) % 8, c * P:c * P + w],
                                          xy_tile[t % 2][0:w, 0, (4 * g + c) * P:(4 * g + c + 1) * P], ident[0:w, 0:w])
                    mm.then_inc(x_tile_turned, 1)

            def sum_squares(l, k, sq):
                first, n, before, width = NORMS[k]
                for c in range(n):
                    pe.wait_ge(sq_ready.sem, sq_ready.at(l, before + c + 1))
                    for t in range(QT + 1):
                        mm = pe.matmul(ps[0:rows_of(t), 6 + k % 2, t:t + 1], sq[c % 2][:, t * P:t * P + rows_of(t)],
                                       ones[:, 0:1], start=(c == 0 and t == 0), stop=(c == n - 1),
                                       skip_group_check=True)
                    mm.then_inc(sq_summed.sem, 1)

            def spread_roots(l, k, bank):
                pe.wait_ge(rs_ready.sem, rs_ready.at(l, 2 * k + 2))
                pe.sem_inc(waits_alone, 1)
                for t in range(QT + 1):
                    w = rows_of(t)
                    mm = pe.transpose(ps[:, bank + t // 4, (t % 4) * P:(t % 4) * P + w],
                                      roots[0:w, k % 2, t:t + 1].broadcast_to((w, P)), ident[0:w, 0:w])
                mm.then_inc(rs_spread.sem, 1)

            pe.drain().then_inc(met, 1)
            pe.wait_ge(met, 5)
            with pe.Fori(0, DEPTH) as l:
                sum_squares(l, 0, sq1)
                spread_roots(l, 0, 0)
                pe.wait_ge(lo_ready.sem, lo_ready.at(l, 8))
                pe.wait_ge(zeroed.sem, zeroed.at(l, 6))

                def project(u, slot, bank, ns):
                    pe.wait_ge(w_split.sem, w_split.at(l, u + 1))
                    for n in ns:
                        mm = product(pe, ps[:, bank + n, 0:W], lambda a, c: (w_hi, w_lo)[a][:, slot, c, :],
                                     lambda a, c: (h_hi, h_lo)[a][:, c, n * W:(n + 1) * W], DC)
                    if NW - 1 in ns:
                        mm.then_inc(projected.sem, 1)

                def sum_heads(bank, n, r):
                    pe.wait_ge(head_sq.sem, head_sq.at(l, n + 1))
                    pe.wait_ge(rope.sem, rope.at(l, r + 1))
                    for t in range(QT + 1):
                        mm = pe.matmul(ps[0:rows_of(t), bank, 2 * t:2 * t + 2], t_buf[1][:, t * P:t * P + rows_of(t)],
                                       blocks[:, 0:P:HD], start=True, stop=True)
                    mm.then_inc(head_summed.sem, 1)

                def spread_heads(bank, n):
                    pe.wait_ge(head_root.sem, head_root.at(l, 2 * n + 2))
                    pe.sem_inc(waits_alone, 1)
                    for t in range(QT + 1):
                        w = rows_of(t)
                        mm = pe.transpose(ps[:, bank + t // 4, (t % 4) * P:(t % 4) * P + w],
                                          t_buf[1][0:w, t * P:(t + 1) * P], ident[0:w, 0:w])
                    mm.then_inc(head_spread.sem, 1)

                def turn(src, rest, done):
                    for g in range(2):
                        for c in range(4):
                            mm = pe.transpose(ps[:, 6 + g, c * P:(c + 1) * P],
                                              src[:, (4 * g + c) * P:(4 * g + c + 1) * P], ident[:])
                        mm.then_inc(done.sem, 1)
                    pe.transpose(ps[0:NS, rest, 384:512], src[:, SEQ:T], ident[:]).then_inc(done.sem, 1)

                project(0, 0, 0, (0, 1, 2))
                project(1, 1, 3, (0,))
                sum_heads(0, 0, 0)
                project(1, 1, 3, (1,))
                spread_heads(0, 0)
                project(1, 1, 3, (2,))
                pe.wait_ge(rope.sem, rope.at(l, K_ROPE))
                turn(kt_b, 2, k_turned)
                pe.wait_ge(v_staged.sem, v_staged.at(l, 1))
                pe.wait_ge(k_kept.sem, k_kept.at(l, 3))
                turn(stage, 5, v_turned)
                with pe.Fori(0, NP) as p:
                    u, r, h = 2 + 4 * p, K_ROPE + ROPE_P * p, 1 + 3 * p
                    pe.wait_ge(masked.sem, masked.at(l, NST * p))
                    project(u, 0, 0, (0, 1, 2))
                    pe.wait_ge(v_kept.sem, v_kept.at(l, 3 * p + 3))
                    pe.wait_ge(pt_ready.sem, pt_ready.at(l, NGR * p))
                    pe.wait_ge(mix_kept.sem, mix_kept.at(l, NST * p))
                    project(u + 1, 1, 3, (0,))
                    sum_heads(0, h, r)
                    project(u + 1, 1, 3, (1,))
                    spread_heads(0, h)
                    project(u + 1, 1, 3, (2,))
                    pe.wait_ge(rope.sem, rope.at(l, r + K_ROPE))
                    turn(kt_a, 2, k_turned)
                    project(u + 2, 0, 0, (0,))
                    sum_heads(3, h + 1, r + K_ROPE)
                    project(u + 2, 0, 0, (1,))
                    spread_heads(3, h + 1)
                    pe.wait_ge(k_kept.sem, k_kept.at(l, 3 * p + 6))
                    project(u + 2, 0, 0, (2,))
                    pe.wait_ge(rope.sem, rope.at(l, r + K_ROPE + Q_ROPE))
                    project(u + 3, 1, 3, (0,))
                    sum_heads(0, h + 2, r + K_ROPE + Q_ROPE)
                    project(u + 3, 1, 3, (1,))
                    spread_heads(0, h + 2)
                    project(u + 3, 1, 3, (2,))
                    pe.wait_ge(rope.sem, rope.at(l, r + ROPE_P))

                    def score(s):
                        m, i, hh = steps[s]
                        q, kt = (q_a, kt_a) if m == "a" else (q_b, kt_b)
                        n, first = P * len(key_tiles[s]), P * key_tiles[s][0]
                        if s >= 2:
                            pe.wait_ge(masked.sem, masked.at(l, p * NST + s - 1))
                        for c in range(0, n, 512):
                            w = min(512, n - c)
                            mm = pe.matmul(ps[:, 2 * (s % 2) + c // 512, 0:w], q[:, hh, i * P:(i + 1) * P],
                                           kt[:, first + c:first + c + w], start=True, stop=True)
                        mm.then_inc(scores.sem, 1)

                    def turn_probs(s):
                        pe.wait_ge(probs.sem, probs.at(l, p * NST + s + 1))
                        for g in groups_of[s]:
                            _, a, b = groups[g]
                            if g >= 2:
                                pe.wait_ge(pt_ready.sem, pt_ready.at(l, p * NGR + g - 1))
                            for c in range(a, b):
                                mm = pe.transpose(ps[:, 4 + g % 2, (c - a) * P:(c - a + 1) * P],
                                                  t_buf[s % 3][:, c * P:(c + 1) * P], ident[:])
                            mm.then_inc(p_turned.sem, 1)

                    def mix(s):
                        m, i, hh = steps[s]
                        v = v_a if m == "a" else v_b
                        if s >= 2:
                            pe.wait_ge(mix_kept.sem, mix_kept.at(l, p * NST + s - 1))
                        for g in groups_of[s]:
                            _, a, b = groups[g]
                            pe.wait_ge(pt_ready.sem, pt_ready.at(l, p * NGR + g + 1))
                            for c in range(a, b):
                                mm = pe.matmul(ps[:, 6 + s % 2, 0:P], v[:, key_tiles[s][c], :],
                                               pt[:, g % 3, (c - a) * P:(c - a + 1) * P],
                                               start=(c == 0), stop=(c == len(key_tiles[s]) - 1))
                        mm.then_inc(mixed.sem, 1)

                    score(0)
                    pe.wait_ge(v_staged.sem, v_staged.at(l, p + 2))
                    score(1)
                    turn(stage, 5, v_turned)
                    pe.wait_ge(v_kept.sem, v_kept.at(l, 3 * p + 6))
                    for s in range(NST):
                        if s + 2 < NST:
                            score(s + 2)
                        turn_probs(s)
                        if s >= 1:
                            mix(s - 1)
                    mix(NST - 1)
                meet(pe, l, 0)

                def turn_cache(i, bb):
                    b = 2 * bb + i
                    pe.wait_ge(k_in[i].sem, k_in[i].at(l, 48 * (bb + 1)))
                    pe.sem_inc(waits_alone, 1)
                    for pr in range(NP):
                        if pr >= 2:
                            pe.wait_ge(near_kept.sem, near_kept.at(l, 4 * b + pr - 1))
                            pe.sem_inc(waits_alone, 1)
                        for c in range(4):
                            mm = pe.transpose(ps[:, 2 * (pr % 2), c * P:(c + 1) * P],
                                              near[i][:, c, pr * P:(pr + 1) * P], ident[:])
                        mm.then_inc(s_turned.sem, 1)
                        if pr >= 2:
                            pe.wait_ge(far_kept.sem, far_kept.at(l, 5 * b + pr - 1))
                            pe.sem_inc(waits_alone, 1)
                        for c in range(4):
                            mm = pe.transpose(ps[:, 2 * (pr % 2) + 1, c * NFAR:(c + 1) * NFAR],
                                              far[i][:, c, pr * P:(pr + 1) * P], ident[0:NFAR, 0:NFAR])
                        if pr == NP - 1:
                            mm = pe.transpose(ps[:, 3, 384:512], last[i][:, 0, :], ident[:])
                        mm.then_inc(s_turned.sem, 1)

                def sample(i, bb, following):
                    b = 2 * bb + i
                    pe.wait_ge(near_kept.sem, near_kept.at(l, 4 * b + 4))
                    pe.wait_ge(far_kept.sem, far_kept.at(l, 5 * b + 5))
                    pe.wait_ge(s_query.sem, s_query.at(l, 4 * b + 4))
                    pe.wait_ge(s_mix_kept.sem, s_mix_kept.at(l, 4 * b))
                    for out, keys in ((ps[0:NS, 5, :], lambda pr: kt_s[:, pr, 0:WIN]),
                                      (ps[0:NS, 6, 0:4 * NFAR], lambda pr: kt_s[:, pr, WIN:]),
                                      (ps[0:NS, 6, 4 * NFAR:NKEYS - WIN], lambda pr: k_new_a[:, pr, :])):
                        for pr in range(NP):
                            pe.matmul(out, q_now_a[:, pr, :], keys(pr), start=(pr == 0), stop=(pr == NP - 1))
                    pe.matmul(ps[0:NS, 7, 0:LB], q_now_b[:], kt_t[:], start=True, stop=True)
                    pe.matmul(ps[0:NS, 7, LB:LB + NS], q_now_b[:], k_new_b[:], start=True, stop=True
                              ).then_inc(s_scores.sem, 1)
                    if following:
                        turn_cache(1 - i, bb + i)
                    pe.wait_ge(s_soft.sem, s_soft.at(l, 8 * b + 8))
                    pe.sem_inc(waits_alone, 1)
                    cols = [(c * P, P) for c in range(4)] + [(WIN + c * NFAR, NFAR) for c in range(4)] + \
                           [(WIN + 4 * NFAR, NS), (NKEYS, LB), (NKEYS + LB, NS)]
                    for c, (a, w) in enumerate(cols):
                        mm = pe.transpose(ps[0:w, 4, c * NS:(c + 1) * NS], p_s[:, a:a + w], ident[0:NS, 0:NS])
                    mm.then_inc(s_pturned.sem, 1)
                    pe.wait_ge(s_pkept.sem, s_pkept.at(l, 5 * b + 5))
                    pe.wait_ge(v_in[i].sem, v_in[i].at(l, 48 * (bb + 1)))
                    pe.sem_inc(waits_alone, 1)
                    for c in range(4):
                        pe.matmul(ps[0:NS, 5, :], pt_s[:, c, :], near[i][:, c, WA:], start=(c == 0), stop=False)
                    for c in range(4):
                        pe.matmul(ps[0:NS, 5, :], pt_s[0:NFAR, 4 + c, :], far[i][:, c, WA:], start=False, stop=False)
                    pe.matmul(ps[0:NS, 5, :], pt_s[0:NS, 8, :], kv_rows[:, 1, 0:NP, :].rearrange("q c n -> q (c n)"),
                              start=False, stop=True).then_inc(s_mixed.sem, 1)
                    pe.matmul(ps[:, 6, 0:NS], last[i][:, 1, :], pt_s[:, 9, :], start=True, stop=False)
                    pe.matmul(ps[:, 6, 0:NS], kv_rows[:, 1, NP, :], pt_s[0:NS, 10, :], start=False, stop=True
                              ).then_inc(s_mixed.sem, 1)
                    pe.wait_ge(s_rows.sem, s_rows.at(l, b + 1))
                    pe.sem_inc(waits_alone, 1)
                    for pr in range(NP):
                        mm = pe.transpose(ps[:, 7, pr * NS:(pr + 1) * NS], p_s[:, pr * P:(pr + 1) * P],
                                          ident[0:NS, 0:NS])
                    mm.then_inc(s_mix_turned.sem, 1)

                turn_cache(0, 0)
                with pe.Fori(0, NB // 2 - 1) as bb:
                    sample(0, bb, True)
                    sample(1, bb, True)
                sample(0, NB // 2 - 1, True)
                sample(1, NB // 2 - 1, False)
                meet(pe, l, 1)

                sum_squares(l, 1, sq2)
                sum_squares(l, 2, sq2)
                spread_roots(l, 1, 0)
                spread_roots(l, 2, 3)
                pe.wait_ge(lo_ready.sem, lo_ready.at(l, 16))
                pe.sem_inc(waits_alone, 1)
                with pe.Fori(0, DC // 2) as dd:
                    for i in range(2):
                        pe.wait_ge(o_split.sem, o_split.at(l, 2 * dd + i + 1))
                        pe.wait_ge(o_added[i].sem, o_added[i].at(l, dd))
                        for n in range(NW):
                            mm = product(pe, ps[:, 3 * i + n, 0:W], lambda a, c: (f_hi, f_lo)[a][i][:, D + c * P:D + (c + 1) * P],
                                         lambda a, c: (g_hi, g_lo)[a][:, c, n * W:(n + 1) * W], DC)
                        mm.then_inc(o_done[i].sem, 1)
                pe.wait_ge(o_added[0].sem, o_added[0].at(l, DC // 2))
                sum_squares(l, 3, sq2)
                spread_roots(l, 3, 0)

                pe.wait_ge(lo_ready.sem, lo_ready.at(l, 24))
                pe.sem_inc(waits_alone, 1)
                with pe.Fori(0, FI) as f:
                    pe.wait_ge(f_split.sem, f_split.at(l, 3 * f + 2))
                    for k in range(HID):
                        a, n = divmod(k, NW)
                        pe.wait_ge(gated.sem, gated.at(l, HID * f + max(k - 1, 0)))
                        for j in range(2):
                            mm = product(pe, ps[:, 2 * (k % 2) + j, 0:W],
                                         lambda h, c: (f_hi, f_lo)[h][j][:, c * 2 * P + a * P:c * 2 * P + (a + 1) * P],
                                         lambda h, c: (g_hi, g_lo)[h][:, c, n * W:(n + 1) * W], DC)
                        mm.then_inc(hid.sem, 1)
                    pe.wait_ge(f_split.sem, f_split.at(l, 3 * f + 3))
                    for n in range(NW):
                        pe.wait_ge(act_lo.sem, act_lo.at(l, HID * f + NW + n + 1))
                        for d in range(DC):
                            x = n * DC + d
                            pe.wait_ge(ffn_added.sem, ffn_added.at(l, DOWN * f + max(x - 3, 0)))
                            product(pe, ps[:, 4 + x % 4, 0:W],
                                    lambda h, c: (f_hi, f_lo)[h][2][:, c * D + d * P:c * D + (d + 1) * P],
                                    lambda h, c: (a_hi, a_lo)[h][:, c, n * W:(n + 1) * W], 2
                                    ).then_inc(downed.sem, 1)
                meet(pe, l, 2)
            for t in range(QT + 1):
                w = rows_of(t)
                for g in range(2):
                    if 2 * t + g >= 8:
                        pe.wait_ge(y_tile_kept, 2 * t + g - 7)
                    for c in range(4):
                        mm = pe.transpose(ps[0:w, (2 * t + g) % 8, c * P:(c + 1) * P],
                                          xm[:, 4 * g + c, t * P:t * P + w], ident[:])
                    mm.then_inc(y_tile_turned, 1)


_INS = ["x_prompt", "x_sample", "cache_a", "cache_b", "attn_norm", "w_in", "q_norm_a", "k_norm_a", "q_norm_b",
        "k_norm_b", "sinks_b", "out_norm_a", "out_norm_b", "w_out", "ffn_norm", "w_gate_up", "w_down"]
_OUTS = [(1, SEQ, D), (NB, TS, D), (DEPTH, 1, SEQ, 2, HA, HD), (DEPTH, 1, LB, 2, KVB, HD),
         (DEPTH, NB, LA, 2, HA, HD), (DEPTH, NB, LB, 2, KVB, HD)]


def kernel(**inputs):
    import concourse.bacc as _bacc
    from concourse.bass_utils import run_bass_kernel_spmd as _run

    nc = _bacc.Bacc("TRN2", target_bir_lowering=False, num_devices=1)
    arrays, args = {}, []
    tables = constants()
    for name, a in [(n, np.ascontiguousarray(inputs[n])) for n in _INS] + list(tables.items()):
        arrays[f"in_{name}_dram"] = a
        args.append(nc.dram_tensor(f"in_{name}_dram", a.shape, mybir.dt.from_np(a.dtype), kind="ExternalInput").ap())
    for i, shape in enumerate(_OUTS):
        args.append(nc.dram_tensor(f"out_{i}_dram", shape, F32, kind="ExternalOutput").ap())
    trunk(nc, *args)
    r = _run(nc, [arrays], core_ids=[0])
    return tuple(r.results[0][f"out_{i}_dram"] for i in range(len(_OUTS)))
```
